# Optimizing a Trainium2 kernel written in Bass

```python
import math
import jax, jax.numpy as jnp
from jax import lax
import numpy as np
import jax
import jax.numpy as jnp

D_MODEL = 1024
BATCH = 1
SEQ = 256
DEPTH = 2

RMS_EPS = 1e-6
Q_BLOCK = 128
NEG_INF = -1e30

T5_BUCKETS = 32
T5_MAX_EXACT = T5_BUCKETS // 2
T5_MAX_DISTANCE = 1024

DIFF_HEADS = 4
DIFF_HEAD_DIM = 64
DIFF_QK_WIDTH = DIFF_HEADS * 2 * DIFF_HEAD_DIM
DIFF_V_WIDTH = DIFF_HEADS * 2 * DIFF_HEAD_DIM

MOBA_HEADS = 4
MOBA_HEAD_DIM = 128
MOBA_BLOCK = 256
MOBA_TOPK = 3
MOBA_Q_CHUNK = 32
MOBA_WIDTH = MOBA_HEADS * MOBA_HEAD_DIM

MLA_HEADS = 8
MLA_Q_RANK = 256
MLA_KV_RANK = 128
MLA_NOPE_DIM = 64
MLA_ROPE_DIM = 32
MLA_V_DIM = 64
MLA_WIDTH = MLA_HEADS * MLA_V_DIM
ROPE_THETA = 10000.0

N_BRANCH = 3
BRANCH_WIDTH = 512
N_BIAS_HEADS = DIFF_HEADS + MOBA_HEADS
D_FF = 4 * D_MODEL

IN_SPLITS = (DIFF_QK_WIDTH, DIFF_QK_WIDTH, DIFF_V_WIDTH,
             MOBA_WIDTH, MOBA_WIDTH, MOBA_WIDTH,
             MLA_Q_RANK, MLA_KV_RANK, MLA_ROPE_DIM,
             N_BRANCH * D_MODEL)
IN_OFFSETS = tuple(sum(IN_SPLITS[:i + 1]) for i in range(len(IN_SPLITS) - 1))
D_IN = sum(IN_SPLITS)


def _rms_norm(x, w):
    xf = x.astype(jnp.float32)
    y = xf * lax.rsqrt(jnp.mean(xf * xf, axis=-1, keepdims=True) + RMS_EPS)
    return (y * w.astype(jnp.float32)).astype(x.dtype)

def _t5_bucket(rel):
    n = jnp.maximum(rel, 0)
    nf = jnp.maximum(n, 1).astype(jnp.float32)
    large = T5_MAX_EXACT + (jnp.log(nf / T5_MAX_EXACT)
                            / math.log(T5_MAX_DISTANCE / T5_MAX_EXACT)
                            * (T5_BUCKETS - T5_MAX_EXACT)).astype(jnp.int32)
    large = jnp.minimum(large, T5_BUCKETS - 1)
    return jnp.where(n < T5_MAX_EXACT, n, large)

def _rope(x, positions):
    d = x.shape[-1]
    half = d // 2
    inv_freq = ROPE_THETA ** (-jnp.arange(half, dtype=jnp.float32) * 2.0 / d)
    ang = positions.astype(jnp.float32)[:, :, None, None] * inv_freq
    cos, sin = jnp.cos(ang), jnp.sin(ang)
    xf = x.astype(jnp.float32)
    x1, x2 = xf[..., :half], xf[..., half:]
    return jnp.concatenate([x1 * cos - x2 * sin, x2 * cos + x1 * sin], axis=-1).astype(x.dtype)

def _diff_attention(q1, q2, k1, k2, v, lam, bias_table):
    B, S, H, dh = q1.shape
    scale = 1.0 / math.sqrt(dh)
    k_pos = jnp.arange(S)
    table = bias_table.astype(jnp.float32)

    def block(c):
        start = c * Q_BLOCK
        q_pos = start + jnp.arange(Q_BLOCK)
        rel = q_pos[:, None] - k_pos[None, :]
        bias = jnp.transpose(table[_t5_bucket(rel)], (2, 0, 1))
        visible = rel >= 0

        def probs(q, k):
            qb = lax.dynamic_slice_in_dim(q, start, Q_BLOCK, axis=1)
            s = jnp.einsum('bqhd,bkhd->bhqk', qb, k).astype(jnp.float32) * scale + bias
            return jax.nn.softmax(jnp.where(visible, s, NEG_INF), axis=-1)

        w = probs(q1, k1) - lam * probs(q2, k2)
        return jnp.einsum('bhqk,bkhd->bqhd', w.astype(v.dtype), v)

    out = lax.map(block, jnp.arange(S // Q_BLOCK))
    return jnp.transpose(out, (1, 0, 2, 3, 4)).reshape(B, S, H, v.shape[-1])

def _moba_attention(q, k, v, bias_table):
    B, S, H, d = q.shape
    scale = 1.0 / math.sqrt(d)
    n_blk = -(-S // MOBA_BLOCK)
    s_pad = n_blk * MOBA_BLOCK
    topk = min(MOBA_TOPK, n_blk)
    pad = ((0, 0), (0, s_pad - S), (0, 0), (0, 0))
    kbh = jnp.transpose(jnp.pad(k, pad).reshape(B, n_blk, MOBA_BLOCK, H, d), (0, 3, 1, 2, 4))
    vbh = jnp.transpose(jnp.pad(v, pad).reshape(B, n_blk, MOBA_BLOCK, H, d), (0, 3, 1, 2, 4))
    k_mean = jnp.mean(kbh.astype(jnp.float32), axis=3)
    blk_ids = jnp.arange(n_blk)
    offs = jnp.arange(MOBA_BLOCK)
    table = bias_table.astype(jnp.float32)
    table_t = table.T
    bi = jnp.arange(B)[:, None, None, None]
    hi = jnp.arange(H)[None, :, None, None]
    hi5 = jnp.arange(H)[None, :, None, None, None]

    def chunk(c):
        start = c * MOBA_Q_CHUNK
        own = start // MOBA_BLOCK
        q_pos = start + jnp.arange(MOBA_Q_CHUNK)
        qbt = jnp.transpose(lax.dynamic_slice_in_dim(q, start, MOBA_Q_CHUNK, axis=1), (0, 2, 1, 3))
        gate = jnp.einsum('bhqd,bhnd->bhqn', qbt.astype(jnp.float32), k_mean)
        gate = jnp.where(blk_ids < own, gate, NEG_INF)
        _, idx = lax.top_k(gate, topk)
        valid = idx < own
        k_sel = kbh[bi, hi, idx]
        v_sel = vbh[bi, hi, idx]
        s_sel = jnp.einsum('bhqd,bhqnld->bhqnl', qbt, k_sel).astype(jnp.float32) * scale
        sel_pos = idx[..., None] * MOBA_BLOCK + offs
        rel_sel = q_pos[None, None, :, None, None] - sel_pos
        s_sel = jnp.where(valid[..., None], s_sel + table_t[hi5, _t5_bucket(rel_sel)], NEG_INF)
        k_own = lax.dynamic_index_in_dim(kbh, own, axis=2, keepdims=False)
        v_own = lax.dynamic_index_in_dim(vbh, own, axis=2, keepdims=False)
        rel_own = q_pos[:, None] - (own * MOBA_BLOCK + offs)[None, :]
        bias_own = jnp.transpose(table[_t5_bucket(rel_own)], (2, 0, 1))
        s_own = jnp.einsum('bhqd,bhld->bhql', qbt, k_own).astype(jnp.float32) * scale + bias_own
        s_own = jnp.where(rel_own >= 0, s_own, NEG_INF)
        n_sel = topk * MOBA_BLOCK
        s = jnp.concatenate([s_sel.reshape(B, H, MOBA_Q_CHUNK, n_sel), s_own], axis=-1)
        p = jax.nn.softmax(s, axis=-1).astype(v.dtype)
        p_sel = p[..., :n_sel].reshape(B, H, MOBA_Q_CHUNK, topk, MOBA_BLOCK)
        p_own = p[..., n_sel:]
        return (jnp.einsum('bhqnl,bhqnld->bqhd', p_sel, v_sel)
                + jnp.einsum('bhql,bhld->bqhd', p_own, v_own))

    out = lax.map(chunk, jnp.arange(S // MOBA_Q_CHUNK))
    return jnp.transpose(out, (1, 0, 2, 3, 4)).reshape(B, S, H, d)

def _dense_causal_attention(q, k, v, scale):
    B, S, H, _ = q.shape
    k_pos = jnp.arange(S)

    def block(c):
        start = c * Q_BLOCK
        qb = lax.dynamic_slice_in_dim(q, start, Q_BLOCK, axis=1)
        s = jnp.einsum('bqhd,bkhd->bhqk', qb, k).astype(jnp.float32) * scale
        rel = (start + jnp.arange(Q_BLOCK))[:, None] - k_pos[None, :]
        p = jax.nn.softmax(jnp.where(rel >= 0, s, NEG_INF), axis=-1).astype(v.dtype)
        return jnp.einsum('bhqk,bkhd->bqhd', p, v)

    out = lax.map(block, jnp.arange(S // Q_BLOCK))
    return jnp.transpose(out, (1, 0, 2, 3, 4)).reshape(B, S, H, v.shape[-1])

def first_inputs(seed: int = 0) -> dict:
    key = jax.random.key(seed)
    ks = jax.random.split(key, 20)

    def nrm(k, shape, scale):
        return jax.random.normal(k, shape, jnp.float32) * scale

    x = nrm(ks[0], (BATCH, SEQ, D_MODEL), 1.0)
    offsets = jax.random.randint(ks[1], (BATCH, 1), 0, 4096, dtype=jnp.int32)
    positions = offsets + jnp.arange(SEQ, dtype=jnp.int32)[None, :]
    return {
        'x': x,
        'positions': positions,
        'rel_bias': nrm(ks[2], (T5_BUCKETS, N_BIAS_HEADS), 0.5),
        'norm_mix_pre': 1.0 + nrm(ks[3], (DEPTH, D_MODEL), 0.05),
        'norm_mix_post': 1.0 + nrm(ks[4], (DEPTH, D_MODEL), 0.05),
        'norm_mlp_pre': 1.0 + nrm(ks[5], (DEPTH, D_MODEL), 0.05),
        'norm_mlp_post': 1.0 + nrm(ks[6], (DEPTH, D_MODEL), 0.05),
        'w_in': nrm(ks[7], (DEPTH, D_MODEL, D_IN), D_MODEL ** -0.5),
        'diff_lambda': nrm(ks[8], (DEPTH, 4, DIFF_HEAD_DIM), 0.1),
        'diff_subln': 1.0 + nrm(ks[9], (DEPTH, 2 * DIFF_HEAD_DIM), 0.05),
        'mla_q_norm': 1.0 + nrm(ks[10], (DEPTH, MLA_Q_RANK), 0.05),
        'mla_w_uq': nrm(ks[11], (DEPTH, MLA_Q_RANK, MLA_HEADS * (MLA_NOPE_DIM + MLA_ROPE_DIM)), MLA_Q_RANK ** -0.5),
        'mla_kv_norm': 1.0 + nrm(ks[12], (DEPTH, MLA_KV_RANK), 0.05),
        'mla_w_ukv': nrm(ks[13], (DEPTH, MLA_KV_RANK, MLA_HEADS * (MLA_NOPE_DIM + MLA_V_DIM)), MLA_KV_RANK ** -0.5),
        'w_branch': nrm(ks[14], (DEPTH, N_BRANCH, BRANCH_WIDTH, D_MODEL), BRANCH_WIDTH ** -0.5),
        'w_out': nrm(ks[15], (DEPTH, D_MODEL, D_MODEL), D_MODEL ** -0.5),
        'w_up': nrm(ks[16], (DEPTH, D_MODEL, D_FF), D_MODEL ** -0.5),
        'w_down': nrm(ks[17], (DEPTH, D_FF, D_MODEL), D_FF ** -0.5),
    }

def first_block(x, positions, rel_bias, norm_mix_pre, norm_mix_post, norm_mlp_pre, norm_mlp_post,
              w_in, diff_lambda, diff_subln, mla_q_norm, mla_w_uq, mla_kv_norm, mla_w_ukv,
              w_branch, w_out, w_up, w_down):
    B, S, _ = x.shape
    for l in range(DEPTH):
        lam_init = 0.8 - 0.6 * math.exp(-0.3 * l)
        h = _rms_norm(x, norm_mix_pre[l])
        proj = jnp.einsum('bsd,de->bse', h, w_in[l])
        dq, dk, dv, mq, mk, mv, c_q, c_kv, k_pe, g = jnp.split(proj, IN_OFFSETS, axis=-1)

        dq = dq.reshape(B, S, DIFF_HEADS, 2, DIFF_HEAD_DIM)
        dk = dk.reshape(B, S, DIFF_HEADS, 2, DIFF_HEAD_DIM)
        dv = dv.reshape(B, S, DIFF_HEADS, 2 * DIFF_HEAD_DIM)
        lam_vecs = diff_lambda[l].astype(jnp.float32)
        lam = (jnp.exp(jnp.sum(lam_vecs[0] * lam_vecs[1]))
               - jnp.exp(jnp.sum(lam_vecs[2] * lam_vecs[3])) + lam_init)
        oa = _diff_attention(dq[..., 0, :], dq[..., 1, :], dk[..., 0, :], dk[..., 1, :], dv,
                             lam, rel_bias[:, :DIFF_HEADS])
        oa = (_rms_norm(oa, diff_subln[l]) * (1.0 - lam_init)).reshape(B, S, DIFF_V_WIDTH)

        ob = _moba_attention(mq.reshape(B, S, MOBA_HEADS, MOBA_HEAD_DIM),
                             mk.reshape(B, S, MOBA_HEADS, MOBA_HEAD_DIM),
                             mv.reshape(B, S, MOBA_HEADS, MOBA_HEAD_DIM),
                             rel_bias[:, DIFF_HEADS:]).reshape(B, S, MOBA_WIDTH)

        q = jnp.einsum('bsr,re->bse', _rms_norm(c_q, mla_q_norm[l]), mla_w_uq[l])
        q = q.reshape(B, S, MLA_HEADS, MLA_NOPE_DIM + MLA_ROPE_DIM)
        q = jnp.concatenate([q[..., :MLA_NOPE_DIM], _rope(q[..., MLA_NOPE_DIM:], positions)], axis=-1)
        kv = jnp.einsum('bsr,re->bse', _rms_norm(c_kv, mla_kv_norm[l]), mla_w_ukv[l])
        kv = kv.reshape(B, S, MLA_HEADS, MLA_NOPE_DIM + MLA_V_DIM)
        k_rope = jnp.broadcast_to(_rope(k_pe[:, :, None, :], positions), (B, S, MLA_HEADS, MLA_ROPE_DIM))
        k = jnp.concatenate([kv[..., :MLA_NOPE_DIM], k_rope], axis=-1)
        oc = _dense_causal_attention(q, k, kv[..., MLA_NOPE_DIM:],
                                     1.0 / math.sqrt(MLA_NOPE_DIM + MLA_ROPE_DIM)).reshape(B, S, MLA_WIDTH)

        branches = jnp.stack([oa, ob, oc], axis=2)
        br = jnp.einsum('bsgc,gcd->bsgd', branches, w_branch[l])
        gates = jax.nn.sigmoid(g.reshape(B, S, N_BRANCH, D_MODEL))
        mixed = jnp.einsum('bsd,de->bse', jnp.sum(gates * br, axis=2), w_out[l])
        x = x + _rms_norm(mixed, norm_mix_post[l])

        h = _rms_norm(x, norm_mlp_pre[l])
        u = jnp.square(jax.nn.relu(jnp.einsum('bsd,df->bsf', h, w_up[l])))
        x = x + _rms_norm(jnp.einsum('bsf,fd->bsd', u, w_down[l]), norm_mlp_post[l])
    return x


PLE_DIM = 256
MIX_WIDTH = D_MODEL
N_EVEN = (DEPTH + 1) // 2
N_ODD = DEPTH // 2
DEEPNORM_ALPHA = (2.0 * DEPTH) ** 0.25
DEEPNORM_BETA = (8.0 * DEPTH) ** -0.25
LN_EPS = 1e-5

DN_HEADS = 4
DN_DK = 128
DN_DV = 128
DN_WIDTH = DN_HEADS * DN_DV
DN_QKV = 2 * DN_HEADS * DN_DK + DN_WIDTH
DN_AB = 4 * DN_HEADS
DN_CONV = 5
DN_CHUNK = 64

RK_HEADS = 8
RK_HEAD = 64
RK_WIDTH = RK_HEADS * RK_HEAD
RK_DECAY_LORA = 64
RK_ICLR_LORA = 64
RK_SHIFT = 3 * RK_WIDTH + 2 * RK_DECAY_LORA + RK_ICLR_LORA
RK_GN_EPS = 64e-5

EVEN_SPLITS = [DN_QKV, DN_QKV + DN_AB, DN_QKV + DN_AB + DN_WIDTH, DN_QKV + DN_AB + DN_WIDTH + RK_SHIFT]
EVEN_IN = DN_QKV + DN_AB + DN_WIDTH + RK_SHIFT + RK_WIDTH
RK_SPLITS = [RK_WIDTH, 2 * RK_WIDTH, 3 * RK_WIDTH, 3 * RK_WIDTH + RK_DECAY_LORA, 3 * RK_WIDTH + 2 * RK_DECAY_LORA]

HY_WIDTH = MIX_WIDTH
HY_ORDER = 2
HY_SHORT = 3
HY_EMB = 33
HY_FILTER_WIDTH = 64
HY_N_FILTERS = HY_ORDER * 2 * HY_WIDTH
HY_TARGET = 1e-2
HY_FAST_PCT = 0.3
HY_SLOW_PCT = 1.5
ODD_IN = (HY_ORDER + 1) * HY_WIDTH + HY_WIDTH


def layer_norm(u, g, b):
    uf = u.astype(jnp.float32)
    mu = jnp.mean(uf, -1, keepdims=True)
    var = jnp.mean(jnp.square(uf - mu), -1, keepdims=True)
    return ((uf - mu) * lax.rsqrt(var + LN_EPS) * g + b).astype(u.dtype)

def rms_norm(u, g):
    uf = u.astype(jnp.float32)
    return (uf * lax.rsqrt(jnp.mean(jnp.square(uf), -1, keepdims=True) + RMS_EPS) * g).astype(u.dtype)

def l2_normalize(u):
    return u * lax.rsqrt(jnp.sum(jnp.square(u), -1, keepdims=True) + RMS_EPS)

def dwconv_centred(u, w, b=None):
    width = w.shape[0]
    pad = width // 2
    y = lax.conv_general_dilated(u, w.astype(u.dtype)[:, None, :], window_strides=(1,), padding=[(pad, pad)],
                                 dimension_numbers=('NWC', 'WIO', 'NWC'), feature_group_count=u.shape[-1])
    return y if b is None else y + b.astype(u.dtype)

def bidir_token_shift(s, mu):
    prev = jnp.pad(s, ((0, 0), (1, 0), (0, 0)))[:, :-1]
    nxt = jnp.pad(s, ((0, 0), (0, 1), (0, 0)))[:, 1:]
    return s + mu[0] * (prev - s) + mu[1] * (nxt - s)

def gated_delta_chunked(q, k, v, g, beta):
    bsz, heads, seq, dk = q.shape
    dv = v.shape[-1]
    c = DN_CHUNK
    n = seq // c
    q = q * (dk ** -0.5)
    chunks = lambda t: t.reshape(bsz, heads, n, c, *t.shape[3:])
    q, k, v, g, beta = chunks(q), chunks(k), chunks(v), chunks(g), chunks(beta)
    g = jnp.cumsum(g, axis=-1)
    incl = jnp.tril(jnp.ones((c, c), dtype=bool))
    strict = jnp.tril(jnp.ones((c, c), dtype=bool), -1)
    decay = jnp.exp(jnp.where(incl, g[..., :, None] - g[..., None, :], -jnp.inf))
    k_beta = k * beta[..., None]
    kk = jnp.einsum('bhnid,bhnjd->bhnij', k_beta, k) * decay
    t_mat = jnp.where(strict, kk, 0.0) + jnp.eye(c, dtype=q.dtype)
    u = lax.linalg.triangular_solve(t_mat, v * beta[..., None], left_side=True, lower=True, unit_diagonal=True)
    w = lax.linalg.triangular_solve(t_mat, k_beta * jnp.exp(g)[..., None], left_side=True, lower=True, unit_diagonal=True)
    qk = jnp.einsum('bhnid,bhnjd->bhnij', q, k) * decay
    q_dec = q * jnp.exp(g)[..., None]
    g_last = g[..., -1]
    k_tail = k * jnp.exp(g_last[..., None] - g)[..., None]

    def step(state, xs):
        u_n, w_n, qd_n, qk_n, kt_n, gl_n = xs
        v_new = u_n - jnp.einsum('bhck,bhkv->bhcv', w_n, state)
        o_n = jnp.einsum('bhck,bhkv->bhcv', qd_n, state) + jnp.einsum('bhij,bhjv->bhiv', qk_n, v_new)
        state = state * jnp.exp(gl_n)[..., None, None] + jnp.einsum('bhck,bhcv->bhkv', kt_n, v_new)
        return state, o_n

    xs = tuple(jnp.moveaxis(t, 2, 0) for t in (u, w, q_dec, qk, k_tail, g_last))
    s0 = jnp.zeros((bsz, heads, dk, dv), jnp.float32)
    _, o = lax.scan(step, s0, xs)
    return jnp.moveaxis(o, 0, 2).reshape(bsz, heads, seq, dv)

def rwkv7_scan(r, w, k, v, a, b):
    bsz, seq, heads, hd = r.shape

    def step(state, xs):
        r_t, w_t, k_t, v_t, a_t, b_t = xs
        sa = jnp.einsum('bhvk,bhk->bhv', state, a_t)
        state = state * w_t[:, :, None, :] + sa[..., None] * b_t[:, :, None, :] + v_t[..., None] * k_t[:, :, None, :]
        return state, jnp.einsum('bhvk,bhk->bhv', state, r_t)

    xs = tuple(jnp.moveaxis(t.astype(jnp.float32), 1, 0) for t in (r, w, k, v, a, b))
    _, y = lax.scan(step, jnp.zeros((bsz, heads, hd, hd), jnp.float32), xs)
    return jnp.moveaxis(y, 0, 1)

def rwkv_decay(wd, w0, w2):
    w_log = -jax.nn.softplus(-(w0 + jnp.tanh(wd) @ w2)) - 0.5
    return jnp.exp(-jnp.exp(w_log))

def hyena_position_features(seq):
    bands = (HY_EMB - 1) // 2
    t = jnp.linspace(0.0, 1.0, seq, dtype=jnp.float32)[:, None]
    f = jnp.linspace(1e-4, bands - 1, bands, dtype=jnp.float32)[None, :]
    ang = (2.0 * math.pi / seq) * jnp.arange(seq, dtype=jnp.float32)[:, None] * f
    return jnp.concatenate([t, jnp.cos(ang), -jnp.sin(ang)], axis=-1), t

def hyena_filters(seq, w1, b1, w2, b2, w3, b3, freq, w_out, deltas):
    f32 = jnp.float32
    feats, t = hyena_position_features(seq)
    freq = freq.astype(f32)
    hdn = jnp.sin(freq * (feats @ w1.astype(f32) + b1.astype(f32)))
    hdn = jnp.sin(freq * (hdn @ w2.astype(f32) + b2.astype(f32)))
    hdn = jnp.sin(freq * (hdn @ w3.astype(f32) + b3.astype(f32)))
    h = (hdn @ w_out.astype(f32)) * jnp.exp(-t * jnp.abs(deltas.astype(f32)))
    h = h.reshape(seq, HY_ORDER, 2, HY_WIDTH)
    fwd, bwd = h[:, :, 0], h[:, :, 1]
    circ = jnp.concatenate([fwd, jnp.zeros_like(fwd[:1]), jnp.flip(bwd[1:], axis=0)], axis=0)
    return circ / (jnp.sum(jnp.abs(circ), axis=0, keepdims=True) + RMS_EPS)

def fft_long_conv(u, filt):
    seq = u.shape[1]
    u_f = jnp.fft.rfft(u, n=2 * seq, axis=1)
    h_f = jnp.fft.rfft(filt, axis=0)
    return jnp.fft.irfft(u_f * h_f[None], n=2 * seq, axis=1)[:, :seq]

def even_mixer(x, w_in, dn_conv, dn_a_log, dn_dt_bias, dn_norm, rk_mu, rk_w0, rk_w2, rk_a0, rk_a2,
               rk_k_k, rk_k_a, rk_r_k, rk_ln_w, rk_ln_b):
    bsz, seq, _ = x.shape
    f32 = jnp.float32
    proj = x @ w_in
    dn_qkv, dn_ab, dn_gate, rk_in, rk_gate = jnp.split(proj, EVEN_SPLITS, axis=-1)

    qkv = jax.nn.silu(dwconv_centred(dn_qkv, dn_conv)).astype(f32)
    q, k, v = jnp.split(qkv, [DN_HEADS * DN_DK, 2 * DN_HEADS * DN_DK], axis=-1)
    q = l2_normalize(q.reshape(bsz, seq, DN_HEADS, DN_DK)).transpose(0, 2, 1, 3)
    k = l2_normalize(k.reshape(bsz, seq, DN_HEADS, DN_DK)).transpose(0, 2, 1, 3)
    v = v.reshape(bsz, seq, DN_HEADS, DN_DV).transpose(0, 2, 1, 3)
    ab = dn_ab.astype(f32).reshape(bsz, seq, 4, DN_HEADS).transpose(2, 0, 3, 1)
    g = -jnp.exp(dn_a_log.astype(f32))[:, None, :, None] * jax.nn.softplus(ab[:2] + dn_dt_bias.astype(f32)[:, None, :, None])
    beta = jax.nn.sigmoid(ab[2:])
    flip_l = lambda t: jnp.flip(t, axis=2)
    o = gated_delta_chunked(q, k, v, g[0], beta[0]) + flip_l(
        gated_delta_chunked(flip_l(q), flip_l(k), flip_l(v), flip_l(g[1]), flip_l(beta[1])))
    o = rms_norm(o.transpose(0, 2, 1, 3), dn_norm).reshape(bsz, seq, DN_WIDTH)
    y_dn = o.astype(x.dtype) * jax.nn.silu(dn_gate)

    s = bidir_token_shift(rk_in, rk_mu).astype(f32)
    r, k, v, wd_f, wd_b, a_d = jnp.split(s, RK_SPLITS, axis=-1)
    w_f = rwkv_decay(wd_f, rk_w0[0], rk_w2[0])
    w_b = rwkv_decay(wd_b, rk_w0[1], rk_w2[1])
    a = jax.nn.sigmoid(rk_a0 + a_d @ rk_a2)
    heads = lambda t: t.reshape(bsz, seq, RK_HEADS, RK_HEAD)
    kk = l2_normalize(heads(k * rk_k_k))
    k = k * (1.0 + (a - 1.0) * rk_k_a)
    r, k, v, a, w_f, w_b = heads(r), heads(k), heads(v), heads(a), heads(w_f), heads(w_b)
    a_vec = -kk
    b_vec = kk * a
    flip_t = lambda t: jnp.flip(t, axis=1)
    wkv = rwkv7_scan(r, w_f, k, v, a_vec, b_vec) + flip_t(
        rwkv7_scan(flip_t(r), flip_t(w_b), flip_t(k), flip_t(v), flip_t(a_vec), flip_t(b_vec)))
    mean = jnp.mean(wkv, -1, keepdims=True)
    var = jnp.mean(jnp.square(wkv - mean), -1, keepdims=True)
    wkv = ((wkv - mean) * lax.rsqrt(var + RK_GN_EPS)).reshape(bsz, seq, RK_WIDTH) * rk_ln_w + rk_ln_b
    bonus = (jnp.sum(r * k * rk_r_k, -1, keepdims=True) * v).reshape(bsz, seq, RK_WIDTH)
    y_rk = (wkv + bonus).astype(x.dtype) * jax.nn.silu(rk_gate)
    return jnp.concatenate([y_dn, y_rk], axis=-1)

def odd_mixer(x, w_in, conv_w, conv_b, f_w1, f_b1, f_w2, f_b2, f_w3, f_b3, f_freq, f_out, deltas, skip):
    bsz, seq, _ = x.shape
    f32 = jnp.float32
    proj = x @ w_in
    xv, gate = jnp.split(proj, [(HY_ORDER + 1) * HY_WIDTH], axis=-1)
    xv = dwconv_centred(xv, conv_w, conv_b).astype(f32)
    x1, x2, v = jnp.split(xv, 3, axis=-1)
    filt = hyena_filters(seq, f_w1, f_b1, f_w2, f_b2, f_w3, f_b3, f_freq, f_out, deltas)
    skip = skip.astype(f32)
    z = x1 * (fft_long_conv(v, filt[:, 0]) + skip[0] * v)
    y = x2 * (fft_long_conv(z, filt[:, 1]) + skip[1] * z)
    return y.astype(x.dtype) * jax.nn.silu(gate)

def second_inputs(seed: int = 0) -> dict:
    key = jax.random.key(seed)
    keys = iter(list(jax.random.split(key, 48)))
    f32 = jnp.float32
    nrm = lambda shape, scale: jax.random.normal(next(keys), shape, f32) * scale
    unif = lambda shape, lo, hi: jax.random.uniform(next(keys), shape, f32, lo, hi)
    x = nrm((BATCH, SEQ, D_MODEL), 1.0)
    p = nrm((DEPTH, BATCH, SEQ, PLE_DIM), 1.0)
    even_w_in = nrm((N_EVEN, D_MODEL, EVEN_IN), D_MODEL ** -0.5)
    dn_conv = nrm((N_EVEN, DN_CONV, DN_QKV), DN_CONV ** -0.5)
    dn_a_log = jnp.log(unif((N_EVEN, 2, DN_HEADS), 1.0, 16.0))
    dt = jnp.exp(unif((N_EVEN, 2, DN_HEADS), math.log(1e-3), math.log(1e-1)))
    dn_dt_bias = dt + jnp.log(-jnp.expm1(-dt))
    dn_norm = 1.0 + nrm((N_EVEN, DN_DV), 0.02)
    rk_mu = unif((N_EVEN, 2, RK_SHIFT), 0.0, 0.5)
    rk_w0 = unif((N_EVEN, 2, RK_WIDTH), -6.0, -1.0)
    rk_w2 = nrm((N_EVEN, 2, RK_DECAY_LORA, RK_WIDTH), 0.1 * RK_DECAY_LORA ** -0.5)
    rk_a0 = nrm((N_EVEN, RK_WIDTH), 0.1)
    rk_a2 = nrm((N_EVEN, RK_ICLR_LORA, RK_WIDTH), 0.5 * RK_ICLR_LORA ** -0.5)
    rk_k_k = 0.85 + nrm((N_EVEN, RK_WIDTH), 0.02)
    rk_k_a = 1.0 + nrm((N_EVEN, RK_WIDTH), 0.02)
    rk_r_k = -0.04 + nrm((N_EVEN, RK_HEADS, RK_HEAD), 0.1)
    rk_ln_w = 1.0 + nrm((N_EVEN, RK_WIDTH), 0.02)
    rk_ln_b = nrm((N_EVEN, RK_WIDTH), 0.02)
    odd_w_in = nrm((N_ODD, D_MODEL, ODD_IN), D_MODEL ** -0.5)
    hy_conv_w = nrm((N_ODD, HY_SHORT, (HY_ORDER + 1) * HY_WIDTH), HY_SHORT ** -0.5)
    hy_conv_b = nrm((N_ODD, (HY_ORDER + 1) * HY_WIDTH), 0.02)
    hy_ffn_w1 = nrm((N_ODD, HY_EMB, HY_FILTER_WIDTH), HY_EMB ** -0.5)
    hy_ffn_b1 = nrm((N_ODD, HY_FILTER_WIDTH), 0.1)
    hy_ffn_w2 = nrm((N_ODD, HY_FILTER_WIDTH, HY_FILTER_WIDTH), HY_FILTER_WIDTH ** -0.5)
    hy_ffn_b2 = nrm((N_ODD, HY_FILTER_WIDTH), 0.1)
    hy_ffn_w3 = nrm((N_ODD, HY_FILTER_WIDTH, HY_FILTER_WIDTH), HY_FILTER_WIDTH ** -0.5)
    hy_ffn_b3 = nrm((N_ODD, HY_FILTER_WIDTH), 0.1)
    hy_ffn_freq = 1.0 + nrm((N_ODD, HY_FILTER_WIDTH), 0.02)
    hy_ffn_out = nrm((N_ODD, HY_FILTER_WIDTH, HY_N_FILTERS), HY_FILTER_WIDTH ** -0.5)
    max_decay = math.log(HY_TARGET) / HY_FAST_PCT
    min_decay = math.log(HY_TARGET) / HY_SLOW_PCT
    base = jnp.abs(jnp.linspace(min_decay, max_decay, HY_WIDTH, dtype=f32))
    hy_deltas = jnp.tile(base, HY_ORDER * 2)[None] + nrm((N_ODD, HY_N_FILTERS), 0.01)
    hy_skip = nrm((N_ODD, HY_ORDER, HY_WIDTH), 0.5)
    w_out = nrm((DEPTH, MIX_WIDTH, D_MODEL), MIX_WIDTH ** -0.5 * DEEPNORM_BETA)
    ln_g = 1.0 + nrm((DEPTH, D_MODEL), 0.02)
    ln_b = nrm((DEPTH, D_MODEL), 0.02)
    ple_w = nrm((DEPTH, PLE_DIM, D_MODEL), PLE_DIM ** -0.5)
    ple_norm = 1.0 + nrm((DEPTH, D_MODEL), 0.02)
    ple_gate = nrm((DEPTH, D_MODEL, D_MODEL), D_MODEL ** -0.5)
    return {'x': x, 'p': p, 'even_w_in': even_w_in, 'dn_conv': dn_conv, 'dn_a_log': dn_a_log,
            'dn_dt_bias': dn_dt_bias, 'dn_norm': dn_norm, 'rk_mu': rk_mu, 'rk_w0': rk_w0, 'rk_w2': rk_w2,
            'rk_a0': rk_a0, 'rk_a2': rk_a2, 'rk_k_k': rk_k_k, 'rk_k_a': rk_k_a, 'rk_r_k': rk_r_k,
            'rk_ln_w': rk_ln_w, 'rk_ln_b': rk_ln_b, 'odd_w_in': odd_w_in, 'hy_conv_w': hy_conv_w,
            'hy_conv_b': hy_conv_b, 'hy_ffn_w1': hy_ffn_w1, 'hy_ffn_b1': hy_ffn_b1, 'hy_ffn_w2': hy_ffn_w2,
            'hy_ffn_b2': hy_ffn_b2, 'hy_ffn_w3': hy_ffn_w3, 'hy_ffn_b3': hy_ffn_b3, 'hy_ffn_freq': hy_ffn_freq,
            'hy_ffn_out': hy_ffn_out, 'hy_deltas': hy_deltas, 'hy_skip': hy_skip, 'w_out': w_out,
            'ln_g': ln_g, 'ln_b': ln_b, 'ple_w': ple_w, 'ple_norm': ple_norm, 'ple_gate': ple_gate}

def second_block(x, p, even_w_in, dn_conv, dn_a_log, dn_dt_bias, dn_norm, rk_mu, rk_w0, rk_w2, rk_a0, rk_a2,
              rk_k_k, rk_k_a, rk_r_k, rk_ln_w, rk_ln_b, odd_w_in, hy_conv_w, hy_conv_b, hy_ffn_w1, hy_ffn_b1,
              hy_ffn_w2, hy_ffn_b2, hy_ffn_w3, hy_ffn_b3, hy_ffn_freq, hy_ffn_out, hy_deltas, hy_skip,
              w_out, ln_g, ln_b, ple_w, ple_norm, ple_gate):
    h = x
    for i in range(DEPTH):
        j = i // 2
        if i % 2 == 0:
            mix = even_mixer(h, even_w_in[j], dn_conv[j], dn_a_log[j], dn_dt_bias[j], dn_norm[j], rk_mu[j],
                             rk_w0[j], rk_w2[j], rk_a0[j], rk_a2[j], rk_k_k[j], rk_k_a[j], rk_r_k[j],
                             rk_ln_w[j], rk_ln_b[j])
        else:
            mix = odd_mixer(h, odd_w_in[j], hy_conv_w[j], hy_conv_b[j], hy_ffn_w1[j], hy_ffn_b1[j],
                            hy_ffn_w2[j], hy_ffn_b2[j], hy_ffn_w3[j], hy_ffn_b3[j], hy_ffn_freq[j],
                            hy_ffn_out[j], hy_deltas[j], hy_skip[j])
        h = layer_norm(DEEPNORM_ALPHA * h + mix @ w_out[i], ln_g[i], ln_b[i])
        e = rms_norm(p[i] @ ple_w[i], ple_norm[i])
        h = h + jax.nn.sigmoid(h @ ple_gate[i]) * e
    return h


def setup_inputs(seed=0):
    out = dict(first_inputs(seed))
    for name, value in second_inputs(seed + 1).items():
        if name != "x":
            out[name + "_2"] = value
    return out


def reference(
    x, positions, rel_bias, norm_mix_pre, norm_mix_post, norm_mlp_pre, norm_mlp_post, w_in,
    diff_lambda, diff_subln, mla_q_norm, mla_w_uq, mla_kv_norm, mla_w_ukv, w_branch, w_out,
    w_up, w_down, p_2, even_w_in_2, dn_conv_2, dn_a_log_2, dn_dt_bias_2, dn_norm_2, rk_mu_2,
    rk_w0_2, rk_w2_2, rk_a0_2, rk_a2_2, rk_k_k_2, rk_k_a_2, rk_r_k_2, rk_ln_w_2, rk_ln_b_2,
    odd_w_in_2, hy_conv_w_2, hy_conv_b_2, hy_ffn_w1_2, hy_ffn_b1_2, hy_ffn_w2_2, hy_ffn_b2_2,
    hy_ffn_w3_2, hy_ffn_b3_2, hy_ffn_freq_2, hy_ffn_out_2, hy_deltas_2, hy_skip_2, w_out_2,
    ln_g_2, ln_b_2, ple_w_2, ple_norm_2, ple_gate_2,
):
    x = first_block(
        x, positions, rel_bias, norm_mix_pre, norm_mix_post, norm_mlp_pre, norm_mlp_post, w_in,
        diff_lambda, diff_subln, mla_q_norm, mla_w_uq, mla_kv_norm, mla_w_ukv, w_branch, w_out,
        w_up, w_down,
    )
    return second_block(
        x, p_2, even_w_in_2, dn_conv_2, dn_a_log_2, dn_dt_bias_2, dn_norm_2, rk_mu_2, rk_w0_2,
        rk_w2_2, rk_a0_2, rk_a2_2, rk_k_k_2, rk_k_a_2, rk_r_k_2, rk_ln_w_2, rk_ln_b_2,
        odd_w_in_2, hy_conv_w_2, hy_conv_b_2, hy_ffn_w1_2, hy_ffn_b1_2, hy_ffn_w2_2,
        hy_ffn_b2_2, hy_ffn_w3_2, hy_ffn_b3_2, hy_ffn_freq_2, hy_ffn_out_2, hy_deltas_2,
        hy_skip_2, w_out_2, ln_g_2, ln_b_2, ple_w_2, ple_norm_2, ple_gate_2,
    )


_drawn_inputs = setup_inputs


def setup_inputs(seed=0):
    import zlib

    import numpy as np

    out = dict(_drawn_inputs(seed))
    spreads = {}
    factors = {'mla_q_norm': 6.193,
     'mla_kv_norm': 3.008,
     'dn_a_log_2': 5.673,
     'dn_norm_2': 64.0,
     'rk_w2_2': 8.0,
     'rk_a0_2': 4.594,
     'rk_k_k_2': 24.247,
     'rk_k_a_2': 9.051,
     'rk_ln_w_2': 64.0,
     'rk_ln_b_2': 64.0,
     'hy_conv_b_2': 8.0,
     'hy_ffn_b1_2': 7.375,
     'hy_ffn_b2_2': 5.408,
     'hy_ffn_b3_2': 5.146,
     'hy_ffn_freq_2': 8.0,
     'hy_deltas_2': 5.603,
     'ple_norm_2': 4.477,
     'ln_g_2': 4.058,
     'ln_b_2': 3.922}
    for name, (base, spread) in spreads.items():
        noise = np.random.default_rng([zlib.crc32(name.encode()), seed]).standard_normal(out[name].shape)
        drawn = base * np.exp(spread * noise) if base else spread * noise
        out[name] = jnp.asarray(drawn.astype(out[name].dtype))
    for name, factor in factors.items():
        out[name] = (out[name] * factor).astype(out[name].dtype)
    return out
```

```python
import math

import numpy as np

import concourse.bass as bass
from concourse import mybir
from concourse.alu_op_type import AluOpType as ALU

FP32 = mybir.dt.float32
INT32 = mybir.dt.int32
ACT = mybir.ActivationFunctionType
AX = mybir.AxisListType

P = 128
S = 256
TT = S // P
D = 1024
KT = D // P
DEPTH = 2
D_FF = 4 * D
EPS_RMS = 1e-6
EPS_LN = 1e-5
EPS_GN = 64e-5
NEG = -1e30
DIFF_HEADS, MOBA_HEADS, MLA_HEADS = 4, 4, 8
Q_RANK, KV_RANK, NOPE, ROPE, VDIM = 256, 128, 64, 32, 64
WB = 512
N_BRANCH = 3
MLA_IN = 6 * WB
GATE_IN = MLA_IN + Q_RANK + KV_RANK + ROPE
BUCKETS = 32
N_BIAS = DIFF_HEADS + MOBA_HEADS
REL_W = S + P - 1
SCORE_W = S + P
ALPHA = (2.0 * DEPTH) ** 0.25
DN_HEADS, DN_CONV = 4, 5
DN_QKV = 3 * DN_HEADS * P
DN_AB = 4 * DN_HEADS
RK_HEADS, RK_W, LORA = 8, 512, 64
RK_PAIRS = RK_HEADS // 2
RK_SHIFT = 3 * RK_W + 3 * LORA
AB_IN = DN_QKV
DN_GATE_IN = AB_IN + DN_AB
RK_IN = DN_GATE_IN + WB
RK_GATE_IN = RK_IN + RK_SHIFT
HY_ORDER, HY_SHORT, HY_EMB, HY_F = 2, 3, 33, 64
HY_XV = 3 * D
PLE = 256
LEVELS = 7
BASE = 600
RING = 4
SLOT = 4096


class Mark:

    def __init__(self, queue, n, tag):
        self.queue, self.n, self.tag = queue, n, tag


class Buf:

    def __init__(self, ap=None):
        self.ap, self.free = ap, []


class Counter:

    def __init__(self, nc):
        self.nc, self.dry, self.tag, self.tags = nc, False, 0, 0
        self.queues, self.bufs, self.done = [], [], {}
        self.per, self.i, self.bank = {}, None, 0

    def buf(self, ap=None):
        b = Buf(ap)
        self.bufs.append(b)
        return b

    def value(self, m):
        if m.tag == 0:
            return m.n
        if m.tag == self.tag:
            return m.n + self.i * self.per[m.queue]
        count, per = self.done[m.tag]
        return m.n + (count - 1) * per[m.queue]

    def loop(self, count, body):
        self.tags += 1
        start = [q.n for q in self.queues]
        before = [b.free for b in self.bufs]
        bank = self.bank
        self.dry, self.tag = True, self.tags
        body(0)
        self.per = {q: q.n - n for q, n in zip(self.queues, start)}
        for q, n in zip(self.queues, start):
            q.n = n
        for b, old in zip(self.bufs, before):
            b.free = old + [Mark(m.queue, m.n - self.per[m.queue], m.tag) for m in b.free if m.tag == self.tag]
        self.bank = bank
        self.dry = False
        with self.nc.Fori(0, count) as i:
            self.i = i
            body(i)
        for q, n in zip(self.queues, start):
            q.n = n + count * self.per[q]
        self.done[self.tag] = (count, self.per)
        self.tag = 0


class Queue:

    def __init__(self, counter, engine, sem):
        self.c, self.engine, self.sem, self.n, self.seen = counter, engine, sem, 0, {}
        counter.queues.append(self)

    def mark(self):
        return Mark(self, self.n, self.c.tag)

    def wait(self, marks):
        if self.c.dry:
            return
        for m in marks:
            m = m.mark() if isinstance(m, Queue) else m
            value = self.c.value(m)
            key = (m.queue, m.tag if m.tag == self.c.tag else 0)
            n = m.n if key[1] else value
            if n <= self.seen.get(key, 0) or n == 0:
                continue
            assert n > 0
            self.seen[key] = n
            self.engine.wait_ge(m.queue.sem, value)

    def __call__(self, op, *args, after=(), inc=True, **kw):
        self.wait(after)
        if inc:
            self.n += 1
        if not self.c.dry:
            ins = op(*args, **kw)
            if inc:
                ins.then_inc(self.sem, 1)
        return self.mark()

    def dma(self, dsem, out, in_, after=()):
        self.wait(after)
        dsem.n += 16
        if not self.c.dry:
            self.engine.dma_start(out, in_).then_inc(dsem.sem, 16)
        return dsem.mark()


def const_tables():
    f32 = np.float32
    p = np.arange(P)[:, None]
    c = np.arange(P)[None, :]
    out = {}
    out["ident"] = (p == c)
    out["ones"] = np.ones((P, P))
    out["pairs"] = (p // 64 == c // 64)
    out["flip"] = (p + c == P - 1)
    causal = lambda off: np.where(off + p - np.arange(S)[None, :] >= 0, 0.0, NEG)
    out["causal"] = np.concatenate([causal(P), causal(0)[:, :P]], 1)
    incl = [(c >= p), (c <= p)]
    strict = [(c > p), (c < p)]
    for d in range(2):
        out[f"incl{d}"] = incl[d]
        out[f"strict{d}"] = strict[d]
        out[f"rk_mask{d}"] = np.concatenate([-1.0 * strict[d], incl[d], strict[d], incl[d]], 1)
        for lv in range(LEVELS):
            b = 1 << lv
            same = (p // (2 * b) == c // (2 * b))
            m = same & (c // b % 2 == 1) & (p // b % 2 == 0)
            out[f"level{d}_{lv}"] = m if d == 0 else m.T
    fresh = np.ones((P, 4 * S))
    fresh[:, ::P] = 0.0
    out["fresh"] = fresh
    out["head_sel"] = (p // 64 == np.arange(2)[None, :])
    rel = S - 1 - np.arange(REL_W)
    n = np.maximum(rel, 0)
    nf = np.maximum(n, 1).astype(f32)
    large = 16 + (np.log(nf / f32(16)).astype(f32) / f32(math.log(1024 / 16)) * f32(16)).astype(np.int32)
    bucket = np.where(n < 16, n, np.minimum(large, BUCKETS - 1))
    onehot = np.zeros((P, REL_W))
    onehot[bucket, np.arange(REL_W)] = 1.0
    onehot[:, rel < 0] = 0.0
    onehot[BUCKETS, rel < 0] = NEG
    out["bucket"] = onehot
    inv = np.power(f32(10000.0), -np.arange(ROPE // 2, dtype=f32) * f32(2.0) / f32(ROPE)).astype(f32)
    out["inv_freq"] = np.repeat(inv[None, :], P, 0)
    lam = [0.8 - 0.6 * math.exp(-0.3 * l) for l in range(DEPTH)]
    out["lam"] = np.repeat(np.array([[v for x in lam for v in (x, 1.0 - x)]]), P, 0)
    t = np.arange(S)[:, None]
    f = np.arange(S)[None, :]
    ang = 2.0 * np.pi * ((t * f) % (2 * S)) / (2 * S)
    alt = np.where(np.arange(S) % 2 == 0, 1.0, -1.0)
    tiles = lambda m: m.reshape(TT, P, -1).transpose(1, 0, 2).reshape(P, -1)
    re, im = np.cos(ang), -np.sin(ang)
    im[:, 0] = 0.0
    im_u, re_2 = im.copy(), re[:, :P].copy()
    im_u[:, 0] = alt
    re_2[:, 0] = alt
    out["dft_re"] = tiles(re)
    out["dft_im_signal"] = tiles(im_u)
    out["dft_im_filter0"] = tiles(im[:, :P])
    out["dft_re_cross0"] = tiles(re_2)
    ire = np.cos(ang.T) * 2.0 / (2 * S)
    ire[0] /= 2.0
    iim = -np.sin(ang.T) * 2.0 / (2 * S)
    iim[0] = alt / (2 * S)
    out["idft"] = np.concatenate([tiles(ire), tiles(iim)], 1)
    out["minus_t"] = tiles(-np.linspace(0.0, 1.0, S, dtype=f32)[:, None])
    tl = np.linspace(0.0, 1.0, S, dtype=f32)[:, None]
    fb = np.linspace(1e-4, 15, 16, dtype=f32)[None, :]
    an = (f32(2.0 * math.pi / S) * np.arange(S, dtype=f32)[:, None] * fb).astype(f32)
    feats = np.zeros((P, S))
    feats[:HY_EMB] = np.concatenate([tl, np.cos(an), -np.sin(an)], -1).T
    out["feats"] = feats
    stage = lambda name: ("all" if name in ("ident", "ones", "pairs", "head_sel") else
                          "first" if name in ("flip", "causal", "bucket", "inv_freq", "lam") else
                          "even" if name[:4] in ("incl", "stri", "rk_m", "leve", "fres") else "odd")
    return {which: {name: np.ascontiguousarray(v, dtype=f32) for name, v in out.items() if stage(name) == which}
            for which in ("all", "first", "even", "odd")}


def offsets(sets):
    out, most, start = {}, 0, 0
    for which, tables in sets.items():
        at = start
        for name, a in tables.items():
            out[name] = (at, a.shape[1])
            at += a.shape[1]
        if which == "all":
            start = at
        most = max(most, at)
    return out, most


class Core:

    def __init__(self, nc, dram, table_at, table_words):
        self.nc, self.dram, self.table_at = nc, dram, table_at
        c = self.c = Counter(nc)
        sem = nc.alloc_semaphore
        self.T = Queue(c, nc.tensor, sem("tensor_done"))
        self.V = Queue(c, nc.vector, sem("vector_done"))
        self.A = Queue(c, nc.scalar, sem("scalar_done"))
        self.G = Queue(c, nc.gpsimd, sem("gpsimd_done"))
        self.SP = Queue(c, nc.sync, sem("sync_done"))
        self.slot_loaded = [Queue(c, None, sem(f"slot{k}_loaded")) for k in range(RING)]
        self.small_loaded = Queue(c, None, sem("small_loaded"))
        self.rows_loaded = Queue(c, None, sem("rows_loaded"))
        self.scratch_stored = Queue(c, None, sem("scratch_stored"))
        self.out_stored = Queue(c, None, sem("out_stored"))
        words = (nc.sbuf_usable_end - nc.sbuf_base) // 4 - 64
        self.words = words
        self.memory = nc.alloc_sbuf_tensor("memory", [P, words], FP32)
        self.top = 0
        self.banks = [c.buf(nc.alloc_psum_tensor(f"bank{k}", [P, 512], FP32)[:]) for k in range(8)]
        self.slots = [c.buf(self.take(SLOT)) for _ in range(RING)]
        self.next_slot = 0
        self.tables = self.take(table_words)

    def take(self, *dims):
        n = int(np.prod(dims))
        ap = self.memory[:, self.top:self.top + n]
        self.top += n
        assert self.top <= self.words, (self.top, self.words)
        return split(ap, *dims)

    def load_tables(self, which, after=()):
        src = self.dram[f"tables_{which}"]
        at = 0 if which == "all" else self.dram["tables_all"].shape[1]
        return self.SP.dma(self.small_loaded, self.tables[:, at:at + src.shape[1]], src, after=after)

    def table(self, name):
        at, n = self.table_at[name]
        return self.tables[:, at:at + n]

    def bank(self):
        b = self.banks[self.c.bank % 8]
        self.c.bank += 1
        return b

    def load_slot(self, parts, slot=None):
        if slot is None:
            slot = self.next_slot
            self.next_slot = (slot + 1) % RING
        b = self.slots[slot]
        for at, dims, src in parts:
            n = int(np.prod(dims))
            m = self.SP.dma(self.slot_loaded[slot], split(b.ap[:, at:at + n], *dims), src, after=b.free)
        return b, m

    def begin(self):
        nc, c = self.nc, self.c
        nc.all_engine_barrier()
        for q in c.queues:
            nc.sync.sem_clear(q.sem)
            q.n, q.seen = 0, {}
        for b in c.bufs:
            b.free = []
        nc.all_engine_barrier()
        for q in (self.T, self.V, self.A, self.G):
            q.engine.sem_inc(q.sem, BASE)
            q.n = BASE

    def matmul(self, out, lhsT, rhs, start, stop, after=(), inc=None):
        return self.T(self.nc.tensor.matmul, out, lhsT, rhs, start=start, stop=stop, after=after,
                      inc=stop if inc is None else inc)

    def transpose(self, out, in_, after=(), inc=True):
        return self.T(self.nc.tensor.transpose, out, in_, self.table("ident"), after=after, inc=inc)

    def feature_major(self, weights, ready, xT, columns, kt=KT):
        for m0 in range(0, columns, 2):
            b = self.bank()
            tiles = min(2, columns - m0)
            for j in range(tiles):
                for k in range(kt):
                    mark = self.matmul(b.ap[:, j * S:(j + 1) * S], weights(k, m0 + j), xT[:, k, :],
                                       start=k == 0, stop=k == kt - 1, after=[*b.free, *ready] if k == 0 else (),
                                       inc=k == kt - 1)
            yield m0, b, tiles, mark

    def token_major(self, weights, ready, xT, columns, kt=KT):
        for t in range(TT):
            b = self.bank()
            for k in range(kt):
                mark = self.matmul(b.ap[:, 0:columns], xT[:, k, t * P:(t + 1) * P], weights(k),
                                   start=k == 0, stop=k == kt - 1, after=[*b.free, *ready] if k == 0 else ())
            yield t, b, mark

    def copy(self, engine, out, in_, after=(), scale=None):
        nc = self.nc
        if engine is self.V:
            if scale is None:
                return self.V(nc.vector.tensor_copy, out, in_, after=after)
            return self.V(nc.vector.tensor_scalar, out, in_, scale, None, ALU.mult, after=after)
        if scale is None:
            return self.A(nc.scalar.activation, out, in_, ACT.Copy, after=after)
        return self.A(nc.scalar.activation, out, in_, ACT.Copy, scale=scale, after=after)

    def rstd(self, out, sums, n, eps, after):
        nc, V, A = self.nc, self.V, self.A
        V(nc.vector.tensor_scalar, out, sums, 1.0 / n, eps, ALU.mult, ALU.add, after=after)
        A(nc.scalar.activation, out, out, ACT.Sqrt, after=[V])
        return V(nc.vector.reciprocal, out, out, after=[A])

    def transposes(self, src, dstT, tiles, after, scale=None):
        for k0 in range(0, tiles, 2):
            b = self.bank()
            pair = min(2, tiles - k0)
            for j in range(pair):
                for t in range(TT):
                    self.transpose(b.ap[:, j * S + t * P:j * S + (t + 1) * P],
                                   src[:, t, (k0 + j) * P:(k0 + j + 1) * P],
                                   after=[*b.free, *after] if j + t == 0 else ())
            moved = self.T.mark()
            e = self.V if k0 % 4 == 0 else self.A
            if scale is None:
                self.copy(e, dstT[:, k0:k0 + pair, :], split(b.ap, 2, S)[:, 0:pair, :], after=[moved])
            else:
                for j in range(pair):
                    self.copy(e, dstT[:, k0 + j, :], b.ap[:, j * S:(j + 1) * S], after=[moved],
                              scale=scale[:, k0 + j:k0 + j + 1])
            b.free = [e.mark()]

    def add_normed(self, x, banks, row, row_ready, junk, stats):
        nc, V, A, G = self.nc, self.V, self.A, self.G
        for t in range(TT):
            for h in range(2):
                b, mark = banks[t][h]
                A(nc.scalar.activation, junk[:, t * 2 + h, :], b.ap, ACT.Square, after=[mark],
                  accum_out=stats[:, t * 2 + h:t * 2 + h + 1])
        sums = split(stats[:, 0:4], 2, 2)
        V(nc.vector.tensor_tensor, stats[:, 4:6], sums[:, :, 0], sums[:, :, 1], ALU.add, after=[A])
        self.rstd(stats[:, 6:8], stats[:, 4:6], D, EPS_RMS, after=[V])
        for t in range(TT):
            for h in range(2):
                b, mark = banks[t][h]
                m = V(nc.vector.scalar_tensor_tensor, junk[:, t * 2 + h, :], b.ap, stats[:, 6 + t:7 + t],
                      row[:, h * WB:(h + 1) * WB], ALU.mult, ALU.mult, after=[V, A, row_ready])
                b.free = [m]
                xs = x[:, t, h * WB:(h + 1) * WB]
                G(nc.gpsimd.tensor_tensor, xs, xs, junk[:, t * 2 + h, :], ALU.add, after=[m])

    def wrapped_sin(self, out, angle, turns, work, quarter, after):
        nc, V, A = self.nc, self.V, self.A
        magic = 1.5 * 2.0 ** 23
        V(nc.vector.tensor_scalar, turns, angle, 1.0 / (2.0 * math.pi), 0.25 * quarter, ALU.mult, ALU.add, after=after)
        V(nc.vector.tensor_scalar, turns, turns, magic, None, ALU.add, after=[V])
        V(nc.vector.tensor_scalar, turns, turns, -magic, None, ALU.add, after=[V])
        c1, c2 = 6.28125, 0.0019350051879882812
        c3 = 2.0 * math.pi - c1 - c2
        src = angle
        for c in (c1, c2, c3):
            V(nc.vector.scalar_tensor_tensor, work, turns, -c, src, ALU.mult, ALU.add, after=[V])
            src = work
        if quarter:
            V(nc.vector.tensor_scalar, work, work, 0.5 * math.pi * quarter, None, ALU.add, after=[V])
        V(nc.vector.tensor_scalar, work, work, PI_IN, -PI_IN, ALU.min, ALU.max, after=[V])
        return A(nc.scalar.activation, out, work, ACT.Sin, after=[V])


PI_IN = 3.1415925


def split(ap, *dims):
    if len(dims) == 1:
        return ap
    names = "abcde"[:len(dims)]
    return ap.rearrange(f"p ({' '.join(names)}) -> p {' '.join(names)}", **dict(zip(names, dims)))


def first_block(k, x):
    nc, T, V, A, G, SP = k.nc, k.T, k.V, k.A, k.G, k.SP
    dram, table, take = k.dram, k.table, k.take
    w_in = dram["w_in"].rearrange("l (k p) n -> p l k n", p=P)
    w_branch = dram["w_branch"].rearrange("l b (k p) n -> p l b k n", p=P)
    w_out = dram["w_out"].rearrange("l (k p) n -> p l k n", p=P)
    w_up = dram["w_up"].rearrange("l (k p) n -> p l k n", p=P)
    w_down = dram["w_down"].rearrange("l (k p) n -> p l k n", p=P)
    w_uq = dram["mla_w_uq"].rearrange("l (k p) n -> p l k n", p=P)
    w_ukv = dram["mla_w_ukv"].rearrange("l p n -> p l n")
    floor = k.top

    bias = take(N_BIAS, SCORE_W)
    cos, sin = take(TT, ROPE // 2), take(TT, ROPE // 2)
    cols = take(20)
    post = take(D)
    hT = take(KT, S)
    junk = take(4, WB)
    stats = take(64)
    qkT = take(4, 4, S)
    v_at = k.top
    diff_v, moba_v, mla_v = take(TT, WB), take(TT, WB), take(TT, WB)
    low = take(TT, Q_RANK + KV_RANK + ROPE)
    lowT = take(3, S)
    qnT, knT = take(4, S), take(4, S)
    qr, kr = take(TT, MLA_HEADS * ROPE), take(TT, P)
    qrT, krT = take(2, S), take(S)
    heads_out = take(TT, WB)
    branchT = take(N_BRANCH, 4, S)
    scores = [k.c.buf(take(SCORE_W)) for _ in range(4)]
    probsT = [k.c.buf(take(SCORE_W)) for _ in range(2)]
    lam = take(4, 64)
    over = qkT.rearrange("p a b c -> p (a b c)")
    mixT, upT = split(over[:, 0:D * TT], KT, S), split(over[:, D * TT:2 * D * TT], 2, 4, S)
    gateT = split(k.memory[:, v_at:v_at + 2 * D], 2, 4, S)

    k.begin()
    rel = diff_v[:, 0, 0:N_BIAS]
    k.load_tables("first")
    V(nc.vector.memset, rel, 1.0)
    SP.dma(k.small_loaded, diff_v[0:BUCKETS, 0, 0:N_BIAS], dram["rel_bias"], after=[V])
    b = k.bank()
    pos = diff_v[:, 1, 0:TT].bitcast(INT32)
    SP.dma(k.small_loaded, pos, dram["positions"])
    T(nc.tensor.matmul, b.ap[0:N_BIAS, 0:REL_W], diff_v[0:BUCKETS + 1, 0, 0:N_BIAS],
      table("bucket")[0:BUCKETS + 1, :], start=True, stop=True, after=[k.small_loaded])
    V(nc.vector.tensor_copy, moba_v[0:N_BIAS, 0, 0:REL_W], b.ap[0:N_BIAS, 0:REL_W], after=[T])
    diag = dram["diagonals"]
    SP.dma(k.scratch_stored, diag[:, 0:REL_W], moba_v[0:N_BIAS, 0, 0:REL_W], after=[V])
    for h in range(N_BIAS):
        row = diag[h:h + 1, :]
        skewed = qkT.rearrange("p a b c -> p (a b c)")[:, h * SCORE_W:(h + 1) * SCORE_W]
        for at, first, n in ((0, 0, S), (S, P, P)):
            SP.dma(k.small_loaded, skewed[:, at:at + n], bass.AP(tensor=row.tensor, offset=row.offset + first, ap=[[1, P], [1, n]]),
                   after=[k.scratch_stored])
    for h in range(N_BIAS):
        skewed = qkT.rearrange("p a b c -> p (a b c)")[:, h * SCORE_W:(h + 1) * SCORE_W]
        b = k.bank()
        k.matmul(b.ap[:, 0:SCORE_W], table("flip"), skewed, True, True, after=[k.small_loaded, *b.free])
        b.free = [k.copy(A, bias[:, h, :], b.ap[:, 0:SCORE_W], after=[T])]
    angle = moba_v[:, 1, 0:TT * 16]
    posf = moba_v[:, 1, 64:64 + TT]
    V(nc.vector.tensor_copy, posf, pos, after=[k.small_loaded])
    for t in range(TT):
        V(nc.vector.tensor_scalar, angle[:, t * 16:(t + 1) * 16], table("inv_freq"), posf[:, t:t + 1], None,
          ALU.mult, after=[V])
    turns, work = moba_v[:, 1, 128:160], moba_v[:, 1, 160:192]
    k.wrapped_sin(sin.rearrange("p a b -> p (a b)"), angle, turns, work, 0, after=[V])
    k.wrapped_sin(cos.rearrange("p a b -> p (a b)"), angle, turns, work, 1, after=[V, A])

    def layer(l):
        at = lambda ap: ap[:, bass.ds(l, 1)]
        k.begin()
        k.next_slot = 0
        cols_in = SP.dma(k.small_loaded, cols, at(dram["cols"])[:, 0, :])
        dl = dram["diff_lambda"][bass.ds(l, 1), :].partition_broadcast(P)
        SP.dma(k.small_loaded, lam.rearrange("p a b -> p (a b)"), dl[:, 0, :])
        post_in = SP.dma(k.rows_loaded, post, dram["norm_mix_post"][bass.ds(l, 1), :].partition_broadcast(P)[:, 0, :])

        normed_T(k, x, hT, cols[:, 0:8], junk, stats, after=[k.small_loaded])
        h_ready = [V.mark(), A.mark()]

        def piece(column, width=WB):
            return k.load_slot([(0, (KT, width), at(w_in)[:, 0, :, column:column + width])])

        for n, column in ((0, 0), (1, WB), (None, 2 * WB), (2, 3 * WB), (3, 4 * WB), (None, 5 * WB)):
            slot, loaded = piece(column)
            w = split(slot.ap, KT, WB)
            if n is None:
                dst = diff_v if column == 2 * WB else moba_v
                for t, b, mark in k.token_major(lambda kk: w[:, kk, :], [loaded, *h_ready], hT, WB):
                    e = (V, A)[t]
                    b.free = [k.copy(e, dst[:, t, :], b.ap, after=[mark])]
            else:
                for m0, b, _, mark in k.feature_major(lambda kk, m: w[:, kk, m * P:(m + 1) * P],
                                                      [loaded, *h_ready], hT, 4):
                    e = V if m0 else A
                    b.free = [k.copy(e, qkT[:, n, m0:m0 + 2, :], split(b.ap, 2, S), after=[mark])]
            slot.free = [T.mark()]
        width = Q_RANK + KV_RANK + ROPE
        slot, loaded = piece(MLA_IN, width)
        w = split(slot.ap[:, 0:KT * width], KT, width)
        for t, b, mark in k.token_major(lambda kk: w[:, kk, :], [loaded], hT, width):
            b.free = [k.copy((V, A)[t], low[:, t, :], b.ap[:, 0:width], after=[mark])]
        slot.free = [T.mark()]

        for t in range(TT):
            A(nc.scalar.activation, junk[:, 0, 0:Q_RANK], low[:, t, 0:Q_RANK], ACT.Square,
              accum_out=stats[:, 8 + t:9 + t], after=[V, A])
            A(nc.scalar.activation, junk[:, 0, 0:KV_RANK], low[:, t, Q_RANK:Q_RANK + KV_RANK], ACT.Square,
              accum_out=stats[:, 10 + t:11 + t], after=[A])
        k.rstd(stats[:, 12:14], stats[:, 8:10], Q_RANK, EPS_RMS, after=[A])
        k.rstd(stats[:, 14:16], stats[:, 10:12], KV_RANK, EPS_RMS, after=[A])
        for t in range(TT):
            V(nc.vector.tensor_scalar, low[:, t, 0:Q_RANK], low[:, t, 0:Q_RANK], stats[:, 12 + t:13 + t], None,
              ALU.mult, after=[V])
            V(nc.vector.tensor_scalar, low[:, t, Q_RANK:Q_RANK + KV_RANK], low[:, t, Q_RANK:Q_RANK + KV_RANK],
              stats[:, 14 + t:15 + t], None, ALU.mult, after=[V])
        k.transposes(low, lowT, 3, after=[V], scale=cols[:, 17:20])
        low_ready = [V.mark(), A.mark()]

        slot, loaded = k.load_slot([(0, (2, 768), at(w_uq)[:, 0]), (1536, (1024,), at(w_ukv)[:, 0])])
        uq = split(slot.ap[:, 0:1536], 2, 768)
        ukv = slot.ap[:, 1536:2560]
        for m0, b, _, mark in k.feature_major(lambda kk, m: uq[:, kk, m * P:(m + 1) * P], [loaded, *low_ready], lowT, 4, kt=2):
            b.free = [k.copy(V, qnT[:, m0:m0 + 2, :], split(b.ap, 2, S), after=[mark])]
        for m0, b, _, mark in k.feature_major(lambda kk, m: ukv[:, m * P:(m + 1) * P], (), lowT[:, 2:3, :], 4, kt=1):
            b.free = [k.copy(A, knT[:, m0:m0 + 2, :], split(b.ap, 2, S), after=[mark])]
        for t, b, mark in k.token_major(lambda kk: ukv[:, WB:], (), lowT[:, 2:3, :], WB, kt=1):
            b.free = [k.copy(A, mla_v[:, t, :], b.ap, after=[mark])]
        for t, b, mark in k.token_major(lambda kk: uq[:, kk, WB:], (), lowT, S, kt=2):
            b.free = [k.copy(V, qr[:, t, :], b.ap[:, 0:S], after=[mark])]
        slot.free = [T.mark()]

        half = ROPE // 2

        def rotate(src, dst, heads):
            tmp = split(junk[:, 2, 0:TT * heads * half], TT, heads, half)
            c = cos.unsqueeze(2).to_broadcast([P, TT, heads, half])
            s = sin.unsqueeze(2).to_broadcast([P, TT, heads, half])
            x1, x2 = src[:, :, :, 0:half], src[:, :, :, half:]
            for t in range(TT):
                for a, bb, op, o in ((x1, x2, ALU.subtract, dst[:, :, :, 0:half]), (x2, x1, ALU.add, dst[:, :, :, half:])):
                    V(nc.vector.tensor_tensor, tmp[:, t], bb[:, t], s[:, t], ALU.mult, after=[V])
                    V(nc.vector.tensor_tensor, o[:, t], a[:, t], c[:, t], ALU.mult, after=[V])
                    V(nc.vector.tensor_tensor, o[:, t], o[:, t], tmp[:, t], op, after=[V])

        rot = split(junk[:, 0, :], TT, MLA_HEADS, ROPE)
        rotate(qr.rearrange("p t (h j) -> p t h j", h=MLA_HEADS), rot, MLA_HEADS)
        pe = low[:, :, Q_RANK + KV_RANK:].unsqueeze(2).to_broadcast([P, TT, 4, ROPE])
        rotate(pe, kr.rearrange("p t (h j) -> p t h j", h=4), 4)
        k.transposes(rot.rearrange("p t h j -> p t (h j)"), qrT, 2, after=[V])
        k.transposes(kr, krT.unsqueeze(1), 1, after=[V])
        attention_ready = [V.mark(), A.mark(), T.mark()]

        V(nc.vector.tensor_tensor, junk[:, 1, 0:128].rearrange("p (a b) -> p a b", a=2), lam[:, 0::2, :],
          lam[:, 1::2, :], ALU.mult, after=[k.small_loaded, V])
        V(nc.vector.tensor_reduce, stats[:, 16:18], split(junk[:, 1, 0:128], 2, 64), AX.X, ALU.add, after=[V])
        A(nc.scalar.activation, stats[:, 18:20], stats[:, 16:18], ACT.Exp, after=[V])
        V(nc.vector.tensor_tensor, stats[:, 20:21], stats[:, 18:19], stats[:, 19:20], ALU.subtract, after=[A])
        init = split(table("lam"), DEPTH, 2)[:, bass.ds(l, 1), :]
        V(nc.vector.tensor_tensor, stats[:, 21:22], stats[:, 20:21], init[:, 0, 0:1], ALU.add, after=[V])
        V(nc.vector.tensor_scalar, stats[:, 22:23], stats[:, 21:22], -1.0, None, ALU.mult, after=[V])
        V(nc.vector.tensor_tensor, stats[:, 23:24], cols[:, 16:17], init[:, 0, 1:2], ALU.mult, after=[V])
        minus_lam, subln = stats[:, 22:23], stats[:, 23:24]

        def score_map(n, pairs, add, scale):
            b, s = k.bank(), scores[n % 4]
            for at_, keys, q0 in ((0, S, P), (S, P, 0)):
                for j, (kT, qT) in enumerate(pairs):
                    last = k.matmul(b.ap[:, at_:at_ + keys], qT[:, q0:q0 + P], kT[:, 0:keys],
                                    start=j == 0, stop=j == len(pairs) - 1, after=[*b.free, *attention_ready] if at_ + j == 0 else ())
            m = V(nc.vector.scalar_tensor_tensor, s.ap, b.ap[:, 0:SCORE_W], scale, add, ALU.mult, ALU.add,
                  after=[last, *s.free])
            b.free = [m]
            st = stats[:, 24 + 6 * (n % 4):30 + 6 * (n % 4)]
            V(nc.vector.tensor_reduce, st[:, 0:1], s.ap[:, 0:S], AX.X, ALU.max, negate=True, after=[m])
            m = V(nc.vector.tensor_reduce, st[:, 1:2], s.ap[:, S:], AX.X, ALU.max, negate=True, after=[m])
            A(nc.scalar.activation, s.ap[:, 0:S], s.ap[:, 0:S], ACT.Exp, bias=st[:, 0:1], accum_out=st[:, 2:3], after=[m])
            m = A(nc.scalar.activation, s.ap[:, S:], s.ap[:, S:], ACT.Exp, bias=st[:, 1:2], accum_out=st[:, 3:4])
            V(nc.vector.reciprocal, st[:, 4:6], st[:, 2:4], after=[m])
            return s, st, V.mark()

        def weighted(n, s, ready, v, width, out, sums, sums_ready):
            b, pt = k.bank(), probsT[n % 2]
            for j in range(3):
                k.transpose(b.ap[:, j * P:(j + 1) * P], s.ap[:, j * P:(j + 1) * P],
                            after=[*b.free, *ready] if j == 0 else ())
            s.free = [T.mark()]
            m = k.copy(A, pt.ap, b.ap[:, 0:SCORE_W], after=[T, *pt.free])
            b.free = [m]
            b = k.bank()
            k.matmul(b.ap[:, 0:width], pt.ap[:, 0:P], v[:, 0, :], start=True, stop=False, after=[m, *b.free])
            k.matmul(b.ap[:, 0:width], pt.ap[:, P:S], v[:, 1, :], start=False, stop=True)
            k.matmul(b.ap[:, width:2 * width], pt.ap[:, S:], v[:, 0, :], start=True, stop=True)
            pt.free = [T.mark()]
            for t, at_, r in ((1, 0, 0), (0, width, 1)):
                src = b.ap[:, at_:at_ + width]
                if sums is None:
                    V(nc.vector.tensor_copy, out[:, t, :], src, after=[T])
                else:
                    V(nc.vector.tensor_scalar, out[:, t, :], src, sums[:, r:r + 1], None, ALU.mult, after=[T, sums_ready])
            b.free = [V.mark()]

        def differential(h):
            out = []
            for j in range(2):
                rows = slice(64 * j, 64 * j + 64)
                out.append(score_map(2 * h + j, [(qkT[rows, 1, h, :], qkT[rows, 0, h, :])], bias[:, h, :], 64 ** -0.5))
            (s1, st1, _), (s2, st2, _) = out
            V(nc.vector.tensor_scalar, st2[:, 4:6], st2[:, 4:6], minus_lam, None, ALU.mult, after=[V])
            for at_, keys, r in ((0, S, 4), (S, P, 5)):
                cut = slice(at_, at_ + keys)
                V(nc.vector.tensor_scalar, s1.ap[:, cut], s1.ap[:, cut], st1[:, r:r + 1], None, ALU.mult, after=[V])
                V(nc.vector.scalar_tensor_tensor, s1.ap[:, cut], s2.ap[:, cut], st2[:, r:r + 1], s1.ap[:, cut],
                  ALU.mult, ALU.add, after=[V])
            s2.free = [V.mark()]
            return s1, None, V.mark(), diff_v[:, :, h * P:(h + 1) * P], P

        def moba(h):
            s, st, m = score_map(8 + h, [(qkT[:, 3, h, :], qkT[:, 2, h, :])], bias[:, DIFF_HEADS + h, :], P ** -0.5)
            return s, st[:, 4:6], m, moba_v[:, :, h * P:(h + 1) * P], P

        def latent(h):
            rows = slice(64 * (h % 2), 64 * (h % 2) + 64)
            rot_rows = slice(32 * (h % 4), 32 * (h % 4) + 32)
            s, st, m = score_map(12 + h, [(knT[rows, h // 2, :], qnT[rows, h // 2, :]),
                                          (krT[rot_rows, :], qrT[rot_rows, h // 4, :])],
                                 table("causal"), (NOPE + ROPE) ** -0.5)
            return s, st[:, 4:6], m, mla_v[:, :, h * VDIM:(h + 1) * VDIM], VDIM

        jobs = [(0, differential, h) for h in range(DIFF_HEADS)]
        jobs += [(1, moba, h) for h in range(MOBA_HEADS)] + [(2, latent, h) for h in range(MLA_HEADS)]
        waiting = []
        turned = [None]

        def finish_branch(g):
            if g == 0:
                sq = junk.rearrange("p a b -> p (a b)")[:, 0:1024]
                ho = heads_out.rearrange("p t c -> p (t c)")
                V(nc.vector.tensor_tensor, sq, ho, ho, ALU.mult, after=[V])
                V(nc.vector.tensor_reduce, stats[:, 48:56], split(sq, 8, P), AX.X, ALU.add, after=[V])
                k.rstd(stats[:, 56:64], stats[:, 48:56], P, EPS_RMS, after=[V])
                V(nc.vector.tensor_tensor, split(ho, 8, P), split(ho, 8, P),
                  stats[:, 56:64].unsqueeze(2).to_broadcast([P, 8, P]), ALU.mult, after=[V])
            k.transposes(heads_out, branchT[:, g], 4, after=[V],
                         scale=subln.to_broadcast([P, 4]) if g == 0 else None)
            turned[0] = T.mark()

        def finish_head():
            n, g, h, s, sums, ready, v, width = waiting.pop(0)
            if h == 0 and turned[0] is not None:
                V.wait([turned[0]])
            weighted(n, s, [ready, A], v, width, heads_out[:, :, h * width:(h + 1) * width], sums, ready)
            if h == (DIFF_HEADS, MOBA_HEADS, MLA_HEADS)[g] - 1:
                finish_branch(g)

        for n, (g, job, h) in enumerate(jobs):
            s, sums, ready, v, width = job(h)
            waiting.append((n, g, h, s, sums, ready, v, width))
            if len(waiting) > 1:
                finish_head()
        finish_head()
        branches_ready = [V.mark(), A.mark()]

        V(nc.vector.memset, mixT.rearrange("p a b -> p (a b)"), 0.0)
        gates = [k.c.buf(gateT[:, j]) for j in range(2)]

        def branch(i):
            half = []
            for j in range(2):
                slot, loaded = k.load_slot([(0, (KT, WB), at(w_in)[:, 0, :, bass.ds(i * D + (GATE_IN + j * WB), WB)])], slot=j)
                half.append((slot, loaded))
            slot_b, loaded_b = k.load_slot([(0, (4, D), w_branch[:, bass.ds(l, 1), bass.ds(i, 1)][:, 0, 0])], slot=2)
            for j in range(2):
                slot, loaded = half[j]
                w = split(slot.ap, KT, WB)
                for m0, b, _, mark in k.feature_major(lambda kk, m: w[:, kk, m * P:(m + 1) * P], [loaded, *branches_ready], hT, 4):
                    A(nc.scalar.activation, gates[j].ap[:, m0:m0 + 2, :], split(b.ap, 2, S), ACT.Sigmoid,
                      after=[mark, *gates[j].free])
                    b.free = [A.mark()]
                slot.free = [T.mark()]
            wb = split(slot_b.ap, 4, D)
            rhs = branchT[:, bass.ds(i, 1)][:, 0]
            for j in range(2):
                for m0, b, _, mark in k.feature_major(lambda kk, m: wb[:, kk, j * WB + m * P:j * WB + (m + 1) * P],
                                                      [loaded_b], rhs, 4, kt=4):
                    g = gates[j].ap[:, m0:m0 + 2, :]
                    V(nc.vector.tensor_tensor, g, split(b.ap, 2, S), g, ALU.mult, after=[mark, A])
                    b.free = [V.mark()]
                    mix = mixT[:, 4 * j + m0:4 * j + m0 + 2, :]
                    V(nc.vector.tensor_tensor, mix, mix, g, ALU.add, after=[V])
                gates[j].free = [V.mark()]
            slot_b.free = [T.mark()]

        k.c.loop(N_BRANCH, branch)

        def out_banks(load, xT, ready):
            banks = [[None, None], [None, None]]
            for half in range(2):
                slot, loaded = load(half)
                w = split(slot.ap, KT, WB)
                for t, b, mark in k.token_major(lambda kk: w[:, kk, :], [loaded, *ready], xT, WB):
                    banks[t][half] = (b, mark)
                slot.free = [T.mark()]
            return banks

        mix_ready = [V.mark()]
        banks = out_banks(lambda hf: k.load_slot([(0, (KT, WB), at(w_out)[:, 0, :, hf * WB:(hf + 1) * WB])], slot=3 if hf == 0 else 0),
                          mixT, mix_ready)
        k.add_normed(x, banks, post, post_in, junk, stats)
        post_free = V.mark()
        mlp_post_in = SP.dma(k.rows_loaded, post, dram["norm_mlp_post"][bass.ds(l, 1), :].partition_broadcast(P)[:, 0, :],
                             after=[post_free])

        normed_T(k, x, hT, cols[:, 8:16], junk, stats, after=[G])
        h_ready = [V.mark(), A.mark()]
        acc = [k.bank() for _ in range(4)]
        zeros = mixT.rearrange("p a b -> p (a b)")
        V(nc.vector.memset, zeros[:, 0:P + WB], 0.0, after=[T])
        for b in acc:
            k.matmul(b.ap, zeros[:, 0:P], zeros[:, P:P + WB], start=True, stop=False, inc=True, after=[V, *b.free])
        hidden = [k.c.buf(upT[:, j]) for j in range(2)]
        spare = [k.banks[(k.c.bank + j) % 8] for j in range(4)]

        def mlp(i):
            loads = []
            for j in range(2):
                f = i * (2 * WB) + j * WB
                up = k.load_slot([(0, (KT, WB), at(w_up)[:, 0, :, bass.ds(f, WB)])], slot=2 * j)
                down = k.load_slot([(0, (4, D), at(w_down)[:, 0, bass.ds(i * 8 + j * 4, 4), :])], slot=2 * j + 1)
                loads.append((up, down))
            for j in range(2):
                (slot, loaded), (slot_d, loaded_d) = loads[j]
                w, wd, u = split(slot.ap, KT, WB), split(slot_d.ap, 4, D), hidden[j]
                for m0 in (0, 2):
                    b = spare[2 * j + m0 // 2]
                    for m in range(2):
                        for kk in range(KT):
                            k.matmul(b.ap[:, m * S:(m + 1) * S], w[:, kk, (m0 + m) * P:(m0 + m + 1) * P], hT[:, kk, :],
                                     start=kk == 0, stop=kk == KT - 1, after=[*b.free, loaded, *h_ready] if kk == 0 else ())
                    A(nc.scalar.activation, u.ap[:, m0:m0 + 2, :], split(b.ap, 2, S), ACT.Relu, after=[T, *u.free])
                    b.free = [A.mark()]
                    V(nc.vector.tensor_tensor, u.ap[:, m0:m0 + 2, :], u.ap[:, m0:m0 + 2, :], u.ap[:, m0:m0 + 2, :],
                      ALU.mult, after=[A])
                slot.free = [T.mark()]
                for t in range(TT):
                    for half in range(2):
                        for kk in range(4):
                            T(nc.tensor.matmul, acc[2 * t + half].ap, u.ap[:, kk, t * P:(t + 1) * P],
                              wd[:, kk, half * WB:(half + 1) * WB], start=False, stop=False, skip_group_check=True,
                              inc=kk == 3, after=[loaded_d, V] if t + half + kk == 0 else ())
                slot_d.free = [T.mark()]
                u.free = [T.mark()]

        k.c.loop(D_FF // (2 * WB), mlp)
        for b in acc:
            k.matmul(b.ap, zeros[:, 0:P], zeros[:, P:P + WB], start=False, stop=True)
        done = T.mark()
        k.add_normed(x, [[(acc[0], done), (acc[1], done)], [(acc[2], done), (acc[3], done)]], post, mlp_post_in, junk, stats)

    with nc.Fori(0, DEPTH) as l:
        layer(l)
    k.top = floor


def normed_T(k, src, dstT, weight, junk, stats, after):
    nc, V, A = k.nc, k.V, k.A
    normed = split(junk.rearrange("p a b -> p (a b)"), TT, D)
    for t in range(TT):
        A(nc.scalar.activation, normed[:, t, :], src[:, t, :], ACT.Square, accum_out=stats[:, t:t + 1],
          after=[*after, V, k.G])
    k.rstd(stats[:, 2:4], stats[:, 0:2], D, EPS_RMS, after=[A])
    for t in range(TT):
        V(nc.vector.tensor_scalar, normed[:, t, :], src[:, t, :], stats[:, 2 + t:3 + t], None, ALU.mult, after=[V])
    k.transposes(normed, dstT, KT, after=[V, *after], scale=weight)


def close_layer(k, i, x, mixed, hT, free_at):
    nc, T, V, A, G, SP, dram = k.nc, k.T, k.V, k.A, k.G, k.SP, k.dram
    floor, k.top = k.top, free_at
    rows = k.take(3, D)
    pT = k.take(TT, S)
    e = k.take(TT, D)
    gate = k.take(TT, D)
    junk = k.take(WB)
    stats = k.take(32)
    k.top = floor
    ready = [V.mark(), G.mark(), A.mark(), T.mark()]
    for j, name in enumerate(("ln_g", "ln_b", "ple_norm")):
        SP.dma(k.rows_loaded, rows[:, j, :], dram[name][i:i + 1, :].partition_broadcast(P)[:, 0, :], after=ready)
    SP.dma(k.rows_loaded, pT, dram["pT"][i].rearrange("(a p) s -> p a s", p=P))

    slot, loaded = k.load_slot([(0, (2, D), dram["ple_w"][i].rearrange("(a p) n -> p a n", p=P))])
    w = split(slot.ap[:, 0:2 * D], 2, D)
    for hf in range(2):
        cut = slice(hf * WB, (hf + 1) * WB)
        for t, b, mark in k.token_major(lambda kk: w[:, kk, cut], [loaded, k.rows_loaded], pT, WB, kt=2):
            A(nc.scalar.activation, junk, b.ap, ACT.Square, accum_out=stats[:, 2 * t + hf:2 * t + hf + 1], after=[mark, A])
            A(nc.scalar.activation, e[:, t, cut], b.ap, ACT.Copy)
            b.free = [A.mark()]
    slot.free = [T.mark()]
    sums = split(stats[:, 0:4], 2, 2)
    V(nc.vector.tensor_tensor, stats[:, 4:6], sums[:, :, 0], sums[:, :, 1], ALU.add, after=[A])
    k.rstd(stats[:, 6:8], stats[:, 4:6], D, EPS_RMS, after=[V])
    for t in range(TT):
        V(nc.vector.scalar_tensor_tensor, e[:, t, :], e[:, t, :], stats[:, 6 + t:7 + t], rows[:, 2, :],
          ALU.mult, ALU.mult, after=[V, k.rows_loaded])

    k.transposes(mixed, hT, KT, after=ready)
    mix_ready = [V.mark(), A.mark()]
    w_out = dram["w_out_2"].rearrange("l (k p) n -> p l k n", p=P)
    for hf in range(2):
        cut = slice(hf * WB, (hf + 1) * WB)
        slot, loaded = k.load_slot([(0, (KT, WB), w_out[:, i, :, cut])])
        w = split(slot.ap, KT, WB)
        for t, b, mark in k.token_major(lambda kk: w[:, kk, :], [loaded, *mix_ready], hT, WB):
            V(nc.vector.scalar_tensor_tensor, x[:, t, cut], x[:, t, cut], ALPHA, b.ap, ALU.mult, ALU.add,
              accum_out=stats[:, 8 + 2 * t + hf:9 + 2 * t + hf], after=[mark, V])
            b.free = [V.mark()]
        slot.free = [T.mark()]
    sums = split(stats[:, 8:12], 2, 2)
    V(nc.vector.tensor_tensor, stats[:, 12:14], sums[:, :, 0], sums[:, :, 1], ALU.add, after=[V])
    V(nc.vector.tensor_scalar, stats[:, 14:16], stats[:, 12:14], -1.0 / D, None, ALU.mult, after=[V])
    for t in range(TT):
        A(nc.scalar.activation, gate[:, t, :], x[:, t, :], ACT.Square, bias=stats[:, 14 + t:15 + t],
          accum_out=stats[:, 16 + t:17 + t], after=[V])
    k.rstd(stats[:, 18:20], stats[:, 16:18], D, EPS_LN, after=[A])
    for t in range(TT):
        xt = x[:, t, :]
        V(nc.vector.tensor_scalar, xt, xt, stats[:, 14 + t:15 + t], stats[:, 18 + t:19 + t], ALU.add, ALU.mult, after=[V])
        V(nc.vector.tensor_tensor, xt, xt, rows[:, 0, :], ALU.mult, after=[V])
        V(nc.vector.tensor_tensor, xt, xt, rows[:, 1, :], ALU.add, after=[V])

    k.transposes(x, hT, KT, after=[V])
    x_ready = [V.mark(), A.mark()]
    ple_gate = dram["ple_gate"].rearrange("l (k p) n -> p l k n", p=P)
    for hf in range(2):
        cut = slice(hf * WB, (hf + 1) * WB)
        slot, loaded = k.load_slot([(0, (KT, WB), ple_gate[:, i, :, cut])])
        w = split(slot.ap, KT, WB)
        for t, b, mark in k.token_major(lambda kk: w[:, kk, :], [loaded, *x_ready], hT, WB):
            m = A(nc.scalar.activation, gate[:, t, cut], b.ap, ACT.Sigmoid, after=[mark])
            b.free = [m]
            m = V(nc.vector.tensor_tensor, gate[:, t, cut], gate[:, t, cut], e[:, t, cut], ALU.mult, after=[m, V])
            V(nc.vector.tensor_tensor, x[:, t, cut], x[:, t, cut], gate[:, t, cut], ALU.add, after=[m])
        slot.free = [T.mark()]


def padded_copy(k, dst, bank, tiles, pad, after):
    return k.copy(k.A, dst[:, 0:tiles, pad:pad + S], split(bank.ap, 2, S)[:, 0:tiles, :], after=after)


class Triangles:

    def __init__(self, k):
        self.k, self.n = k, 8
        self.X, self.XT = k.take(8, P), k.take(8, P)
        self.NX = k.take(8, P)
        self.masked = k.take(8, P)

    def invert(self, NT, d, ready):
        k = self.k
        nc, T, V, A, G = k.nc, k.T, k.V, k.A, k.G
        X, XT, NX, masked = self.X, self.XT, self.NX, self.masked
        at, _ = k.table_at[f"level{d}_0"]
        levels = split(k.tables[:, at:at + LEVELS * P], LEVELS, P)
        self.NT, self.levels = NT, levels
        ident8 = k.table("ident").unsqueeze(1).to_broadcast([P, 8, P])
        V(nc.vector.tensor_tensor, masked, NT, levels[:, 0:1].to_broadcast([P, 8, P]), ALU.mult, after=[*ready, T])
        V(nc.vector.tensor_tensor, XT, ident8, masked, ALU.subtract, after=[V])
        for g in range(2):
            b = k.bank()
            for j in range(4):
                k.transpose(b.ap[:, j * P:(j + 1) * P], masked[:, 4 * g + j, :], after=[*b.free, V] if j == 0 else ())
            V(nc.vector.tensor_tensor, X[:, 4 * g:4 * g + 4], ident8[:, 0:4], split(b.ap, 4, P), ALU.subtract, after=[T])
            b.free = [V.mark()]
        mask_buf = k.c.buf()
        mask_buf.free = [T.mark(), V.mark()]
        banks = [k.bank() for _ in range(6)]

        def level(i):
            G(nc.gpsimd.tensor_tensor, masked, NT, levels[:, bass.ds(i + 1, 1)].to_broadcast([P, 8, P]), ALU.mult,
              after=mask_buf.free)
            x_ready = V.mark()
            for g in range(2):
                b = banks[g]
                for j in range(4):
                    k.matmul(b.ap[:, j * P:(j + 1) * P], masked[:, 4 * g + j, :], X[:, 4 * g + j, :], True, True,
                             after=[*b.free, G, x_ready] if j == 0 else (), inc=j == 3)
                k.copy(A, NX[:, 4 * g:4 * g + 4], split(b.ap, 4, P), after=[T])
                b.free = [A.mark()]
            mask_buf.free = [T.mark()]
            for g in range(2):
                bx, bt = banks[2 + g], banks[4 + g]
                for j in range(4):
                    u = 4 * g + j
                    k.matmul(bx.ap[:, j * P:(j + 1) * P], XT[:, u, :], NX[:, u, :], True, True,
                             after=[*bx.free, A] if j == 0 else (), inc=j == 3)
                for j in range(4):
                    u = 4 * g + j
                    k.matmul(bt.ap[:, j * P:(j + 1) * P], NX[:, u, :], XT[:, u, :], True, True,
                             after=bt.free if j == 0 else (), inc=j == 3)
                for dst, b in ((X, bx), (XT, bt)):
                    part = dst[:, 4 * g:4 * g + 4]
                    V(nc.vector.tensor_tensor, part, part, split(b.ap, 4, P), ALU.subtract, after=[T])
                    b.free = [V.mark()]

        k.c.loop(LEVELS - 2, level)
        V(nc.vector.tensor_tensor, masked, NT, levels[:, LEVELS - 1:].to_broadcast([P, 8, P]), ALU.mult, after=[T])
        self.ready = [V.mark()]

    def solve(self, which, rhs, U, work, width, ready):
        k = self.k
        nc, T, V, A = k.nc, k.T, k.V, k.A
        n = len(which)

        def products(mats, right, after):
            b = k.bank()
            for j, u in enumerate(which):
                k.matmul(b.ap[:, j * width:(j + 1) * width], mats[:, u, :], right[:, j, :], True, True,
                         after=[*b.free, *after] if j == 0 else (), inc=j == n - 1)
            return b, split(b.ap[:, 0:n * width], n, width)

        b, out = products(self.XT, rhs, [*ready, *self.ready])
        b.free = [k.copy(A, U, out, after=[T])]
        b, out = products(self.masked, U, [A])
        b.free = [k.copy(A, work, out, after=[T])]
        b, out = products(self.XT, work, [A])
        V(nc.vector.tensor_tensor, U, U, out, ALU.subtract, after=[T, A])
        b.free = [V.mark()]


def even_layer(k, x):
    nc, T, V, A, G, SP = k.nc, k.T, k.V, k.A, k.G, k.SP
    dram, table, take = k.dram, k.table, k.take
    k.begin()
    floor = k.top
    w_in = dram["even_w_in"].rearrange("(k p) n -> p k n", p=P)
    mixed = take(TT, D)
    m_at = k.top
    hT = take(KT, S)
    free_at = k.top
    raw = [k.c.buf(take(2, S + 4)) for _ in range(2)]
    take(m_at + RK_HEADS * 4 * P - k.top)
    cols = take(112)
    small = take(16 + 128 + 2 * WB)
    stats = take(160)
    v_tok = take(TT, WB)
    lora = take(2, WB)
    tri = Triangles(k)
    U, work, rhs = take(WB), take(WB), take(WB)
    state = take(WB)
    body_at = k.top
    cw = split(cols[:, 0:60], DN_CONV, 12)
    mu = split(cols[:, 60:88], 2, 14)
    w0, a0 = split(cols[:, 88:96], 2, 4), cols[:, 96:100]
    k_k, k_a, r_k = cols[:, 100:104], cols[:, 104:108], cols[:, 108:112]

    k.load_tables("even")
    SP.dma(k.small_loaded, cols, dram["even_cols"])
    at = 0
    for name, n in (("dn_a_log", 8), ("dn_dt_bias", 8), ("dn_norm", P), ("rk_ln_w", WB), ("rk_ln_b", WB)):
        SP.dma(k.small_loaded, small[:, at:at + n], dram[name].partition_broadcast(P)[:, 0, :])
        at += n
    SP.dma(k.small_loaded, lora[:, 0, :], dram["rk_w2"])
    SP.dma(k.small_loaded, lora[0:LORA, 1, :], dram["rk_a2"])
    a_log, dt_bias, dn_norm = small[:, 0:8], small[:, 8:16], small[:, 16:16 + P]
    ln_w, ln_b = small[:, 144:144 + WB], small[:, 144 + WB:144 + 2 * WB]
    for r in raw:
        V(nc.vector.memset, r.ap.rearrange("p a b -> p (a b)"), 0.0)
    k.transposes(x, hT, KT, after=[])
    h_ready = [V.mark(), A.mark()]

    qkvT = take(3, DN_HEADS, S)
    k_tok = take(TT, WB)
    abw = take(KT, DN_AB)
    g_beta = take(2, TT, 8)
    AT = take(8, P)
    NT = take(8, P)
    decay = take(8, P)
    silu_dn = take(TT, WB)
    dn_cols = take(64)
    o_dn = mixed[:, :, 0:WB]

    def gate_piece(column, dst):
        slot, loaded = k.load_slot([(0, (KT, WB), w_in[:, :, column:column + WB])])
        w = split(slot.ap, KT, WB)
        for t, b, mark in k.token_major(lambda kk: w[:, kk, :], [loaded, *h_ready], hT, WB):
            A(nc.scalar.activation, dst[:, t, :], b.ap, ACT.Silu, after=[mark])
            b.free = [A.mark()]
        slot.free = [T.mark()]

    SP.dma(k.small_loaded, abw, w_in[:, :, AB_IN:AB_IN + DN_AB])
    small_ready = k.small_loaded.mark()
    for part in range(3):
        slot, loaded = k.load_slot([(0, (KT, WB), w_in[:, :, part * WB:(part + 1) * WB])])
        w = split(slot.ap, KT, WB)
        for m0, b, tiles, mark in k.feature_major(lambda kk, m: w[:, kk, m * P:(m + 1) * P], [loaded, *h_ready], hT, 4):
            r = raw[m0 // 2]
            padded_copy(k, r.ap, b, 2, 2, after=[mark, V, *r.free])
            b.free = [A.mark()]
            for j in range(2):
                f = 4 * part + m0 + j
                y = qkvT[:, part, m0 + j, :]
                m = V(nc.vector.tensor_scalar, y, r.ap[:, j, 0:S], cw[:, 0, f:f + 1], None, ALU.mult, after=[A, small_ready])
                for tap in range(1, DN_CONV):
                    m = V(nc.vector.scalar_tensor_tensor, y, r.ap[:, j, tap:tap + S], cw[:, tap, f:f + 1], y,
                          ALU.mult, ALU.add, after=[m])
            r.free = [m]
            A(nc.scalar.activation, qkvT[:, part, m0:m0 + 2, :], qkvT[:, part, m0:m0 + 2, :], ACT.Silu, after=[m])
        slot.free = [T.mark()]
    gate_piece(DN_GATE_IN, silu_dn)

    ea = dn_cols[:, 0:8]
    A(nc.scalar.activation, ea, a_log, ACT.Exp, after=[small_ready])
    V(nc.vector.tensor_scalar, ea, ea, -1.0, None, ALU.mult, after=[A])
    for t, b, mark in k.token_major(lambda kk: abw[:, kk, :], [small_ready, *h_ready], hT, DN_AB):
        z, ex, ser, big = (dn_cols[:, 8 * j:8 * j + 8] for j in (1, 2, 3, 4))
        A(nc.scalar.activation, g_beta[:, 1, t, :], b.ap[:, 8:16], ACT.Sigmoid, after=[mark])
        V(nc.vector.tensor_tensor, z, b.ap[:, 0:8], dt_bias, ALU.add, after=[A, V])
        b.free = [V.mark()]
        V(nc.vector.scalar_tensor_tensor, ex, z, -1.0, z, ALU.mult, ALU.min, after=[V])
        A(nc.scalar.activation, ex, ex, ACT.Exp, after=[V])
        A(nc.scalar.activation, big, ex, ACT.Ln, bias=1.0, after=[A])
        V(nc.vector.tensor_scalar, ser, ex, -0.25, 1.0 / 3.0, ALU.mult, ALU.add, after=[A])
        V(nc.vector.tensor_tensor, ser, ser, ex, ALU.mult, after=[V])
        V(nc.vector.tensor_scalar, ser, ser, -0.5, None, ALU.add, after=[V])
        V(nc.vector.tensor_tensor, ser, ser, ex, ALU.mult, after=[V])
        V(nc.vector.tensor_scalar, ser, ser, 1.0, None, ALU.add, after=[V])
        V(nc.vector.tensor_tensor, ser, ser, ex, ALU.mult, after=[V])
        V(nc.vector.tensor_scalar, ex, ex, 0.02, None, ALU.is_lt, after=[V])
        V(nc.vector.tensor_tensor, ser, ser, big, ALU.subtract, after=[V])
        V(nc.vector.tensor_tensor, ser, ser, ex, ALU.mult, after=[V])
        V(nc.vector.tensor_tensor, big, big, ser, ALU.add, after=[V])
        V(nc.vector.scalar_tensor_tensor, big, z, 0.0, big, ALU.max, ALU.add, after=[V])
        V(nc.vector.tensor_tensor, g_beta[:, 0, t, :], big, ea, ALU.mult, after=[V])

    def l2_normalise(y, squares, ones, scale, after):
        n = y.shape[1]
        V(nc.vector.tensor_tensor, squares, y, y, ALU.mult, after=after)
        for j in range(0, n, 2):
            b = k.bank()
            k.matmul(b.ap, ones, squares[:, j:j + 2, :], True, True, after=[*b.free, V])
            V(nc.vector.tensor_scalar, squares[:, j:j + 2, :], split(b.ap, 2, S), 1.0, EPS_RMS, ALU.mult, ALU.add, after=[T])
            b.free = [V.mark()]
        A(nc.scalar.activation, squares, squares, ACT.Sqrt, after=[V])
        V(nc.vector.reciprocal, squares, squares, after=[A])
        V(nc.vector.scalar_tensor_tensor, y, squares, scale, y, ALU.mult, ALU.mult, after=[V])

    squares = decay.rearrange("p a b -> p (a b)")
    l2_normalise(qkvT[:, 0], split(squares, 4, S), table("ones"), P ** -0.5, after=[A, V])
    l2_normalise(qkvT[:, 1], split(squares, 4, S), table("ones"), 1.0, after=[A, V])

    def tokens_first(src, dst, tiles, after):
        for t in range(TT):
            b = k.bank()
            for j in range(tiles):
                k.transpose(b.ap[:, j * P:(j + 1) * P], src[:, j, t * P:(t + 1) * P],
                            after=[*b.free, *after] if j == 0 else (), inc=j == tiles - 1)
            b.free = [k.copy((V, A)[t], dst[:, t, :], b.ap[:, 0:tiles * P], after=[T])]

    tokens_first(qkvT[:, 1], k_tok, 4, after=[V, A])
    tokens_first(qkvT[:, 2], v_tok, 4, after=[V, A])

    for d in range(2):
        incl, strict = table(f"incl{d}"), table(f"strict{d}")
        g = g_beta[:, 0, :, 4 * d:4 * d + 4]
        beta = g_beta[:, 1, :, 4 * d:4 * d + 4]
        Gc, tail, eG = (split(dn_cols[:, 8 * j:8 * j + 8], TT, 4) for j in (5, 6, 7))
        b = k.bank()
        k.matmul(b.ap[:, 0:8], incl, g, True, True, after=[*b.free, V, A])
        V(nc.vector.tensor_copy, Gc, split(b.ap[:, 0:8], TT, 4), after=[T])
        b.free = [V.mark()]
        b = k.bank()
        k.matmul(b.ap[:, 0:8], table("ones"), g, True, True, after=b.free)
        V(nc.vector.tensor_tensor, tail, split(b.ap[:, 0:8], TT, 4), Gc, ALU.subtract, after=[T, V])
        b.free = [V.mark()]
        A(nc.scalar.activation, tail, tail, ACT.Exp, after=[V])
        A(nc.scalar.activation, eG, Gc, ACT.Exp, after=[V])
        for c in range(TT):
            b = k.bank()
            for h in range(4):
                k.matmul(b.ap[:, h * P:(h + 1) * P], g[:, c, h:h + 1].to_broadcast([P, P]), incl, True, True,
                         after=b.free if h == 0 else (), inc=h == 3)
            for h in range(4):
                V(nc.vector.tensor_scalar, decay[:, 4 * c + h, :], b.ap[:, h * P:(h + 1) * P], Gc[:, c, h:h + 1], 0.0,
                  ALU.subtract, ALU.min, after=[T, V])
            b.free = [V.mark()]
        A(nc.scalar.activation, decay, decay, ACT.Exp, after=[V])
        V(nc.vector.tensor_tensor, decay, decay, incl.unsqueeze(1).to_broadcast([P, 8, P]), ALU.mult, after=[A])
        for c in range(TT):
            cut = slice(c * P, (c + 1) * P)
            us = slice(4 * c, 4 * c + 4)
            for right, dst in ((0, AT), (1, NT)):
                b = k.bank()
                for h in range(4):
                    k.matmul(b.ap[:, h * P:(h + 1) * P], qkvT[:, 1, h, cut], qkvT[:, right, h, cut], True, True,
                             after=[*b.free, V] if h == 0 else (), inc=h == 3)
                V(nc.vector.tensor_tensor, dst[:, us], split(b.ap, 4, P), decay[:, us], ALU.mult, after=[T, V])
                b.free = [V.mark()]
            b = k.bank()
            for h in range(4):
                k.matmul(b.ap[:, h * P:(h + 1) * P], beta[:, c, h:h + 1].to_broadcast([P, P]), table("ident"), True, True,
                         after=b.free if h == 0 else (), inc=h == 3)
            V(nc.vector.tensor_tensor, NT[:, us], NT[:, us], split(b.ap, 4, P), ALU.mult, after=[T, V])
            b.free = [V.mark()]
        V(nc.vector.tensor_tensor, NT, NT, strict.unsqueeze(1).to_broadcast([P, 8, P]), ALU.mult, after=[V])
        tri.invert(NT, d, [V.mark()])
        bc = lambda col: col.unsqueeze(2).to_broadcast([P, 4, P])
        rhs4, U4, work4 = (split(a, 4, P) for a in (rhs, U, work))
        for step in range(TT):
            c = step if d == 0 else TT - 1 - step
            cut = slice(c * P, (c + 1) * P)
            units = list(range(4 * c, 4 * c + 4))
            vs = split(v_tok[:, c, :], 4, P)
            if step == 0:
                V(nc.vector.tensor_tensor, rhs4, vs, bc(beta[:, c, :]), ALU.mult, after=[V, A])
            else:
                b = k.bank()
                for h in range(4):
                    k.matmul(b.ap[:, h * P:(h + 1) * P], qkvT[:, 1, h, cut], state[:, h * P:(h + 1) * P], True, True,
                             after=[*b.free, V, A] if h == 0 else (), inc=h == 3)
                V(nc.vector.tensor_tensor, rhs4, split(b.ap, 4, P), bc(eG[:, c, :]), ALU.mult, after=[T, V])
                b.free = [V.mark()]
                V(nc.vector.tensor_tensor, rhs4, vs, rhs4, ALU.subtract, after=[V])
                V(nc.vector.tensor_tensor, rhs4, rhs4, bc(beta[:, c, :]), ALU.mult, after=[V])
            tri.solve(units, rhs4, U4, work4, P, [V.mark()])
            b = k.bank()
            for h in range(4):
                k.matmul(b.ap[:, h * P:(h + 1) * P], AT[:, 4 * c + h, :], U4[:, h, :], True, True,
                         after=[*b.free, V] if h == 0 else (), inc=h == 3)
            o = o_dn[:, c, :]
            if d == 0:
                V(nc.vector.tensor_copy, o, b.ap, after=[T])
            else:
                V(nc.vector.tensor_tensor, o, o, b.ap, ALU.add, after=[T, V])
            b.free = [V.mark()]
            if step == 0:
                V(nc.vector.tensor_tensor, work4, U4, bc(tail[:, c, :]), ALU.mult, after=[V, A, T])
                b = k.bank()
                for h in range(4):
                    k.matmul(b.ap[:, h * P:(h + 1) * P], k_tok[:, c, h * P:(h + 1) * P], work4[:, h, :], True, True,
                             after=[*b.free, V] if h == 0 else (), inc=h == 3)
                b.free = [k.copy(A, state, b.ap, after=[T])]
            else:
                b = k.bank()
                for h in range(4):
                    k.matmul(b.ap[:, h * P:(h + 1) * P], qkvT[:, 0, h, cut], state[:, h * P:(h + 1) * P], True, True,
                             after=b.free if h == 0 else (), inc=h == 3)
                V(nc.vector.tensor_tensor, work4, split(b.ap, 4, P), bc(eG[:, c, :]), ALU.mult, after=[T, V])
                b.free = [V.mark()]
                V(nc.vector.tensor_tensor, o, o, work, ALU.add, after=[V])

    sq = squares[:, 0:WB]
    for t in range(TT):
        V(nc.vector.tensor_tensor, sq, o_dn[:, t, :], o_dn[:, t, :], ALU.mult, after=[V])
        V(nc.vector.tensor_reduce, stats[:, 4 * t:4 * t + 4], split(sq, 4, P), AX.X, ALU.add, after=[V])
    k.rstd(stats[:, 8:16], stats[:, 0:8], P, EPS_RMS, after=[V])
    for t in range(TT):
        o4 = split(o_dn[:, t, :], 4, P)
        V(nc.vector.tensor_tensor, o4, o4, stats[:, 8 + 4 * t:12 + 4 * t].unsqueeze(2).to_broadcast([P, 4, P]), ALU.mult, after=[V])
        V(nc.vector.tensor_tensor, o4, o4, dn_norm.unsqueeze(1).to_broadcast([P, 4, P]), ALU.mult, after=[V])
        V(nc.vector.tensor_tensor, o_dn[:, t, :], o_dn[:, t, :], silu_dn[:, t, :], ALU.mult, after=[V, A])

    k.top = body_at
    dn_done = [V.mark(), T.mark(), A.mark()]
    rkvT = take(3, 4, S)
    loraT = take(2, S)
    kkT, bT = take(4, S), take(4, S)
    arT = take(4, 2, S)
    dbT, dkT = take(4, S), take(4, S)
    cur = take(4, S)
    tmp = take(4, S)
    M = split(k.memory[:, m_at:m_at + RK_HEADS * 4 * P], RK_HEADS, 4, P)
    db_tok, dk_tok = take(WB), take(WB)
    bonus = take(TT, 8)
    scale_state = take(4)
    silu_rk = take(TT, WB)
    o_rk = mixed[:, :, WB:]
    mu_c = stats[:, 32:46]
    V(nc.vector.tensor_tensor, mu_c, mu[:, 0, :], mu[:, 1, :], ALU.add, after=[V])
    V(nc.vector.tensor_scalar, mu_c, mu_c, -1.0, 1.0, ALU.mult, ALU.add, after=[V])
    for part in range(4):
        tiles, width = (4, WB) if part < 3 else (2, 3 * LORA)
        slot, loaded = k.load_slot([(0, (KT, width), w_in[:, :, RK_IN + part * WB:RK_IN + part * WB + width])])
        w = split(slot.ap[:, 0:KT * width], KT, width)
        for m0 in range(0, tiles, 2):
            b = k.bank()
            for j in range(2):
                rows = P if part < 3 or j == 0 else LORA
                for kk in range(KT):
                    mark = k.matmul(b.ap[0:rows, j * S:(j + 1) * S], w[:, kk, (m0 + j) * P:(m0 + j) * P + rows],
                                    hT[:, kk, :], kk == 0, kk == KT - 1, after=[*b.free, loaded, *dn_done] if kk == 0 else ())
            r = raw[m0 // 2]
            for j in range(2):
                rows = P if part < 3 or j == 0 else LORA
                f = 4 * part + m0 + j
                y = (rkvT[:, part, m0 + j, :] if part < 3 else loraT[:, j, :])[0:rows, :]
                rr = r.ap[0:rows, j, :]
                A(nc.scalar.activation, rr[:, 2:2 + S], b.ap[0:rows, j * S:(j + 1) * S], ACT.Copy, after=[mark, *r.free])
                m = V(nc.vector.tensor_scalar, y, rr[:, 2:2 + S], mu_c[0:rows, f:f + 1], None, ALU.mult, after=[A, V])
                m = V(nc.vector.scalar_tensor_tensor, y, rr[:, 1:1 + S], mu[0:rows, 0, f:f + 1], y, ALU.mult, ALU.add, after=[m])
                m = V(nc.vector.scalar_tensor_tensor, y, rr[:, 3:3 + S], mu[0:rows, 1, f:f + 1], y, ALU.mult, ALU.add, after=[m])
            b.free = [A.mark()]
            r.free = [m]
        slot.free = [T.mark()]
    gate_piece(RK_GATE_IN, silu_rk)
    for m0 in range(0, 4, 2):
        b = k.bank()
        for j in range(2):
            k.matmul(b.ap[:, j * S:(j + 1) * S], lora[0:LORA, 1, (m0 + j) * P:(m0 + j + 1) * P], loraT[0:LORA, 1, :],
                     True, True, after=[*b.free, V] if j == 0 else ())
        for j in range(2):
            A(nc.scalar.activation, bT[:, m0 + j, :], b.ap[:, j * S:(j + 1) * S], ACT.Sigmoid, bias=a0[:, m0 + j:m0 + j + 1], after=[T])
        b.free = [A.mark()]
    for m in range(4):
        V(nc.vector.tensor_scalar, kkT[:, m, :], rkvT[:, 1, m, :], k_k[:, m:m + 1], None, ALU.mult, after=[V])
        V(nc.vector.tensor_scalar, tmp[:, m, :], bT[:, m, :], -1.0, k_a[:, m:m + 1], ALU.add, ALU.mult, after=[A, V])
    V(nc.vector.scalar_tensor_tensor, rkvT[:, 1], tmp, 1.0, rkvT[:, 1], ALU.add, ALU.mult, after=[V])
    l2_normalise(kkT, tmp, table("pairs"), 1.0, after=[V])
    V(nc.vector.tensor_tensor, bT, bT, kkT, ALU.mult, after=[V])
    for m in range(4):
        V(nc.vector.scalar_tensor_tensor, tmp[:, m, :], rkvT[:, 0, m, :], r_k[:, m:m + 1], rkvT[:, 1, m, :],
          ALU.mult, ALU.mult, after=[V])
    b = k.bank()
    for t in range(TT):
        for m in range(4):
            k.matmul(b.ap[:, 8 * t + 2 * m:8 * t + 2 * m + 2], tmp[:, m, t * P:(t + 1) * P], table("head_sel"), True, True,
                     after=[*b.free, V] if t + m == 0 else ())
    V(nc.vector.tensor_copy, bonus, split(b.ap[:, 0:16], TT, 8), after=[T])
    b.free = [V.mark()]
    tokens_first(rkvT[:, 2], v_tok, 4, after=[V, T])
    v_ready = [V.mark(), A.mark()]
    A(nc.scalar.activation, loraT[:, 0, :], loraT[:, 0, :], ACT.Tanh, after=[V])

    for d in range(2):
        rows = slice(64 * d, 64 * d + 64)
        logw = arT[:, :, 0, :]
        for m0 in range(0, 4, 2):
            b = k.bank()
            for j in range(2):
                k.matmul(b.ap[:, j * S:(j + 1) * S], lora[rows, 0, (m0 + j) * P:(m0 + j + 1) * P], loraT[rows, 0, :],
                         True, True, after=[*b.free, A, V] if j == 0 else ())
            for j in range(2):
                A(nc.scalar.activation, cur[:, m0 + j, :], b.ap[:, j * S:(j + 1) * S], ACT.Sigmoid,
                  bias=w0[:, d, m0 + j:m0 + j + 1], after=[T, V])
            b.free = [A.mark()]
        flat = lambda a: a.rearrange("p a b -> p (a b)")
        V(nc.vector.tensor_scalar, flat(cur), flat(cur), -math.exp(-0.5), None, ALU.mult, after=[A])
        V(nc.vector.tensor_tensor_scan, flat(tmp), table("fresh"), flat(cur), 0.0, ALU.mult, ALU.add, after=[V, T])
        V(nc.vector.tensor_tensor, flat(cur), flat(tmp), flat(cur), ALU.subtract, after=[V])
        chunked = lambda a: split(flat(a), 8, P)
        upto, before = chunked(tmp), chunked(cur)
        mid = (upto[:, :, 63:64], before[:, :, 64:65])[d]
        total = stats[:, 48:56]
        mids = stats[:, 56:64]
        V(nc.vector.tensor_copy, total.unsqueeze(2), upto[:, :, P - 1:P], after=[V])
        V(nc.vector.tensor_copy, mids.unsqueeze(2), mid, after=[V])
        midb = mids.unsqueeze(2).to_broadcast([P, 8, P])
        total2, mids2 = split(total, 4, 2), split(mids, 4, 2)
        if d == 0:
            V(nc.vector.tensor_tensor, upto, upto, midb, ALU.subtract, after=[V])
            V(nc.vector.tensor_tensor, before, before, midb, ALU.subtract, after=[V])
            plus, less = tmp, cur
            V(nc.vector.tensor_tensor, scale_state, total2[:, :, 0], mids2[:, :, 0], ALU.subtract, after=[V])
            V(nc.vector.tensor_tensor, scale_state, scale_state, mids2[:, :, 1], ALU.add, after=[V])
        else:
            V(nc.vector.tensor_tensor, upto, midb, upto, ALU.subtract, after=[V])
            V(nc.vector.tensor_tensor, before, midb, before, ALU.subtract, after=[V])
            plus, less = cur, tmp
            V(nc.vector.tensor_tensor, scale_state, total2[:, :, 0], mids2[:, :, 0], ALU.subtract, after=[V])
            V(nc.vector.tensor_tensor, scale_state, scale_state, mids2[:, :, 1], ALU.add, after=[V])
        A(nc.scalar.activation, scale_state, scale_state, ACT.Exp, after=[V])
        A(nc.scalar.activation, flat(less), flat(less), ACT.Exp, after=[V])
        V(nc.vector.scalar_tensor_tensor, arT[:, :, 0, :], less, -1.0, kkT, ALU.mult, ALU.mult, after=[A])
        A(nc.scalar.activation, flat(less), flat(plus), ACT.Exp, scale=-1.0, after=[V])
        V(nc.vector.tensor_tensor, dbT, less, bT, ALU.mult, after=[A])
        V(nc.vector.tensor_tensor, dkT, less, rkvT[:, 1], ALU.mult, after=[A])
        A(nc.scalar.activation, flat(plus), flat(plus), ACT.Exp, after=[A])
        V(nc.vector.tensor_tensor, arT[:, :, 1, :], plus, rkvT[:, 0], ALU.mult, after=[A])

        for step in range(TT):
            c = step if d == 0 else TT - 1 - step
            cut = slice(c * P, (c + 1) * P)
            for h in range(RK_HEADS):
                hr = slice(64 * (h % 2), 64 * (h % 2) + 64)
                b = k.bank()
                for j, left in enumerate((dbT, dkT)):
                    k.matmul(b.ap[:, j * 2 * P:(j + 1) * 2 * P], left[hr, h // 2, cut], arT[hr, h // 2, :, cut], True, True,
                             after=[*b.free, V] if j == 0 else ())
                V(nc.vector.tensor_tensor, M[:, h].rearrange("p a b -> p (a b)"), b.ap, table(f"rk_mask{d}"), ALU.mult, after=[T])
                b.free = [V.mark()]
            tri.invert(M[:, :, 0, :], d, [V.mark()])
            heads = lambda a: split(a, 8, 64)

            def pair_sums(terms, through_state, after):
                b = k.bank()
                first = True
                for m in range(RK_PAIRS):
                    if step:
                        k.matmul(b.ap[:, m * P:(m + 1) * P], arT[:, m, through_state, cut], state[:, m * P:(m + 1) * P],
                                 True, False, after=[*b.free, *after] if first else ())
                        first = False
                    for h in (2 * m, 2 * m + 1):
                        for j, (which, right) in enumerate(terms):
                            k.matmul(b.ap[:, h * 64:(h + 1) * 64], M[:, h, which, :], right[:, h * 64:(h + 1) * 64],
                                     not step and j == 0, j == len(terms) - 1 and (not step or h % 2 == 1), after=[*b.free, *after] if first else ())
                            first = False
                return b

            b = pair_sums([(2, v_tok[:, c, :])], 0, [V, A, *v_ready])
            b.free = [k.copy(V, rhs, b.ap, after=[T])]
            tri.solve(list(range(8)), heads(rhs), heads(U), heads(work), 64, [V.mark()])
            b = pair_sums([(1, U), (3, v_tok[:, c, :])], 1, [V])
            if d == 0:
                V(nc.vector.tensor_copy, o_rk[:, c, :], b.ap, after=[T])
            else:
                V(nc.vector.tensor_tensor, o_rk[:, c, :], o_rk[:, c, :], b.ap, ALU.add, after=[T, V])
            b.free = [V.mark()]
            if step == 0:
                for src, dst in ((dbT, db_tok), (dkT, dk_tok)):
                    b = k.bank()
                    for m in range(4):
                        k.transpose(b.ap[:, m * P:(m + 1) * P], src[:, m, cut], after=[*b.free, V] if m == 0 else (), inc=m == 3)
                    b.free = [k.copy(A, dst, b.ap, after=[T])]
                b = k.bank()
                for m in range(RK_PAIRS):
                    ms = slice(m * P, (m + 1) * P)
                    k.matmul(b.ap[:, ms], db_tok[:, ms], U[:, ms], True, False, after=[*b.free, A, V] if m == 0 else ())
                    k.matmul(b.ap[:, ms], dk_tok[:, ms], v_tok[:, c, ms], False, True)
                for m in range(RK_PAIRS):
                    ms = slice(m * P, (m + 1) * P)
                    V(nc.vector.scalar_tensor_tensor, state[:, ms], b.ap[:, ms], scale_state[:, m:m + 1], table("pairs"),
                      ALU.mult, ALU.mult, after=[T, A])
                b.free = [V.mark()]

    for t in range(TT):
        o = o_rk[:, t, :]
        o8, w8 = split(o, 8, 64), split(work, 8, 64)
        mean, var, st = stats[:, 64:72], stats[:, 72:80], stats[:, 80:88]
        bc = lambda a: a.unsqueeze(2).to_broadcast([P, 8, 64])
        V(nc.vector.tensor_reduce, mean, o8, AX.X, ALU.add, after=[V, T])
        V(nc.vector.tensor_scalar, mean, mean, 1.0 / 64, None, ALU.mult, after=[V])
        V(nc.vector.tensor_tensor, o8, o8, bc(mean), ALU.subtract, after=[V])
        V(nc.vector.tensor_tensor, work, o, o, ALU.mult, after=[V])
        V(nc.vector.tensor_reduce, var, w8, AX.X, ALU.add, after=[V])
        k.rstd(st, var, 64, EPS_GN, after=[V])
        V(nc.vector.tensor_tensor, o8, o8, bc(st), ALU.mult, after=[V])
        V(nc.vector.tensor_tensor, o, o, ln_w, ALU.mult, after=[V])
        V(nc.vector.tensor_tensor, o, o, ln_b, ALU.add, after=[V])
        V(nc.vector.tensor_tensor, w8, split(v_tok[:, t, :], 8, 64), bc(bonus[:, t, :]), ALU.mult, after=[V])
        V(nc.vector.tensor_tensor, o, o, work, ALU.add, after=[V])
        V(nc.vector.tensor_tensor, o, o, silu_rk[:, t, :], ALU.mult, after=[V, A])
    close_layer(k, 0, x, mixed, hT, free_at)
    k.top = floor


def odd_layer(k, x):
    nc, T, V, A, G, SP = k.nc, k.T, k.V, k.A, k.G, k.SP
    dram, table, take = k.dram, k.table, k.take
    k.begin()
    floor = k.top
    w_in = dram["odd_w_in"].rearrange("(k p) n -> p k n", p=P)
    mixed = take(TT, D)
    hT = take(KT, S)
    free_at = k.top
    cols = take(100)
    xv = take(3, TT, D)
    H = take(5, D)
    U = take(4, D)
    Y = take(4, D)
    deltas = take(2, D)
    skip = take(D)
    sine = take(4, S)
    w123 = take(3, HY_F)
    over = U.rearrange("p a b -> p (a b)")
    raw = [k.c.buf(split(over[:, j * 2 * (S + 4):(j + 1) * 2 * (S + 4)], 2, S + 4)) for j in range(2)]
    conv = [k.c.buf(split(over[:, (4 + j) * WB:(5 + j) * WB], 2, S)) for j in range(2)]
    norm = take(D)
    cw, cb = split(cols[:, 0:72], HY_SHORT, 24), cols[:, 72:96]
    fb, freq = cols[0:HY_F, 96:99], cols[0:HY_F, 99:100]

    k.load_tables("odd")
    SP.dma(k.small_loaded, cols, dram["odd_cols"])
    for j, (name, n) in enumerate((("hy_w1", HY_EMB), ("hy_w2", HY_F), ("hy_w3", HY_F))):
        SP.dma(k.small_loaded, w123[0:n, j, :], dram[name])
    small_ready = k.small_loaded.mark()
    for r in raw:
        V(nc.vector.memset, r.ap.rearrange("p a b -> p (a b)"), 0.0)
    k.transposes(x, hT, KT, after=[])
    h_ready = [V.mark(), A.mark()]

    hid = sine[0:HY_F, 0, :]
    for j, n in enumerate((HY_EMB, HY_F, HY_F)):
        b = k.bank()
        right = table("feats")[0:n, :] if j == 0 else hid
        k.matmul(b.ap[0:HY_F, 0:S], w123[0:n, j, :], right, True, True, after=[*b.free, small_ready, A])
        ang, turns, work = (sine[0:HY_F, m, :] for m in (1, 2, 3))
        V(nc.vector.tensor_scalar, ang, b.ap[0:HY_F, 0:S], fb[:, j:j + 1], freq, ALU.add, ALU.mult, after=[T, small_ready])
        b.free = [V.mark()]
        k.wrapped_sin(hid, ang, turns, work, 0, after=[V])
    hid_ready = A.mark()

    conv_flat, bias_flat = cw, cb

    def project(i):
        for j in range(2):
            slot, loaded = k.load_slot([(0, (KT, WB), w_in[:, :, bass.ds(i * D + j * WB, WB)])], slot=j)
            w = split(slot.ap, KT, WB)
            for m0, b, _, mark in k.feature_major(lambda kk, m: w[:, kk, m * P:(m + 1) * P], [loaded, *h_ready], hT, 4):
                r, y = raw[m0 // 2], conv[m0 // 2]
                padded_copy(k, r.ap, b, 2, 2, after=[mark, *r.free, *raw_zeroed])
                b.free = [A.mark()]
                for q in range(2):
                    f = i * 8 + (j * 4 + m0 + q)
                    col = lambda a: a[:, bass.ds(f, 1)]
                    m = V(nc.vector.tensor_scalar, y.ap[:, q, :], r.ap[:, q, 1:1 + S], col(cw[:, 0, :]), col(cb),
                          ALU.mult, ALU.add, after=[A, small_ready, *y.free])
                    for tap in (1, 2):
                        m = V(nc.vector.scalar_tensor_tensor, y.ap[:, q, :], r.ap[:, q, 1 + tap:1 + tap + S],
                              col(cw[:, tap, :]), y.ap[:, q, :], ALU.mult, ALU.add, after=[m])
                r.free = [m]
                bt = k.bank()
                for t in range(TT):
                    for q in range(2):
                        k.transpose(bt.ap[:, (2 * t + q) * P:(2 * t + q + 1) * P], y.ap[:, q, t * P:(t + 1) * P],
                                    after=[*bt.free, m] if t + q == 0 else (), inc=t + q == 2)
                y.free = [T.mark()]
                at = (j * 4 + m0) * P
                dst = xv[:, bass.ds(i, 1)][:, 0][:, :, at:at + 2 * P]
                bt.free = [k.copy(A, dst, split(bt.ap, TT, 2 * P), after=[T])]
            slot.free = [T.mark()]

    raw_zeroed = [V.mark()]
    k.c.loop(3, project)
    for hf in range(2):
        slot, loaded = k.load_slot([(0, (KT, WB), w_in[:, :, HY_XV + hf * WB:HY_XV + (hf + 1) * WB])], slot=2 + hf)
        w = split(slot.ap, KT, WB)
        for t, b, mark in k.token_major(lambda kk: w[:, kk, :], [loaded], hT, WB):
            A(nc.scalar.activation, mixed[:, t, hf * WB:(hf + 1) * WB], b.ap, ACT.Silu, after=[mark])
            b.free = [A.mark()]
        slot.free = [T.mark()]

    ft = split(Y.rearrange("p a b -> p (a b)"), 2, TT, D)
    dft_re = split(table("dft_re"), TT, S)
    dft_im = split(table("dft_im_signal"), TT, S)
    dft_im0 = split(table("dft_im_filter0"), TT, P)
    dft_rc0 = split(table("dft_re_cross0"), TT, P)
    idft = split(table("idft"), 4, S)
    fw = dram["hy_out"]
    for o in range(HY_ORDER):
        SP.dma(k.rows_loaded, deltas.rearrange("p a b -> p (a b)"),
               dram["hy_deltas"][:, o * 2 * D:(o + 1) * 2 * D].partition_broadcast(P)[:, 0, :], after=[V, A, G])
        SP.dma(k.rows_loaded, skip, dram["hy_skip"][o:o + 1, :].partition_broadcast(P)[:, 0, :], after=[G])
        A(nc.scalar.activation, deltas.rearrange("p a b -> p (a b)"), deltas.rearrange("p a b -> p (a b)"), ACT.Abs,
          after=[k.rows_loaded])
        slot, loaded = load_rows(k, fw[:, o * 2 * D:(o + 1) * 2 * D], o)
        for t in range(TT):
            for n in range(4):
                f, hf = n // 2, n % 2
                cut = slice(hf * WB, (hf + 1) * WB)
                b = k.bank()
                k.matmul(b.ap, hid[:, t * P:(t + 1) * P], slot.ap[0:HY_F, n * WB:(n + 1) * WB], True, True,
                         after=[*b.free, loaded, hid_ready])
                A(nc.scalar.activation, ft[:, f, t, cut], deltas[:, f, cut], ACT.Exp, scale=table("minus_t")[:, t:t + 1],
                  after=[A, V, T])
                V(nc.vector.tensor_tensor, ft[:, f, t, cut], ft[:, f, t, cut], b.ap, ALU.mult, after=[A, T])
                b.free = [V.mark()]
        slot.free = [T.mark()]
        V(nc.vector.memset, ft[0:1, 1, 0, :], 0.0, after=[V])
        mag = split(U.rearrange("p a b -> p (a b)"), 2, TT, D)
        A(nc.scalar.activation, mag.rearrange("p a b c -> p (a b c)"), ft.rearrange("p a b c -> p (a b c)"), ACT.Abs, after=[V, T])
        for hf in range(2):
            cut = slice(hf * WB, (hf + 1) * WB)
            b = k.bank()
            for n in range(4):
                k.matmul(b.ap, table("ones"), mag[:, n // 2, n % 2, cut], n == 0, n == 3, after=[*b.free, A] if n == 0 else ())
            V(nc.vector.tensor_scalar, norm[:, cut], b.ap, EPS_RMS, None, ALU.add, after=[T])
            b.free = [V.mark()]
        V(nc.vector.reciprocal, norm, norm, after=[V])
        flat = lambda a: a.rearrange("p a b -> p (a b)")
        G(nc.gpsimd.tensor_tensor, flat(mag[:, 0]), flat(ft[:, 0]), flat(ft[:, 1]), ALU.add, after=[T, V])
        V(nc.vector.tensor_tensor, flat(mag[:, 1]), flat(ft[:, 0]), flat(ft[:, 1]), ALU.subtract, after=[T, V])
        spectrum = [(0, 0, lambda t: dft_re[:, t, 0:P]), (1, 0, lambda t: dft_re[:, t, P:]),
                    (2, 1, lambda t: dft_im0[:, t, :]), (3, 1, lambda t: dft_im[:, t, P:]),
                    (4, 0, lambda t: dft_rc0[:, t, :])]
        for tile, which, left in spectrum:
            for hf in range(2):
                cut = slice(hf * WB, (hf + 1) * WB)
                b = k.bank()
                for t in range(TT):
                    k.matmul(b.ap, left(t), mag[:, which, t, cut], t == 0, t == TT - 1, after=[*b.free, V, G] if t == 0 else ())
                V(nc.vector.tensor_tensor, H[:, tile, cut], b.ap, norm[:, cut], ALU.mult, after=[T])
                b.free = [V.mark()]
        signal = xv[:, 2]
        filter_done = [V.mark(), T.mark()]
        for tile in range(4):
            left = (dft_re if tile < 2 else dft_im)[:, :, (tile % 2) * P:(tile % 2 + 1) * P]
            for hf in range(2):
                cut = slice(hf * WB, (hf + 1) * WB)
                b = k.bank()
                for t in range(TT):
                    k.matmul(b.ap, left[:, t, :], signal[:, t, cut], t == 0, t == TT - 1,
                             after=[*b.free, V, A, G] if t == 0 else ())
                b.free = [k.copy(A, U[:, tile, cut], b.ap, after=[T, *filter_done])]
        for tile in range(2):
            re, im = U[:, tile, :], U[:, 2 + tile, :]
            hr, hi, own = H[:, tile, :], H[:, 2 + tile, :], (H[:, 4, :] if tile == 0 else H[:, 1, :])
            yr, yi = Y[:, tile, :], Y[:, 2 + tile, :]
            V(nc.vector.tensor_tensor, yr, re, hr, ALU.mult, after=[A, V, T, G])
            G(nc.gpsimd.tensor_tensor, yi, re, hi, ALU.mult, after=[A, V, T])
            V(nc.vector.tensor_tensor, re, im, hi, ALU.mult, after=[V, G])
            V(nc.vector.tensor_tensor, yr, yr, re, ALU.subtract, after=[V])
            G(nc.gpsimd.tensor_tensor, im, im, own, ALU.mult, after=[V])
            G(nc.gpsimd.tensor_tensor, yi, yi, im, ALU.add, after=[G])
        product = [V.mark(), G.mark()]
        for t in range(TT):
            for hf in range(2):
                cut = slice(hf * WB, (hf + 1) * WB)
                b = k.bank()
                for kk in range(4):
                    k.matmul(b.ap, idft[:, kk, t * P:(t + 1) * P], Y[:, kk, cut], kk == 0, kk == 3,
                             after=[*b.free, *product] if kk == 0 else ())
                s = signal[:, t, cut]
                V(nc.vector.tensor_tensor, s, s, skip[:, cut], ALU.mult, after=[V, k.rows_loaded, T])
                V(nc.vector.tensor_tensor, s, s, b.ap, ALU.add, after=[T, V])
                b.free = [V.mark()]
                V(nc.vector.tensor_tensor, s, s, xv[:, o, t, cut], ALU.mult, after=[V])
    for t in range(TT):
        V(nc.vector.tensor_tensor, mixed[:, t, :], mixed[:, t, :], xv[:, 2, t, :], ALU.mult, after=[V, A])
    close_layer(k, 1, x, mixed, hT, free_at)
    k.top = floor


def load_rows(k, src, slot):
    b = k.slots[slot]
    return b, k.SP.dma(k.slot_loaded[slot], b.ap[0:HY_F, 0:2 * D], src, after=b.free)


def build(nc, dram, table_at, table_words, parts=(True, True, True)):
    k = Core(nc, dram, table_at, table_words)
    x = k.take(TT, D)
    by_tokens = lambda ap: ap.rearrange("b (t p) d -> p (b t) d", p=P)
    nc.sync.dma_start(x, by_tokens(dram["x"])).then_inc(k.small_loaded.sem, 16)
    nc.sync.dma_start(k.tables[:, 0:dram["tables_all"].shape[1]], dram["tables_all"]).then_inc(k.small_loaded.sem, 16)
    nc.sync.wait_ge(k.small_loaded.sem, 32)
    if parts[0]:
        first_block(k, x)
    if parts[1]:
        even_layer(k, x)
    if parts[2]:
        odd_layer(k, x)
    k.begin()
    k.SP.dma(k.out_stored, by_tokens(dram["out"]), x)
    k.SP.wait([k.out_stored])


def feature_columns(*arrays):
    out = []
    for a in arrays:
        a = a.reshape(-1, a.shape[-1])
        pad = -a.shape[1] % P
        a = np.concatenate([a, np.zeros((a.shape[0], pad), a.dtype)], 1) if pad else a
        out.append(a.reshape(-1, P).T)
    return np.ascontiguousarray(np.concatenate(out, 1))


def heads_apart(w, first):
    l, r, n = w.shape
    w = w.reshape(l, r, MLA_HEADS, n // MLA_HEADS)
    return np.ascontiguousarray(np.concatenate([w[..., :first].reshape(l, r, -1), w[..., first:].reshape(l, r, -1)], 2))


def lay_out(inputs):
    a = {name: np.asarray(v) for name, v in inputs.items()}
    out = {f"tables_{which}": np.concatenate(list(t.values()), 1) for which, t in const_tables().items()}
    for name in ("x", "rel_bias", "w_in", "w_branch", "w_out", "w_up", "w_down", "norm_mix_post", "norm_mlp_post", "w_out_2"):
        out[name] = a[name]
    out["positions"] = np.ascontiguousarray(a["positions"].reshape(TT, P).T)
    out["mla_w_uq"] = heads_apart(a["mla_w_uq"], NOPE)
    out["mla_w_ukv"] = heads_apart(a["mla_w_ukv"], NOPE)
    out["diff_lambda"] = a["diff_lambda"].reshape(DEPTH, -1)
    out["cols"] = np.stack([feature_columns(*(a[n][l] for n in ("norm_mix_pre", "norm_mlp_pre", "diff_subln", "mla_q_norm", "mla_kv_norm")))
                            for l in range(DEPTH)], 1)
    out["pT"] = np.ascontiguousarray(a["p_2"][:, 0].transpose(0, 2, 1))
    out["even_w_in"] = a["even_w_in_2"][0]
    out["odd_w_in"] = a["odd_w_in_2"][0]
    for name in ("dn_a_log", "dn_dt_bias", "dn_norm", "rk_ln_w", "rk_ln_b", "hy_deltas"):
        out[name] = a[name + "_2"].reshape(1, -1)
    out["rk_w2"] = a["rk_w2_2"].reshape(P, RK_W)
    out["rk_a2"] = a["rk_a2_2"][0]
    out["hy_skip"] = a["hy_skip_2"][0]
    for j in (1, 2, 3):
        out[f"hy_w{j}"] = a[f"hy_ffn_w{j}_2"][0]
    out["hy_out"] = a["hy_ffn_out_2"][0]
    for name in ("ln_g", "ln_b", "ple_norm", "ple_w", "ple_gate"):
        out[name] = a[name + "_2"]
    out["even_cols"] = feature_columns(a["dn_conv_2"], a["rk_mu_2"], a["rk_w0_2"], a["rk_a0_2"], a["rk_k_k_2"], a["rk_k_a_2"],
                                       a["rk_r_k_2"].reshape(1, -1))
    out["odd_cols"] = feature_columns(a["hy_conv_w_2"], a["hy_conv_b_2"], a["hy_ffn_b1_2"], a["hy_ffn_b2_2"], a["hy_ffn_b3_2"],
                                      a["hy_ffn_freq_2"])
    return out


def declare_and_build(nc, arrays, parts=(True, True, True)):
    dram = {name: nc.dram_tensor(f"{name}_dram", a.shape, mybir.dt.from_np(a.dtype), kind="ExternalInput").ap()
            for name, a in arrays.items()}
    dram["diagonals"] = nc.dram_tensor("diagonals", (N_BIAS, REL_W + 1), FP32).ap()
    dram["out"] = nc.dram_tensor("out_dram", (1, S, D), FP32, kind="ExternalOutput").ap()
    at, words = offsets(const_tables())
    build(nc, dram, at, words, parts)


def kernel(**inputs):
    import concourse.bacc as bacc
    from concourse.bass_utils import run_bass_kernel_spmd

    arrays = lay_out(inputs)
    nc = bacc.Bacc("TRN2", target_bir_lowering=False, num_devices=1)
    declare_and_build(nc, arrays)
    ran = run_bass_kernel_spmd(nc, [{f"{name}_dram": a for name, a in arrays.items()}], core_ids=[0])
    return ran.results[0]["out_dram"]
```

```python
import math

import numpy as np

import concourse.bass as bass
from concourse import mybir
from concourse.alu_op_type import AluOpType as ALU

FP32 = mybir.dt.float32
INT32 = mybir.dt.int32
ACT = mybir.ActivationFunctionType
AX = mybir.AxisListType

P = 128
S = 256
TT = S // P
D = 1024
KT = D // P
DEPTH = 2
D_FF = 4 * D
EPS_RMS = 1e-6
EPS_LN = 1e-5
EPS_GN = 64e-5
NEG = -1e30
DIFF_HEADS, MOBA_HEADS, MLA_HEADS = 4, 4, 8
Q_RANK, KV_RANK, NOPE, ROPE, VDIM = 256, 128, 64, 32, 64
WB = 512
N_BRANCH = 3
MLA_IN = 6 * WB
GATE_IN = MLA_IN + Q_RANK + KV_RANK + ROPE
BUCKETS = 32
N_BIAS = DIFF_HEADS + MOBA_HEADS
REL_W = S + P - 1
SCORE_W = S + P
ALPHA = (2.0 * DEPTH) ** 0.25
DN_HEADS, DN_CONV = 4, 5
DN_QKV = 3 * DN_HEADS * P
DN_AB = 4 * DN_HEADS
RK_HEADS, RK_W, LORA = 8, 512, 64
RK_PAIRS = RK_HEADS // 2
RK_SHIFT = 3 * RK_W + 3 * LORA
AB_IN = DN_QKV
DN_GATE_IN = AB_IN + DN_AB
RK_IN = DN_GATE_IN + WB
RK_GATE_IN = RK_IN + RK_SHIFT
HY_ORDER, HY_SHORT, HY_EMB, HY_F = 2, 3, 33, 64
HY_XV = 3 * D
PLE = 256
LEVELS = 7
BASE = 600
RAW_SLOTS = 4
CUT_SLOTS = 2
PIECE = 2048
FP32R = mybir.dt.float32r


class Mark:

    def __init__(self, queue, n, tag):
        self.queue, self.n, self.tag = queue, n, tag


class Buf:

    def __init__(self, ap=None):
        self.ap, self.free, self.ready = ap, [], []


class Counter:

    def __init__(self, nc):
        self.nc, self.dry, self.tag, self.tags = nc, False, 0, 0
        self.queues, self.bufs, self.done = [], [], {}
        self.per, self.i, self.bank, self.piece = {}, None, 0, 0

    def buf(self, ap=None):
        b = Buf(ap)
        self.bufs.append(b)
        return b

    def value(self, m):
        if m.tag == 0:
            return m.n
        if m.tag == self.tag:
            return m.n + self.i * self.per[m.queue]
        count, per = self.done[m.tag]
        return m.n + (count - 1) * per[m.queue]

    def loop(self, count, body):
        self.tags += 1
        start = [q.n for q in self.queues]
        before = [(b.free, b.ready) for b in self.bufs]
        bank, piece = self.bank, self.piece
        self.dry, self.tag = True, self.tags
        body(0)
        self.per = {q: q.n - n for q, n in zip(self.queues, start)}
        for q, n in zip(self.queues, start):
            q.n = n
        back = lambda marks: [Mark(m.queue, m.n - self.per[m.queue], m.tag) for m in marks if m.tag == self.tag]
        for b, (free, ready) in zip(self.bufs, before):
            b.free, b.ready = free + back(b.free), ready + back(b.ready)
        assert (self.piece - piece) % RAW_SLOTS == 0 and (self.piece - piece) % CUT_SLOTS == 0
        self.bank, self.piece = bank, piece
        self.dry = False
        with self.nc.Fori(0, count) as i:
            self.i = i
            body(i)
        for q, n in zip(self.queues, start):
            q.n = n + count * self.per[q]
        self.done[self.tag] = (count, self.per)
        self.tag = 0


class Queue:

    def __init__(self, counter, engine, sem):
        self.c, self.engine, self.sem, self.n, self.seen = counter, engine, sem, 0, {}
        counter.queues.append(self)

    def mark(self):
        return Mark(self, self.n, self.c.tag)

    def wait(self, marks):
        if self.c.dry:
            return
        for m in marks:
            m = m.mark() if isinstance(m, Queue) else m
            value = self.c.value(m)
            key = (m.queue, m.tag if m.tag == self.c.tag else 0)
            n = m.n if key[1] else value
            if n <= self.seen.get(key, 0) or n == 0:
                continue
            assert n > 0
            self.seen[key] = n
            self.engine.wait_ge(m.queue.sem, value)

    def __call__(self, op, *args, after=(), inc=True, **kw):
        self.wait(after)
        if inc:
            self.n += 1
        if not self.c.dry:
            ins = op(*args, **kw)
            if inc:
                ins.then_inc(self.sem, 1)
        return self.mark()

    def dma(self, dsem, out, in_, after=()):
        self.wait(after)
        dsem.n += 16
        if not self.c.dry:
            self.engine.dma_start(out, in_).then_inc(dsem.sem, 16)
        return dsem.mark()


def const_tables():
    f32 = np.float32
    p = np.arange(P)[:, None]
    c = np.arange(P)[None, :]
    out = {}
    out["ident"] = (p == c)
    out["ones"] = np.ones((P, P))
    out["pairs"] = (p // 64 == c // 64)
    out["flip"] = (p + c == P - 1)
    causal = lambda off: np.where(off + p - np.arange(S)[None, :] >= 0, 0.0, NEG)
    out["causal"] = np.concatenate([causal(P), causal(0)[:, :P]], 1)
    incl = [(c >= p), (c <= p)]
    strict = [(c > p), (c < p)]
    for d in range(2):
        out[f"incl{d}"] = incl[d]
        out[f"strict{d}"] = strict[d]
        out[f"rk_mask{d}"] = np.concatenate([-1.0 * strict[d], incl[d], strict[d], incl[d]], 1)
        for lv in range(LEVELS):
            b = 1 << lv
            same = (p // (2 * b) == c // (2 * b))
            m = same & (c // b % 2 == 1) & (p // b % 2 == 0)
            out[f"level{d}_{lv}"] = m if d == 0 else m.T
    fresh = np.ones((P, 4 * S))
    fresh[:, ::P] = 0.0
    out["fresh"] = fresh
    out["head_sel"] = (p // 64 == np.arange(2)[None, :])
    rel = S - 1 - np.arange(REL_W)
    n = np.maximum(rel, 0)
    nf = np.maximum(n, 1).astype(f32)
    large = 16 + (np.log(nf / f32(16)).astype(f32) / f32(math.log(1024 / 16)) * f32(16)).astype(np.int32)
    bucket = np.where(n < 16, n, np.minimum(large, BUCKETS - 1))
    onehot = np.zeros((P, REL_W))
    onehot[bucket, np.arange(REL_W)] = 1.0
    onehot[:, rel < 0] = 0.0
    onehot[BUCKETS, rel < 0] = NEG
    out["bucket"] = onehot
    inv = np.power(f32(10000.0), -np.arange(ROPE // 2, dtype=f32) * f32(2.0) / f32(ROPE)).astype(f32)
    out["inv_freq"] = np.repeat(inv[None, :], P, 0)
    lam = [0.8 - 0.6 * math.exp(-0.3 * l) for l in range(DEPTH)]
    out["lam"] = np.repeat(np.array([[v for x in lam for v in (x, 1.0 - x)]]), P, 0)
    t = np.arange(S)[:, None]
    f = np.arange(S)[None, :]
    ang = 2.0 * np.pi * ((t * f) % (2 * S)) / (2 * S)
    alt = np.where(np.arange(S) % 2 == 0, 1.0, -1.0)
    tiles = lambda m: m.reshape(TT, P, -1).transpose(1, 0, 2).reshape(P, -1)
    re, im = np.cos(ang), -np.sin(ang)
    im[:, 0] = 0.0
    im_u, re_2 = im.copy(), re[:, :P].copy()
    im_u[:, 0] = alt
    re_2[:, 0] = alt
    out["dft_re"] = tiles(re)
    out["dft_im_signal"] = tiles(im_u)
    out["dft_im_filter0"] = tiles(im[:, :P])
    out["dft_re_cross0"] = tiles(re_2)
    ire = np.cos(ang.T) * 2.0 / (2 * S)
    ire[0] /= 2.0
    iim = -np.sin(ang.T) * 2.0 / (2 * S)
    iim[0] = alt / (2 * S)
    out["idft"] = np.concatenate([tiles(ire), tiles(iim)], 1)
    out["minus_t"] = tiles(-np.linspace(0.0, 1.0, S, dtype=f32)[:, None])
    tl = np.linspace(0.0, 1.0, S, dtype=f32)[:, None]
    fb = np.linspace(1e-4, 15, 16, dtype=f32)[None, :]
    an = (f32(2.0 * math.pi / S) * np.arange(S, dtype=f32)[:, None] * fb).astype(f32)
    feats = np.zeros((P, S))
    feats[:HY_EMB] = np.concatenate([tl, np.cos(an), -np.sin(an)], -1).T
    out["feats"] = feats
    stage = lambda name: ("all" if name in ("ident", "ones", "pairs", "head_sel") else
                          "first" if name in ("flip", "causal", "bucket", "inv_freq", "lam") else
                          "even" if name[:4] in ("incl", "stri", "rk_m", "leve", "fres") else "odd")
    return {which: {name: np.ascontiguousarray(v, dtype=f32) for name, v in out.items() if stage(name) == which}
            for which in ("all", "first", "even", "odd")}


def offsets(sets):
    out, most, start = {}, 0, 0
    for which, tables in sets.items():
        at = start
        for name, a in tables.items():
            out[name] = (at, a.shape[1])
            at += a.shape[1]
        if which == "all":
            start = at
        most = max(most, at)
    return out, most


class Core:

    def __init__(self, nc, dram, table_at, table_words):
        self.nc, self.dram, self.table_at = nc, dram, table_at
        c = self.c = Counter(nc)
        sem = nc.alloc_semaphore
        self.T = Queue(c, nc.tensor, sem("tensor_done"))
        self.V = Queue(c, nc.vector, sem("vector_done"))
        self.A = Queue(c, nc.scalar, sem("scalar_done"))
        self.G = Queue(c, nc.gpsimd, sem("gpsimd_done"))
        self.SP = Queue(c, nc.sync, sem("sync_done"))
        self.slot_loaded = [Queue(c, None, sem(f"slot{k}_loaded")) for k in range(RAW_SLOTS)]
        self.small_loaded = Queue(c, None, sem("small_loaded"))
        self.rows_loaded = Queue(c, None, sem("rows_loaded"))
        self.scratch_stored = Queue(c, None, sem("scratch_stored"))
        self.out_stored = Queue(c, None, sem("out_stored"))
        words = (nc.sbuf_usable_end - nc.sbuf_base) // 4 - 64
        self.words = words
        nc.alloc_sbuf_tensor("memory", [P, words], FP32)
        self.origin = nc.sbuf_base - 4 * words
        assert self.origin % 32 == 0
        self.top = self.places = 0
        self.planned, self.pending = [], None
        self.rotating = 8
        self.banks = [c.buf(nc.alloc_psum_tensor(f"bank{k}", [P, 512], FP32)[:]) for k in range(8)]
        self.raw = [c.buf(self.take(PIECE)) for _ in range(RAW_SLOTS)]
        self.cut = [c.buf(self.take_parts(f"weights{j}", PIECE)) for j in range(CUT_SLOTS)]
        self.tables_at = self.top
        self.tables = self.take(table_words)

    def take(self, *dims):
        n = int(np.prod(dims))
        at = -(-self.top // 8) * 8
        self.top = at + n
        assert self.top <= self.words, (self.top, self.words)
        return split(self.words_at(at, n), *dims)

    def words_at(self, at, n, dtype=FP32, name=None):
        self.places += 1
        return self.nc.alloc_sbuf_tensor_at(name or f"place{self.places}", [P, n], dtype, offset=self.origin + 4 * at)[:]

    def take_parts(self, name, *dims):
        n = int(np.prod(dims))
        parts = []
        for part in ("high", "low"):
            self.top = -(-self.top // 8) * 8 + n
            assert self.top <= self.words
            parts.append(split(self.words_at(self.top - n, n, FP32R, f"{name}_{part}"), *dims))
        return tuple(parts)

    def load_tables(self, which, after=()):
        src = self.dram[f"tables_{which}"]
        at = 0 if which == "all" else self.dram["tables_all"].shape[1]
        return self.SP.dma(self.small_loaded, self.tables[:, at:at + src.shape[1]], src, after=after)

    def table(self, name):
        at, n = self.table_at[name]
        return self.tables[:, at:at + n]

    def bank(self):
        b = self.banks[self.c.bank % self.rotating]
        self.c.bank += 1
        return b

    def fetch(self, *parts):
        c = self.c
        raw, cut = self.raw[c.piece % RAW_SLOTS], self.cut[c.piece % CUT_SLOTS]
        queue = self.slot_loaded[c.piece % RAW_SLOTS]
        c.piece += 1
        at = 0
        for dims, src in parts:
            n = int(np.prod(dims))
            self.SP.dma(queue, split(raw.ap[:, at:at + n], *dims), src, after=raw.free)
            at += n
        high, low = cut.ap
        half = at // 2 // 128 * 128
        for lo, hi in ((0, half), (half, at)) if half else ((0, at),):
            self.cut_in_two(raw.ap[:, lo:hi], (high[:, lo:hi], low[:, lo:hi]), [queue, *cut.free])
        raw.free, cut.ready = [self.V.mark()], [self.V.mark()]
        return cut

    def plan(self, *fetches):
        self.planned += fetches
        if self.pending is None:
            self.pending = self.planned.pop(0)()

    def next(self):
        cut, self.pending = self.pending, None
        if self.planned:
            self.pending = self.planned.pop(0)()
        return cut

    def columns(self, w, first, n=S):
        return lambda: self.fetch(((KT, n), w[:, :, pick(first, n)]))

    def rows(self, w, tile, tiles, first, n):
        return lambda: self.fetch(((tiles, n), w[:, pick(tile, tiles), pick(first, n)]))

    def by_rows(self, w, first, n=WB):
        return [self.rows(w, half * KT // 2, KT // 2, first, n) for half in range(2)]

    def cut_in_two(self, src, parts, after, scale=None):
        nc, (high, low) = self.nc, parts
        if scale is None:
            self.A(nc.scalar.activation, high, src, ACT.Copy, after=after)
            return self.V(nc.vector.tensor_tensor, low, src, high.bitcast(FP32), ALU.subtract, after=[self.A])
        self.A(nc.scalar.activation, high, src, ACT.Copy, scale=scale, after=after)
        return self.V(nc.vector.scalar_tensor_tensor, low, src, scale, high.bitcast(FP32), ALU.mult, ALU.subtract,
                      after=[self.A])

    def begin(self):
        nc, c = self.nc, self.c
        nc.all_engine_barrier()
        for q in c.queues:
            nc.sync.sem_clear(q.sem)
            q.n, q.seen = 0, {}
        for b in c.bufs:
            b.free, b.ready = [], []
        c.piece = 0
        nc.all_engine_barrier()
        for q in (self.T, self.V, self.A, self.G):
            q.engine.sem_inc(q.sem, BASE)
            q.n = BASE

    def matmul(self, out, lhsT, rhs, start, stop, after=(), inc=None):
        return self.T(self.nc.tensor.matmul, out, lhsT, rhs, start=start, stop=stop, after=after,
                      inc=stop if inc is None else inc)

    def transpose(self, out, in_, after=(), inc=True):
        return self.T(self.nc.tensor.transpose, out, in_, self.table("ident"), after=after, inc=inc)

    def product(self, out, left, right, first, last, after=(), inc=None):
        pairs = ((left[0], right[0]), (left[0], right[1]), (left[1], right[0]))
        for j, (a, b) in enumerate(pairs):
            mark = self.matmul(out, a, b, start=first and j == 0, stop=last and j == 2, after=after if j == 0 else (),
                               inc=inc if j == 2 else False)
        return mark

    def feature_major(self, weights, ready, xT, tiles, kt=KT):
        for m0 in range(0, tiles, 2):
            b = self.bank()
            for j in range(2):
                for k in range(kt):
                    mark = self.product(b.ap[:, j * S:(j + 1) * S], [weights(part, k, m0 + j) for part in (0, 1)],
                                        [x[:, k, :] for x in xT], k == 0, k == kt - 1,
                                        after=[*b.free, *ready] if k == 0 else ())
            yield m0, b, mark

    def two_tiles(self, xT, ready, kt=KT):
        cut = self.next()
        look = seen_as(kt, S)
        for _, b, mark in self.feature_major(lambda part, kk, m: look(cut, part, kk)[:, m * P:(m + 1) * P],
                                             [*cut.ready, *ready], xT, 2, kt):
            cut.free = [self.T.mark()]
            return b, mark

    def token_major(self, xT, n, tiles=(KT // 2, KT // 2), ready=(), view=None):
        banks = [self.bank() for _ in range(TT)]
        k0 = 0
        for m in tiles:
            cut = self.next()
            look = view or seen_as(m, n)
            for t in range(TT):
                b = banks[t]
                for k in range(m):
                    self.product(b.ap[:, 0:n], [x[:, k0 + k, t * P:(t + 1) * P] for x in xT],
                                 [look(cut, part, k) for part in (0, 1)], k0 + k == 0, k0 + k == sum(tiles) - 1,
                                 after=[*(b.free if k0 == 0 else ()), *cut.ready, *ready] if k == 0 else (),
                                 inc=k == m - 1)
            cut.free = [self.T.mark()]
            k0 += m
        for t in range(TT):
            yield t, banks[t], self.T.mark()

    def copy(self, engine, out, in_, after=(), scale=None):
        nc = self.nc
        if engine is self.V:
            if scale is None:
                return self.V(nc.vector.tensor_copy, out, in_, after=after)
            return self.V(nc.vector.tensor_scalar, out, in_, scale, None, ALU.mult, after=after)
        if scale is None:
            return self.A(nc.scalar.activation, out, in_, ACT.Copy, after=after)
        return self.A(nc.scalar.activation, out, in_, ACT.Copy, scale=scale, after=after)

    def rstd(self, out, sums, n, eps, after):
        nc, V, A = self.nc, self.V, self.A
        V(nc.vector.tensor_scalar, out, sums, 1.0 / n, eps, ALU.mult, ALU.add, after=after)
        A(nc.scalar.activation, out, out, ACT.Sqrt, after=[V])
        return V(nc.vector.reciprocal, out, out, after=[A])

    def transposes(self, src, dstT, tiles, after, scale=None):
        for k0 in range(0, tiles, 2):
            b = self.bank()
            pair = min(2, tiles - k0)
            for j in range(pair):
                for t in range(TT):
                    self.transpose(b.ap[:, j * S + t * P:j * S + (t + 1) * P],
                                   src[:, t, (k0 + j) * P:(k0 + j + 1) * P],
                                   after=[*b.free, *after] if j + t == 0 else ())
            moved = self.T.mark()
            e = self.V if k0 % 4 == 0 else self.A
            if scale is None:
                self.copy(e, dstT[:, k0:k0 + pair, :], split(b.ap, 2, S)[:, 0:pair, :], after=[moved])
            else:
                for j in range(pair):
                    self.copy(e, dstT[:, k0 + j, :], b.ap[:, j * S:(j + 1) * S], after=[moved],
                              scale=scale[:, k0 + j:k0 + j + 1])
            b.free = [e.mark()]

    def transposes_cut(self, src, dstT, tiles, after):
        for t in range(TT):
            for k0 in range(0, tiles, 4):
                b = self.bank()
                n = min(4, tiles - k0)
                for j in range(n):
                    self.transpose(b.ap[:, j * P:(j + 1) * P], src[:, t, (k0 + j) * P:(k0 + j + 1) * P],
                                   after=[*b.free, *after[t]] if j == 0 else (), inc=j == n - 1)
                self.cut_in_two(split(b.ap, 4, P)[:, 0:n, :], [x[:, k0:k0 + n, t * P:(t + 1) * P] for x in dstT], [self.T])
                b.free = [self.V.mark()]

    def weigh(self, b, mark, t, half, row, row_ready, junk, stats):
        nc, V, A = self.nc, self.V, self.A
        at = t * D + half * WB
        A(nc.scalar.activation, junk[:, at:at + WB], b.ap, ACT.Square, after=[mark, V],
          accum_out=stats[:, t * 2 + half:t * 2 + half + 1])
        b.free = [V(nc.vector.tensor_tensor, junk[:, at:at + WB], b.ap, row[:, half * WB:(half + 1) * WB], ALU.mult,
                    after=[A, row_ready])]

    def add_normed(self, x, junk, stats):
        nc, V = self.nc, self.V
        sums = split(stats[:, 0:4], 2, 2)
        V(nc.vector.tensor_tensor, stats[:, 4:6], sums[:, :, 0], sums[:, :, 1], ALU.add, after=[self.A])
        self.rstd(stats[:, 6:8], stats[:, 4:6], D, EPS_RMS, after=[V])
        return [V(nc.vector.scalar_tensor_tensor, x[:, t, :], junk[:, t * D:(t + 1) * D], stats[:, 6 + t:7 + t],
                  x[:, t, :], ALU.mult, ALU.add, after=[V]) for t in range(TT)]

    def wrapped_sin(self, out, angle, turns, work, quarter, after):
        nc, V, A = self.nc, self.V, self.A
        magic = 1.5 * 2.0 ** 23
        V(nc.vector.tensor_scalar, turns, angle, 1.0 / (2.0 * math.pi), 0.25 * quarter, ALU.mult, ALU.add, after=after)
        V(nc.vector.tensor_scalar, turns, turns, magic, None, ALU.add, after=[V])
        V(nc.vector.tensor_scalar, turns, turns, -magic, None, ALU.add, after=[V])
        c1, c2 = 6.28125, 0.0019350051879882812
        c3 = 2.0 * math.pi - c1 - c2
        src = angle
        for c in (c1, c2, c3):
            V(nc.vector.scalar_tensor_tensor, work, turns, -c, src, ALU.mult, ALU.add, after=[V])
            src = work
        if quarter:
            V(nc.vector.tensor_scalar, work, work, 0.5 * math.pi * quarter, None, ALU.add, after=[V])
        V(nc.vector.tensor_scalar, work, work, PI_IN, -PI_IN, ALU.min, ALU.max, after=[V])
        return A(nc.scalar.activation, out, work, ACT.Sin, after=[V])


PI_IN = 3.1415925


def pick(first, n):
    return slice(first, first + n) if isinstance(first, int) else bass.ds(first, n)


def seen_as(tiles, n):
    return lambda cut, part, k: split(cut.ap[part][:, 0:tiles * n], tiles, n)[:, k, :]


def split(ap, *dims):
    if len(dims) == 1:
        return ap
    names = "abcde"[:len(dims)]
    return ap.rearrange(f"p ({' '.join(names)}) -> p {' '.join(names)}", **dict(zip(names, dims)))


FILL_ORDER = [0, 1, 2, 3, 4, 5, 6, (0, 0), (0, 1), 7, 8, 9, (1, 0), (1, 1), 10, 11]
LAST_BRANCH = [(2, 0), (2, 1)]


def first_block(k, x):
    nc, T, V, A, G, SP = k.nc, k.T, k.V, k.A, k.G, k.SP
    dram, table, take = k.dram, k.table, k.take
    w_in = dram["w_in"].rearrange("l (k p) n -> p l k n", p=P)
    w_branch = dram["w_branch"].rearrange("l b (k p) n -> p l b k n", p=P)
    w_out = dram["w_out"].rearrange("l (k p) n -> p l k n", p=P)
    w_up = dram["w_up"].rearrange("l (k p) n -> p l k n", p=P)
    w_down = dram["w_down"].rearrange("l (k p) n -> p l k n", p=P)
    w_uq = dram["mla_w_uq"].rearrange("l (k p) n -> p l k n", p=P)
    w_ukv = dram["mla_w_ukv"].rearrange("l p n -> p l n")
    floor = k.top

    k.top = k.tables_at + k.dram["tables_all"].shape[1] + k.dram["tables_first"].shape[1]
    bias = take(N_BIAS, SCORE_W)
    assert k.top <= floor - TT * D
    k.top = floor
    cos, sin = take(TT, ROPE // 2), take(TT, ROPE // 2)
    cols = take(4)
    pre, post = take(D), take(D)
    hT = k.take_parts("hT", KT, S)
    flat_junk = take(TT * D)
    junk = split(flat_junk, 4, WB)
    stats = take(64)
    qkT = take(4, 4, S)
    v_at = k.top
    diff_v, moba_v, mla_v = take(TT, WB), take(TT, WB), take(TT, WB)
    qr, kr = take(TT, MLA_HEADS * ROPE), take(TT, P)
    qrT, krT = take(2, S), take(S)
    lam = take(4, 64)
    v_end = k.top
    qnT, knT = take(4, S), take(4, S)
    heads_out = split(pre, TT, WB)
    branchT = k.take_parts("branchT", 3 * 4, S)
    low_at = k.top
    low = take(TT, Q_RANK + KV_RANK + ROPE)
    lowT = k.take_parts("lowT", 3, S)
    low_end, k.top = k.top, low_at
    scores = [k.c.buf(take(SCORE_W)) for _ in range(4)]
    probsT = [k.c.buf(take(SCORE_W)) for _ in range(2)]
    k.top = max(k.top, low_end)
    gates = [take(2, S) for _ in range(4)]
    gates += [qkT[:, j // 2, 2 * (j % 2):2 * (j % 2) + 2, :] for j in range(4)]
    gates += gates[0:4]
    mixT = split(flat_junk, KT, S)
    k.top, last = v_at, k.top
    u = [take(2, S) for _ in range(2)]
    assert k.top <= v_end
    k.top = last
    hidden = [k.c.buf() for _ in range(2)]
    for j in range(2):
        hidden[j].ap = [part[:, 2 * j:2 * j + 2, :] for part in branchT]

    k.begin()
    rel = diff_v[:, 0, 0:N_BIAS]
    k.load_tables("first")
    V(nc.vector.memset, rel, 1.0)
    SP.dma(k.small_loaded, diff_v[0:BUCKETS, 0, 0:N_BIAS], dram["rel_bias"], after=[V])
    b = k.bank()
    pos = diff_v[:, 1, 0:TT].bitcast(INT32)
    SP.dma(k.small_loaded, pos, dram["positions"])
    T(nc.tensor.matmul, b.ap[0:N_BIAS, 0:REL_W], diff_v[0:BUCKETS + 1, 0, 0:N_BIAS],
      table("bucket")[0:BUCKETS + 1, :], start=True, stop=True, after=[k.small_loaded])
    V(nc.vector.tensor_copy, moba_v[0:N_BIAS, 0, 0:REL_W], b.ap[0:N_BIAS, 0:REL_W], after=[T])
    diag = dram["diagonals"]
    SP.dma(k.scratch_stored, diag[:, 0:REL_W], moba_v[0:N_BIAS, 0, 0:REL_W], after=[V])
    for h in range(N_BIAS):
        row = diag[h:h + 1, :]
        skewed = qkT.rearrange("p a b c -> p (a b c)")[:, h * SCORE_W:(h + 1) * SCORE_W]
        for at, first, n in ((0, 0, S), (S, P, P)):
            SP.dma(k.small_loaded, skewed[:, at:at + n], bass.AP(tensor=row.tensor, offset=row.offset + first, ap=[[1, P], [1, n]]),
                   after=[k.scratch_stored])
    for h in range(N_BIAS):
        skewed = qkT.rearrange("p a b c -> p (a b c)")[:, h * SCORE_W:(h + 1) * SCORE_W]
        b = k.bank()
        k.matmul(b.ap[:, 0:SCORE_W], table("flip"), skewed, True, True, after=[k.small_loaded, *b.free])
        b.free = [k.copy(A, bias[:, h, :], b.ap[:, 0:SCORE_W], after=[T])]
    angle = moba_v[:, 1, 0:TT * 16]
    posf = moba_v[:, 1, 64:64 + TT]
    V(nc.vector.tensor_copy, posf, pos, after=[k.small_loaded])
    for t in range(TT):
        V(nc.vector.tensor_scalar, angle[:, t * 16:(t + 1) * 16], table("inv_freq"), posf[:, t:t + 1], None,
          ALU.mult, after=[V])
    turns, work = moba_v[:, 1, 128:160], moba_v[:, 1, 160:192]
    k.wrapped_sin(sin.rearrange("p a b -> p (a b)"), angle, turns, work, 0, after=[V])
    k.wrapped_sin(cos.rearrange("p a b -> p (a b)"), angle, turns, work, 1, after=[V, A])

    def layer(l):
        at = lambda ap: ap[:, bass.ds(l, 1)]
        k.begin()
        cols_in = SP.dma(k.small_loaded, cols, at(dram["cols"])[:, 0, :])
        dl = dram["diff_lambda"][bass.ds(l, 1), :].partition_broadcast(P)
        SP.dma(k.small_loaded, lam.rearrange("p a b -> p (a b)"), dl[:, 0, :])
        broadcast = lambda name: dram[name][bass.ds(l, 1), :].partition_broadcast(P)[:, 0, :]
        pre_in = SP.dma(k.rows_loaded, pre, broadcast("norm_mix_pre"))
        pre_in = SP.dma(k.rows_loaded, post, broadcast("norm_mix_post"))
        width = Q_RANK + KV_RANK + ROPE
        wi, wb, wo, wu, wd = (at(w)[:, 0] for w in (w_in, w_branch, w_out, w_up, w_down))
        two = lambda first: [k.columns(wi, first), k.columns(wi, first + S)]
        k.plan(*two(0), *two(WB), *k.by_rows(wi, 2 * WB), *two(3 * WB), *two(4 * WB), *k.by_rows(wi, 5 * WB),
               *k.by_rows(wi, MLA_IN, width),
               lambda: k.fetch(((2, 768), at(w_uq)[:, 0])), lambda: k.fetch(((2 * WB,), at(w_ukv)[:, 0])),
               *(k.columns(wi, GATE_IN + f * S) if isinstance(f, int) else k.rows(wb[:, f[0]], 0, 4, f[1] * WB, WB)
                 for f in FILL_ORDER + LAST_BRANCH),
               *k.by_rows(wo, 0), *k.by_rows(wo, WB), k.columns(wu, 0))

        normed_T(k, x, hT, pre, [pre_in, k.small_loaded], flat_junk, stats)
        h_ready = [V.mark()]

        for n, column in ((0, 0), (1, WB), (None, 2 * WB), (2, 3 * WB), (3, 4 * WB), (None, 5 * WB)):
            if n is None:
                dst = diff_v if column == 2 * WB else moba_v
                for t, b, mark in k.token_major(hT, WB, ready=h_ready):
                    b.free = [k.copy((V, A)[t], dst[:, t, :], b.ap, after=[mark])]
            else:
                for m0 in (0, 2):
                    b, mark = k.two_tiles(hT, h_ready)
                    b.free = [k.copy(V if m0 else A, qkT[:, n, m0:m0 + 2, :], split(b.ap, 2, S), after=[mark])]
        for t, b, mark in k.token_major(hT, width, ready=h_ready):
            b.free = [k.copy((V, A)[t], low[:, t, :], b.ap[:, 0:width], after=[mark])]

        for t in range(TT):
            A(nc.scalar.activation, junk[:, 0, 0:Q_RANK], low[:, t, 0:Q_RANK], ACT.Square,
              accum_out=stats[:, 8 + t:9 + t], after=[V, A])
            A(nc.scalar.activation, junk[:, 0, 0:KV_RANK], low[:, t, Q_RANK:Q_RANK + KV_RANK], ACT.Square,
              accum_out=stats[:, 10 + t:11 + t], after=[A])
        k.rstd(stats[:, 12:14], stats[:, 8:10], Q_RANK, EPS_RMS, after=[A])
        k.rstd(stats[:, 14:16], stats[:, 10:12], KV_RANK, EPS_RMS, after=[A])
        for t in range(TT):
            V(nc.vector.tensor_scalar, low[:, t, 0:Q_RANK], low[:, t, 0:Q_RANK], stats[:, 12 + t:13 + t], None,
              ALU.mult, after=[V])
            V(nc.vector.tensor_scalar, low[:, t, Q_RANK:Q_RANK + KV_RANK], low[:, t, Q_RANK:Q_RANK + KV_RANK],
              stats[:, 14 + t:15 + t], None, ALU.mult, after=[V])
        for j in range(3):
            b = k.bank()
            for t in range(TT):
                k.transpose(b.ap[:, t * P:(t + 1) * P], low[:, t, j * P:(j + 1) * P], after=[*b.free, V] if t == 0 else ())
            k.cut_in_two(b.ap[:, 0:S], [part[:, j, :] for part in lowT], [T], scale=cols[:, 1 + j:2 + j])
            b.free = [V.mark()]
        low_ready = [V.mark()]

        cut = k.next()
        uq = [split(part[:, 0:1536], 2, 768) for part in cut.ap]
        for m0, b, mark in k.feature_major(lambda part, kk, m: uq[part][:, kk, m * P:(m + 1) * P],
                                           [*cut.ready, *low_ready], lowT, 4, kt=2):
            b.free = [k.copy(V, qnT[:, m0:m0 + 2, :], split(b.ap, 2, S), after=[mark])]
        for t in range(TT):
            b = k.bank()
            for kk in range(2):
                k.product(b.ap[:, 0:S], [part[:, kk, t * P:(t + 1) * P] for part in lowT], [w[:, kk, WB:] for w in uq],
                          kk == 0, kk == 1, after=b.free if kk == 0 else ())
            b.free = [k.copy(V, qr[:, t, :], b.ap[:, 0:S], after=[T])]
        cut.free = [T.mark()]
        cut = k.next()
        c_kv = [part[:, 2:3, :] for part in lowT]
        for m0, b, mark in k.feature_major(lambda part, kk, m: cut.ap[part][:, m * P:(m + 1) * P], cut.ready, c_kv, 4, kt=1):
            b.free = [k.copy(A, knT[:, m0:m0 + 2, :], split(b.ap, 2, S), after=[mark])]
        for t in range(TT):
            b = k.bank()
            k.product(b.ap, [part[:, 0, t * P:(t + 1) * P] for part in c_kv], [part[:, WB:2 * WB] for part in cut.ap],
                      True, True, after=b.free)
            b.free = [k.copy(A, mla_v[:, t, :], b.ap, after=[T])]
        cut.free = [T.mark()]

        half = ROPE // 2

        def rotate(src, dst, heads):
            tmp = split(junk[:, 2, 0:TT * heads * half], TT, heads, half)
            c = cos.unsqueeze(2).to_broadcast([P, TT, heads, half])
            s = sin.unsqueeze(2).to_broadcast([P, TT, heads, half])
            x1, x2 = src[:, :, :, 0:half], src[:, :, :, half:]
            for t in range(TT):
                for a, bb, op, o in ((x1, x2, ALU.subtract, dst[:, :, :, 0:half]), (x2, x1, ALU.add, dst[:, :, :, half:])):
                    V(nc.vector.tensor_tensor, tmp[:, t], bb[:, t], s[:, t], ALU.mult, after=[V])
                    V(nc.vector.tensor_tensor, o[:, t], a[:, t], c[:, t], ALU.mult, after=[V])
                    V(nc.vector.tensor_tensor, o[:, t], o[:, t], tmp[:, t], op, after=[V])

        rot = split(junk[:, 0, :], TT, MLA_HEADS, ROPE)
        rotate(qr.rearrange("p t (h j) -> p t h j", h=MLA_HEADS), rot, MLA_HEADS)
        pe = low[:, :, Q_RANK + KV_RANK:].unsqueeze(2).to_broadcast([P, TT, 4, ROPE])
        rotate(pe, kr.rearrange("p t (h j) -> p t h j", h=4), 4)
        k.transposes(rot.rearrange("p t h j -> p t (h j)"), qrT, 2, after=[V])
        k.transposes(kr, krT.unsqueeze(1), 1, after=[V])
        attention_ready = [V.mark(), A.mark(), T.mark()]

        V(nc.vector.tensor_tensor, junk[:, 1, 0:128].rearrange("p (a b) -> p a b", a=2), lam[:, 0::2, :],
          lam[:, 1::2, :], ALU.mult, after=[k.small_loaded, V])
        V(nc.vector.tensor_reduce, stats[:, 16:18], split(junk[:, 1, 0:128], 2, 64), AX.X, ALU.add, after=[V])
        A(nc.scalar.activation, stats[:, 18:20], stats[:, 16:18], ACT.Exp, after=[V])
        V(nc.vector.tensor_tensor, stats[:, 20:21], stats[:, 18:19], stats[:, 19:20], ALU.subtract, after=[A])
        init = split(table("lam"), DEPTH, 2)[:, bass.ds(l, 1), :]
        V(nc.vector.tensor_tensor, stats[:, 21:22], stats[:, 20:21], init[:, 0, 0:1], ALU.add, after=[V])
        V(nc.vector.tensor_scalar, stats[:, 22:23], stats[:, 21:22], -1.0, None, ALU.mult, after=[V])
        V(nc.vector.tensor_tensor, stats[:, 23:24], cols[:, 0:1], init[:, 0, 1:2], ALU.mult, after=[V])
        minus_lam, subln = stats[:, 22:23], stats[:, 23:24]

        look_gate, look_branch = seen_as(KT, S), seen_as(4, WB)
        held = k.banks[6:8]

        def gate_piece(n):
            cut, b = k.next(), held[n % 2]
            for j in range(2 * KT):
                m, kk = j // KT, j % KT
                k.product(b.ap[:, m * S:(m + 1) * S], [look_gate(cut, part, kk)[:, m * P:(m + 1) * P] for part in (0, 1)],
                          [part[:, kk, :] for part in hT], kk == 0, kk == KT - 1,
                          after=[*b.free, *cut.ready] if kk == 0 else (), inc=True if kk == KT - 1 else False)
                if j in (5, 10):
                    yield
            cut.free = [T.mark()]
            A(nc.scalar.activation, gates[n], split(b.ap, 2, S), ACT.Tanh, scale=0.5, after=[T, V, G])
            b.free = [A.mark()]
            G(nc.gpsimd.tensor_scalar, gates[n], gates[n], 0.5, 0.5, ALU.mult, ALU.add, after=[A])
            yield

        def branch_piece(g, half):
            cut = k.next()
            for m0 in (0, 2):
                b = held[m0 // 2]
                for j in range(8):
                    m, kk = j // 4, j % 4
                    k.product(b.ap[:, m * S:(m + 1) * S],
                              [look_branch(cut, part, kk)[:, (m0 + m) * P:(m0 + m + 1) * P] for part in (0, 1)],
                              [part[:, 4 * g + kk, :] for part in branchT], kk == 0, kk == 3,
                              after=[*b.free, *cut.ready, *turned_ready[g]] if kk == 0 else (), inc=kk == 3)
                    if (m0, j) in ((0, 4), (2, 1)):
                        yield
                tile = 4 * half + m0
                gate, mix = gates[4 * g + tile // 2], mixT[:, tile:tile + 2, :]
                V(nc.vector.tensor_tensor, mix if g == 0 else gate, split(b.ap, 2, S), gate, ALU.mult, after=[T, V, G])
                b.free = [V.mark()]
                if g:
                    G(nc.gpsimd.tensor_tensor, mix, mix, gate, ALU.add, after=[V])
                if g == N_BRANCH - 1:
                    k.cut_in_two(mix, [part[:, tile:tile + 2, :] for part in hT], [G])
            cut.free = [T.mark()]
            yield

        def filler():
            for step in FILL_ORDER:
                yield from gate_piece(step) if isinstance(step, int) else branch_piece(*step)

        filling = [None]

        def fill():
            if filling[0] is not None:
                next(filling[0], None)

        turned_ready = {}

        def score_map(n, pairs, add, scale):
            b, s = k.bank(), scores[n % 4]
            for at_, keys, q0 in ((0, S, P), (S, P, 0)):
                for j, (kT, qT) in enumerate(pairs):
                    last = k.matmul(b.ap[:, at_:at_ + keys], qT[:, q0:q0 + P], kT[:, 0:keys],
                                    start=j == 0, stop=j == len(pairs) - 1, after=[*b.free, *attention_ready] if at_ + j == 0 else ())
            m = V(nc.vector.scalar_tensor_tensor, s.ap, b.ap[:, 0:SCORE_W], scale, add, ALU.mult, ALU.add,
                  after=[last, *s.free])
            b.free = [m]
            st = stats[:, 24 + 6 * (n % 4):30 + 6 * (n % 4)]
            V(nc.vector.tensor_reduce, st[:, 0:1], s.ap[:, 0:S], AX.X, ALU.max, negate=True, after=[m])
            m = V(nc.vector.tensor_reduce, st[:, 1:2], s.ap[:, S:], AX.X, ALU.max, negate=True, after=[m])
            A(nc.scalar.activation, s.ap[:, 0:S], s.ap[:, 0:S], ACT.Exp, bias=st[:, 0:1], accum_out=st[:, 2:3], after=[m])
            m = A(nc.scalar.activation, s.ap[:, S:], s.ap[:, S:], ACT.Exp, bias=st[:, 1:2], accum_out=st[:, 3:4])
            V(nc.vector.reciprocal, st[:, 4:6], st[:, 2:4], after=[m])
            ready = V.mark()
            fill()
            return s, st, ready

        def weighted(n, s, ready, v, width, out, sums, sums_ready):
            b, pt = k.bank(), probsT[n % 2]
            for j in range(3):
                k.transpose(b.ap[:, j * P:(j + 1) * P], s.ap[:, j * P:(j + 1) * P],
                            after=[*b.free, *ready] if j == 0 else ())
            s.free = [T.mark()]
            m = k.copy(A, pt.ap, b.ap[:, 0:SCORE_W], after=[T, *pt.free])
            b.free = [m]
            fill()
            b = k.bank()
            k.matmul(b.ap[:, 0:width], pt.ap[:, 0:P], v[:, 0, :], start=True, stop=False, after=[m, *b.free])
            k.matmul(b.ap[:, 0:width], pt.ap[:, P:S], v[:, 1, :], start=False, stop=True)
            k.matmul(b.ap[:, width:2 * width], pt.ap[:, S:], v[:, 0, :], start=True, stop=True)
            pt.free = [T.mark()]
            for t, at_, r in ((1, 0, 0), (0, width, 1)):
                src = b.ap[:, at_:at_ + width]
                if sums is None:
                    V(nc.vector.tensor_copy, out[:, t, :], src, after=[T])
                else:
                    V(nc.vector.tensor_scalar, out[:, t, :], src, sums[:, r:r + 1], None, ALU.mult, after=[T, sums_ready])
            b.free = [V.mark()]
            fill()

        def differential(h):
            out = []
            for j in range(2):
                rows = slice(64 * j, 64 * j + 64)
                out.append(score_map(2 * h + j, [(qkT[rows, 1, h, :], qkT[rows, 0, h, :])], bias[:, h, :], 64 ** -0.5))
            (s1, st1, _), (s2, st2, _) = out
            V(nc.vector.tensor_scalar, st2[:, 4:6], st2[:, 4:6], minus_lam, None, ALU.mult, after=[V])
            for at_, keys, r in ((0, S, 4), (S, P, 5)):
                cut = slice(at_, at_ + keys)
                V(nc.vector.tensor_scalar, s1.ap[:, cut], s1.ap[:, cut], st1[:, r:r + 1], None, ALU.mult, after=[V])
                V(nc.vector.scalar_tensor_tensor, s1.ap[:, cut], s2.ap[:, cut], st2[:, r:r + 1], s1.ap[:, cut],
                  ALU.mult, ALU.add, after=[V])
            s2.free = [V.mark()]
            return s1, None, V.mark(), diff_v[:, :, h * P:(h + 1) * P], P

        def moba(h):
            s, st, m = score_map(8 + h, [(qkT[:, 3, h, :], qkT[:, 2, h, :])], bias[:, DIFF_HEADS + h, :], P ** -0.5)
            return s, st[:, 4:6], m, moba_v[:, :, h * P:(h + 1) * P], P

        def latent(h):
            rows = slice(64 * (h % 2), 64 * (h % 2) + 64)
            rot_rows = slice(32 * (h % 4), 32 * (h % 4) + 32)
            s, st, m = score_map(12 + h, [(knT[rows, h // 2, :], qnT[rows, h // 2, :]),
                                          (krT[rot_rows, :], qrT[rot_rows, h // 4, :])],
                                 table("causal"), (NOPE + ROPE) ** -0.5)
            return s, st[:, 4:6], m, mla_v[:, :, h * VDIM:(h + 1) * VDIM], VDIM

        jobs = [(0, differential, h) for h in range(DIFF_HEADS)]
        jobs += [(1, moba, h) for h in range(MOBA_HEADS)] + [(2, latent, h) for h in range(MLA_HEADS)]
        waiting = []
        turned = [None]

        def finish_branch(g):
            if g == 0:
                sq = flat_junk[:, 0:TT * WB]
                ho = heads_out.rearrange("p t c -> p (t c)")
                V(nc.vector.tensor_tensor, sq, ho, ho, ALU.mult, after=[V])
                V(nc.vector.tensor_reduce, stats[:, 48:56], split(sq, 8, P), AX.X, ALU.add, after=[V])
                k.rstd(stats[:, 56:64], stats[:, 48:56], P, EPS_RMS, after=[V])
                V(nc.vector.tensor_tensor, split(ho, 8, P), split(ho, 8, P),
                  stats[:, 56:64].unsqueeze(2).to_broadcast([P, 8, P]), ALU.mult, after=[V])
            for j in range(4):
                b = k.bank()
                for t in range(TT):
                    k.transpose(b.ap[:, t * P:(t + 1) * P], heads_out[:, t, j * P:(j + 1) * P],
                                after=[*b.free, V] if t == 0 else ())
                k.cut_in_two(b.ap[:, 0:S], [part[:, 4 * g + j, :] for part in branchT], [T], scale=subln if g == 0 else None)
                b.free = [V.mark()]
            turned[0] = T.mark()
            turned_ready[g] = [V.mark()]

        def finish_head():
            n, g, h, s, sums, ready, v, width = waiting.pop(0)
            if h == 0 and turned[0] is not None:
                V.wait([turned[0]])
            weighted(n, s, [ready, A], v, width, heads_out[:, :, h * width:(h + 1) * width], sums, ready)
            if h == (DIFF_HEADS, MOBA_HEADS, MLA_HEADS)[g] - 1:
                finish_branch(g)

        k.rotating = 6
        filling[0] = filler()
        for n, (g, job, h) in enumerate(jobs):
            s, sums, ready, v, width_v = job(h)
            waiting.append((n, g, h, s, sums, ready, v, width_v))
            if len(waiting) > 1:
                finish_head()
        finish_head()
        for _ in filling[0]:
            pass
        for half in range(2):
            for _ in branch_piece(N_BRANCH - 1, half):
                pass
        k.rotating = 8

        for half in range(2):
            for t, b, mark in k.token_major(hT, WB, ready=[V.mark()]):
                k.weigh(b, mark, t, half, post, k.rows_loaded, flat_junk, stats)
        pre_in = SP.dma(k.rows_loaded, pre, broadcast("norm_mlp_pre"), after=[V, T])
        post_in = SP.dma(k.rows_loaded, post, broadcast("norm_mlp_post"))
        k.add_normed(x, flat_junk, stats)

        normed_T(k, x, hT, pre, [post_in], flat_junk, stats)
        h_ready = [V.mark()]
        acc = [k.bank() for _ in range(4)]
        zeros = flat_junk
        V(nc.vector.memset, zeros[:, 0:P + WB], 0.0, after=[T])
        for b in acc:
            k.matmul(b.ap, zeros[:, 0:P], zeros[:, P:P + WB], start=True, stop=False, inc=True, after=[V, *b.free])
        spare = [k.banks[(k.c.bank + j) % 8] for j in range(4)]

        def mlp(i, more):
            ahead = [k.columns(wu, i * WB + WB)] if more else []
            k.plan(k.columns(wu, i * WB + S), k.rows(wd, i * 4, 2, 0, D), k.rows(wd, i * 4 + 2, 2, 0, D), *ahead)
            for j in range(2):
                cut, b, h = k.next(), spare[j], hidden[j]
                look = seen_as(KT, S)
                for m in range(2):
                    for kk in range(KT):
                        k.product(b.ap[:, m * S:(m + 1) * S], [look(cut, part, kk)[:, m * P:(m + 1) * P] for part in (0, 1)],
                                  [part[:, kk, :] for part in hT], kk == 0, kk == KT - 1,
                                  after=[*b.free, *cut.ready, *h_ready] if kk == 0 else ())
                cut.free = [T.mark()]
                A(nc.scalar.activation, u[j], split(b.ap, 2, S), ACT.Relu, after=[T, V])
                b.free = [A.mark()]
                V(nc.vector.tensor_tensor, u[j], u[j], u[j], ALU.mult, after=[A])
                k.cut_in_two(u[j], h.ap, [V, *h.free])
                h.ready = [V.mark()]
            for j in range(2):
                cut, h = k.next(), hidden[j]
                look = seen_as(2, D)
                for t in range(TT):
                    for half in range(2):
                        for kk in range(2):
                            for a, b in ((0, 0), (0, 1), (1, 0)):
                                T(nc.tensor.matmul, acc[2 * t + half].ap, h.ap[a][:, kk, t * P:(t + 1) * P],
                                  look(cut, b, kk)[:, half * WB:(half + 1) * WB], start=False, stop=False,
                                  skip_group_check=True, inc=kk == 1 and a == 1,
                                  after=[*cut.ready, *h.ready] if t + half + kk + a + b == 0 else ())
                cut.free = [T.mark()]
                h.free = [T.mark()]

        turns = D_FF // WB
        k.c.loop(turns - 1, lambda i: mlp(i, True))
        mlp(turns - 1, False)
        for b in acc:
            k.matmul(b.ap, zeros[:, 0:P], zeros[:, P:P + WB], start=False, stop=True)
        done = T.mark()
        for t in range(TT):
            for half in range(2):
                k.weigh(acc[2 * t + half], done, t, half, post, k.rows_loaded, flat_junk, stats)
        k.add_normed(x, flat_junk, stats)

    with nc.Fori(0, DEPTH) as l:
        layer(l)
    k.top = floor


def normed_T(k, src, dstT, weight, weight_ready, normed, stats):
    nc, V, A = k.nc, k.V, k.A
    normed = split(normed, TT, D)
    A(nc.scalar.activation, normed[:, 0, :], src[:, 0, :], ACT.Square, accum_out=stats[:, 0:1], after=[V, k.T])
    V(nc.vector.scalar_tensor_tensor, normed[:, 1, :], src[:, 1, :], 1.0, src[:, 1, :], ALU.mult, ALU.mult,
      accum_out=stats[:, 1:2], after=[V, k.T])
    k.rstd(stats[:, 2:4], stats[:, 0:2], D, EPS_RMS, after=[A, V])
    marks = [[V(nc.vector.scalar_tensor_tensor, normed[:, t, :], src[:, t, :], stats[:, 2 + t:3 + t], weight,
                ALU.mult, ALU.mult, after=[V, *weight_ready])] for t in range(TT)]
    k.transposes_cut(normed, dstT, KT, marks)


def embedding(k, i, after=()):
    nc, V, A = k.nc, k.V, k.A
    pT_in, e, stats = k.take(TT, S), k.take(TT, D), k.take(8)
    pT = k.take_parts(f"pT{i}", TT, S)
    k.SP.dma(k.rows_loaded, pT_in, k.dram["pT"][i].rearrange("(a p) s -> p a s", p=P), after=after)
    k.cut_in_two(pT_in, pT, [k.rows_loaded])
    for hf in range(2):
        cut = slice(hf * WB, (hf + 1) * WB)
        for t, b, mark in k.token_major(pT, WB, tiles=(2,), ready=[V.mark()]):
            A(nc.scalar.activation, e[:, t, cut], b.ap, ACT.Square, accum_out=stats[:, 2 * t + hf:2 * t + hf + 1], after=[mark])
            A(nc.scalar.activation, e[:, t, cut], b.ap, ACT.Copy, after=[A])
            b.free = [A.mark()]
    sums = split(stats[:, 0:4], 2, 2)
    V(nc.vector.tensor_tensor, stats[:, 4:6], sums[:, :, 0], sums[:, :, 1], ALU.add, after=[A])
    k.rstd(stats[:, 6:8], stats[:, 4:6], D, EPS_RMS, after=[V])
    return e, stats[:, 6:8]


def close_layer(k, i, x, mixed, hT, free_at):
    nc, T, V, A, G, SP, dram = k.nc, k.T, k.V, k.A, k.G, k.SP, k.dram
    floor, k.top = k.top, free_at
    rows = k.take(3, D)
    gate = k.take(TT, D)
    stats = k.take(32)
    ready = [V.mark(), G.mark(), A.mark(), T.mark()]
    for j, name in enumerate(("ln_g", "ln_b", "ple_norm")):
        SP.dma(k.rows_loaded, rows[:, j, :], dram[name][i:i + 1, :].partition_broadcast(P)[:, 0, :], after=ready)
    e, rstd = embedding(k, i, ready)
    k.top = floor
    for t in range(TT):
        V(nc.vector.scalar_tensor_tensor, e[:, t, :], e[:, t, :], rstd[:, t:t + 1], rows[:, 2, :],
          ALU.mult, ALU.mult, after=[V, A, k.rows_loaded])

    k.transposes_cut(mixed, hT, KT, [ready] * TT)
    mix_ready = [V.mark()]
    for hf in range(2):
        cut = slice(hf * WB, (hf + 1) * WB)
        for t, b, mark in k.token_major(hT, WB, ready=mix_ready):
            V(nc.vector.scalar_tensor_tensor, x[:, t, cut], x[:, t, cut], ALPHA, b.ap, ALU.mult, ALU.add,
              accum_out=stats[:, 8 + 2 * t + hf:9 + 2 * t + hf], after=[mark, V])
            b.free = [V.mark()]
    sums = split(stats[:, 8:12], 2, 2)
    V(nc.vector.tensor_tensor, stats[:, 12:14], sums[:, :, 0], sums[:, :, 1], ALU.add, after=[V])
    V(nc.vector.tensor_scalar, stats[:, 14:16], stats[:, 12:14], -1.0 / D, None, ALU.mult, after=[V])
    for t in range(TT):
        A(nc.scalar.activation, gate[:, t, :], x[:, t, :], ACT.Square, bias=stats[:, 14 + t:15 + t],
          accum_out=stats[:, 16 + t:17 + t], after=[V])
    k.rstd(stats[:, 18:20], stats[:, 16:18], D, EPS_LN, after=[A])
    marks = []
    for t in range(TT):
        xt = x[:, t, :]
        V(nc.vector.tensor_scalar, xt, xt, stats[:, 14 + t:15 + t], stats[:, 18 + t:19 + t], ALU.add, ALU.mult, after=[V])
        V(nc.vector.tensor_tensor, xt, xt, rows[:, 0, :], ALU.mult, after=[V])
        marks.append([V(nc.vector.tensor_tensor, xt, xt, rows[:, 1, :], ALU.add, after=[V])])

    k.transposes_cut(x, hT, KT, marks)
    x_ready = [V.mark()]
    for hf in range(2):
        cut = slice(hf * WB, (hf + 1) * WB)
        for t, b, mark in k.token_major(hT, WB, ready=x_ready):
            m = A(nc.scalar.activation, gate[:, t, cut], b.ap, ACT.Sigmoid, after=[mark])
            b.free = [m]
            m = V(nc.vector.tensor_tensor, gate[:, t, cut], gate[:, t, cut], e[:, t, cut], ALU.mult, after=[m, V])
            V(nc.vector.tensor_tensor, x[:, t, cut], x[:, t, cut], gate[:, t, cut], ALU.add, after=[m])


def closing_pieces(k, i):
    rearranged = [k.dram[name].rearrange("l (k p) n -> p l k n", p=P)[:, i] for name in ("ple_w", "w_out_2", "ple_gate")]
    ple_w, w_out, ple_gate = rearranged
    return [k.rows(ple_w, 0, 2, 0, WB), k.rows(ple_w, 0, 2, WB, WB), *k.by_rows(w_out, 0), *k.by_rows(w_out, WB),
            *k.by_rows(ple_gate, 0), *k.by_rows(ple_gate, WB)]


class Filler:

    def __init__(self, k, *steps):
        self.k, self.steps = k, chain(*steps)
        k.rotating = 6

    def __call__(self, n=1):
        for _ in range(n):
            next(self.steps, None)

    def finish(self):
        for _ in self.steps:
            pass
        self.k.rotating = 8


def chain(*steps):
    for s in steps:
        yield from s


def gate_steps(k, xT, ready, dst, free):
    held, look = k.banks[6:8], seen_as(KT // 2, WB)
    for half in range(2):
        cut = k.next()
        for t in range(TT):
            for kk in range(KT // 2):
                k.product(held[t].ap, [x[:, half * KT // 2 + kk, t * P:(t + 1) * P] for x in xT],
                          [look(cut, part, kk) for part in (0, 1)], half + kk == 0, half == 1 and kk == KT // 2 - 1,
                          after=[*held[t].free, *cut.ready, *ready] if kk == 0 else (), inc=kk == KT // 2 - 1)
            if t == TT - 1:
                cut.free = [k.T.mark()]
            yield
    for t in range(TT):
        held[t].free = [k.A(k.nc.scalar.activation, dst[:, t, :], held[t].ap, ACT.Silu, after=[k.T, *free()])]


def padded_copy(k, dst, bank, tiles, pad, after):
    return k.copy(k.A, dst[:, 0:tiles, pad:pad + S], split(bank.ap, 2, S)[:, 0:tiles, :], after=after)


class Triangles:

    def __init__(self, k):
        self.k, self.n, self.fill = k, 8, lambda: None
        self.X, self.XT = k.take(8, P), k.take(8, P)
        self.NX = k.take(8, P)
        self.masked = k.take(8, P)

    def invert(self, NT, d, ready):
        k = self.k
        nc, T, V, A, G = k.nc, k.T, k.V, k.A, k.G
        X, XT, NX, masked = self.X, self.XT, self.NX, self.masked
        at, _ = k.table_at[f"level{d}_0"]
        levels = split(k.tables[:, at:at + LEVELS * P], LEVELS, P)
        self.NT, self.levels = NT, levels
        ident8 = k.table("ident").unsqueeze(1).to_broadcast([P, 8, P])
        joined = V(nc.vector.tensor_tensor, masked, NT, levels[:, 0:1].to_broadcast([P, 8, P]), ALU.mult, after=[*ready, T])
        V(nc.vector.tensor_tensor, XT, ident8, masked, ALU.subtract, after=[V])
        for g in range(2):
            b = k.bank()
            for j in range(4):
                k.transpose(b.ap[:, j * P:(j + 1) * P], masked[:, 4 * g + j, :], after=[*b.free, joined] if j == 0 else (), inc=j == 3)
            V(nc.vector.tensor_tensor, X[:, 4 * g:4 * g + 4], ident8[:, 0:4], split(b.ap, 4, P), ALU.subtract, after=[T])
            b.free = [V.mark()]
            self.fill()
        mask_buf = k.c.buf()
        mask_buf.free = [T.mark(), V.mark()]
        banks = [k.bank() for _ in range(6)]
        x_buf, xt_buf = [k.c.buf() for _ in range(2)], [k.c.buf() for _ in range(2)]
        for b in (*x_buf, *xt_buf):
            b.ready = [V.mark()]

        def level(i):
            G(nc.gpsimd.tensor_tensor, masked, NT, levels[:, bass.ds(i + 1, 1)].to_broadcast([P, 8, P]), ALU.mult,
              after=mask_buf.free)
            nx_ready = []
            for g in range(2):
                b = banks[g]
                for j in range(4):
                    k.matmul(b.ap[:, j * P:(j + 1) * P], masked[:, 4 * g + j, :], X[:, 4 * g + j, :], True, True,
                             after=[*b.free, G, *x_buf[g].ready] if j == 0 else (), inc=j == 3)
                nx_ready.append(k.copy(A, NX[:, 4 * g:4 * g + 4], split(b.ap, 4, P), after=[T]))
                b.free = [A.mark()]
            mask_buf.free = [T.mark()]
            for g in range(2):
                for dst, b, left, right in ((X, banks[2 + g], XT, NX), (XT, banks[4 + g], NX, XT)):
                    for j in range(4):
                        u = 4 * g + j
                        k.matmul(b.ap[:, j * P:(j + 1) * P], left[:, u, :], right[:, u, :], True, True,
                                 after=[*b.free, nx_ready[g], *xt_buf[g].ready] if j == 0 else (), inc=j == 3)
                    if dst is X:
                        x_made = T.mark()
                for dst, buf, b, made in ((X, x_buf[g], banks[2 + g], x_made), (XT, xt_buf[g], banks[4 + g], T.mark())):
                    part = dst[:, 4 * g:4 * g + 4]
                    V(nc.vector.tensor_tensor, part, part, split(b.ap, 4, P), ALU.subtract, after=[made])
                    b.free = buf.ready = [V.mark()]

        k.c.loop(LEVELS - 2, level)
        V(nc.vector.tensor_tensor, masked, NT, levels[:, LEVELS - 1:].to_broadcast([P, 8, P]), ALU.mult, after=[T])
        self.ready = [V.mark()]

    def solve(self, which, rhs, U, work, width, ready):
        k = self.k
        nc, T, V, A = k.nc, k.T, k.V, k.A
        n = len(which)

        def products(mats, right, after):
            b = k.bank()
            for j, u in enumerate(which):
                k.matmul(b.ap[:, j * width:(j + 1) * width], mats[:, u, :], right[:, j, :], True, True,
                         after=[*b.free, *after] if j == 0 else (), inc=j == n - 1)
            return b, split(b.ap[:, 0:n * width], n, width)

        b, out = products(self.XT, rhs, [*ready, *self.ready])
        b.free = [k.copy(A, U, out, after=[T])]
        self.fill()
        b, out = products(self.masked, U, [A])
        b.free = [k.copy(A, work, out, after=[T])]
        self.fill()
        b, out = products(self.XT, work, [A])
        V(nc.vector.tensor_tensor, U, U, out, ALU.subtract, after=[T, A])
        b.free = [V.mark()]
        self.fill()


def even_layer(k, x):
    nc, T, V, A, G, SP = k.nc, k.T, k.V, k.A, k.G, k.SP
    dram, table, take = k.dram, k.table, k.take
    k.begin()
    floor = k.top
    w_in = dram["even_w_in"].rearrange("(k p) n -> p k n", p=P)
    mixed = take(TT, D)
    k.top = m_at = -(-k.top // 8) * 8
    hT = k.take_parts("hT_even", KT, S)
    assert k.top == m_at + RK_HEADS * 4 * P
    free_at = k.top
    raw_at = k.top
    raw = [k.c.buf(take(2, S + 4)) for _ in range(2)]
    cols = take(112)
    small = take(16 + 128 + 2 * WB)
    stats = take(160)
    v_tok = take(TT, WB)
    lora = take(2, WB)
    tri = Triangles(k)
    U, work, rhs = take(WB), take(WB), take(WB)
    state = take(WB)
    body_at = k.top
    cw = split(cols[:, 0:60], DN_CONV, 12)
    mu = split(cols[:, 60:88], 2, 14)
    w0, a0 = split(cols[:, 88:96], 2, 4), cols[:, 96:100]
    k_k, k_a, r_k = cols[:, 100:104], cols[:, 104:108], cols[:, 108:112]

    k.load_tables("even")
    SP.dma(k.small_loaded, cols, dram["even_cols"])
    at = 0
    for name, n in (("dn_a_log", 8), ("dn_dt_bias", 8), ("dn_norm", P), ("rk_ln_w", WB), ("rk_ln_b", WB)):
        SP.dma(k.small_loaded, small[:, at:at + n], dram[name].partition_broadcast(P)[:, 0, :])
        at += n
    SP.dma(k.small_loaded, lora[:, 0, :], dram["rk_w2"])
    SP.dma(k.small_loaded, lora[0:LORA, 1, :], dram["rk_a2"])
    a_log, dt_bias, dn_norm = small[:, 0:8], small[:, 8:16], small[:, 16:16 + P]
    ln_w, ln_b = small[:, 144:144 + WB], small[:, 144 + WB:144 + 2 * WB]
    for r in raw:
        V(nc.vector.memset, r.ap.rearrange("p a b -> p (a b)"), 0.0)
    two = lambda first: [k.columns(w_in, first), k.columns(w_in, first + S)]
    k.plan(*two(0), *two(WB), *two(2 * WB), k.columns(w_in, AB_IN, DN_AB), *k.by_rows(w_in, DN_GATE_IN),
           *two(RK_IN), *two(RK_IN + WB), *two(RK_IN + 2 * WB), k.columns(w_in, RK_IN + 3 * WB),
           *k.by_rows(w_in, RK_GATE_IN), *closing_pieces(k, 0))
    k.transposes_cut(x, hT, KT, [[]] * TT)
    h_ready = [V.mark()]

    qkvT = take(3, DN_HEADS, S)
    k_tok = take(TT, WB)
    g_beta = take(2, TT, 8)
    AT = take(8, P)
    NT = take(8, P)
    decay = take(8, P)
    silu_dn = take(TT, WB)
    dn_cols = take(64)
    o_dn = mixed[:, :, 0:WB]

    small_ready = k.small_loaded.mark()
    for part in range(3):
        for m0 in (0, 2):
            b, mark = k.two_tiles(hT, h_ready)
            r = raw[m0 // 2]
            padded_copy(k, r.ap, b, 2, 2, after=[mark, V, *r.free])
            b.free = [A.mark()]
            for j in range(2):
                f = 4 * part + m0 + j
                y = qkvT[:, part, m0 + j, :]
                m = V(nc.vector.tensor_scalar, y, r.ap[:, j, 0:S], cw[:, 0, f:f + 1], None, ALU.mult, after=[A, small_ready])
                for tap in range(1, DN_CONV):
                    m = V(nc.vector.scalar_tensor_tensor, y, r.ap[:, j, tap:tap + S], cw[:, tap, f:f + 1], y,
                          ALU.mult, ALU.add, after=[m])
            r.free = [m]
            A(nc.scalar.activation, qkvT[:, part, m0:m0 + 2, :], qkvT[:, part, m0:m0 + 2, :], ACT.Silu, after=[m])

    rk_words = 18 * WB + 32
    k.top = body_at + rk_words
    rkvT = take(3, 4, S)
    loraT = take(2, S)
    silu_rk = split(k.words_at(raw_at, TT * WB), TT, WB)
    mu_c = stats[:, 32:46]
    V(nc.vector.tensor_tensor, mu_c, mu[:, 0, :], mu[:, 1, :], ALU.add, after=[small_ready])
    V(nc.vector.tensor_scalar, mu_c, mu_c, -1.0, 1.0, ALU.mult, ALU.add, after=[V])

    def shifted_steps():
        look = seen_as(KT, S)
        for n in range(7):
            part, m0 = n // 2, 2 * (n % 2)
            cut, b, r = k.next(), k.banks[6 + n % 2], raw[n % 2]
            for j in range(2 * KT):
                m, kk = j // KT, j % KT
                k.product(b.ap[:, m * S:(m + 1) * S], [look(cut, q, kk)[:, m * P:(m + 1) * P] for q in (0, 1)],
                          [x[:, kk, :] for x in hT], kk == 0, kk == KT - 1,
                          after=[*b.free, *cut.ready] if kk == 0 else (), inc=kk == KT - 1)
                if j in (5, 10):
                    yield
            cut.free = [T.mark()]
            padded_copy(k, r.ap, b, 2, 2, after=[T, V, *r.free])
            b.free = [A.mark()]
            for j in range(2):
                rows = P if part < 3 or j == 0 else LORA
                f = 4 * part + m0 + j
                y = (rkvT[:, part, m0 + j, :] if part < 3 else loraT[:, j, :])[0:rows, :]
                rr = r.ap[0:rows, j, :]
                m = V(nc.vector.tensor_scalar, y, rr[:, 2:2 + S], mu_c[0:rows, f:f + 1], None, ALU.mult, after=[A, V])
                m = V(nc.vector.scalar_tensor_tensor, y, rr[:, 1:1 + S], mu[0:rows, 0, f:f + 1], y, ALU.mult, ALU.add, after=[m])
                m = V(nc.vector.scalar_tensor_tensor, y, rr[:, 3:3 + S], mu[0:rows, 1, f:f + 1], y, ALU.mult, ALU.add, after=[m])
            r.free = [m]
            yield

    fill = Filler(k, gate_steps(k, hT, h_ready, silu_dn, lambda: []), shifted_steps(),
                  gate_steps(k, hT, h_ready, silu_rk, lambda: raw[0].free + raw[1].free))

    ea = dn_cols[:, 0:8]
    A(nc.scalar.activation, ea, a_log, ACT.Exp, after=[small_ready])
    V(nc.vector.tensor_scalar, ea, ea, -1.0, None, ALU.mult, after=[A])
    for t, b, mark in k.token_major(hT, DN_AB, tiles=(KT,), ready=[small_ready]):
        z, ex, ser, big = (dn_cols[:, 8 * j:8 * j + 8] for j in (1, 2, 3, 4))
        A(nc.scalar.activation, g_beta[:, 1, t, :], b.ap[:, 8:16], ACT.Sigmoid, after=[mark])
        V(nc.vector.tensor_tensor, z, b.ap[:, 0:8], dt_bias, ALU.add, after=[A, V])
        b.free = [V.mark()]
        V(nc.vector.scalar_tensor_tensor, ex, z, -1.0, z, ALU.mult, ALU.min, after=[V])
        A(nc.scalar.activation, ex, ex, ACT.Exp, after=[V])
        A(nc.scalar.activation, big, ex, ACT.Ln, bias=1.0, after=[A])
        V(nc.vector.tensor_scalar, ser, ex, -0.25, 1.0 / 3.0, ALU.mult, ALU.add, after=[A])
        V(nc.vector.tensor_tensor, ser, ser, ex, ALU.mult, after=[V])
        V(nc.vector.tensor_scalar, ser, ser, -0.5, None, ALU.add, after=[V])
        V(nc.vector.tensor_tensor, ser, ser, ex, ALU.mult, after=[V])
        V(nc.vector.tensor_scalar, ser, ser, 1.0, None, ALU.add, after=[V])
        V(nc.vector.tensor_tensor, ser, ser, ex, ALU.mult, after=[V])
        V(nc.vector.tensor_scalar, ex, ex, 0.02, None, ALU.is_lt, after=[V])
        V(nc.vector.tensor_tensor, ser, ser, big, ALU.subtract, after=[V])
        V(nc.vector.tensor_tensor, ser, ser, ex, ALU.mult, after=[V])
        V(nc.vector.tensor_tensor, big, big, ser, ALU.add, after=[V])
        V(nc.vector.scalar_tensor_tensor, big, z, 0.0, big, ALU.max, ALU.add, after=[V])
        V(nc.vector.tensor_tensor, g_beta[:, 0, t, :], big, ea, ALU.mult, after=[V])

    def l2_normalise(y, squares, sel, scale, after):
        n = sel.shape[1]
        sums = stats[:, 88:88 + TT * 4 * n]
        V(nc.vector.tensor_tensor, squares, y, y, ALU.mult, after=after)
        fill()
        b = k.bank()
        for t in range(TT):
            for j in range(4):
                at = (t * 4 + j) * n
                k.matmul(b.ap[:, at:at + n], squares[:, j, t * P:(t + 1) * P], sel, True, True,
                         after=[*b.free, V] if at == 0 else (), inc=at == (TT * 4 - 1) * n)
        fill()
        V(nc.vector.tensor_scalar, sums, b.ap[:, 0:TT * 4 * n], scale ** -2, EPS_RMS * scale ** -2, ALU.mult, ALU.add, after=[T])
        b.free = [V.mark()]
        A(nc.scalar.activation, sums, sums, ACT.Sqrt, after=[V])
        V(nc.vector.reciprocal, sums, sums, after=[A])
        fill()
        rows = P // n
        for t in range(TT):
            b = k.bank()
            for j in range(4):
                for q in range(n):
                    at = (t * 4 + j) * n + q
                    k.matmul(b.ap[q * rows:(q + 1) * rows, j * P:(j + 1) * P], sums[:, at:at + 1].to_broadcast([P, rows]),
                             table("ident"), True, True, after=[*b.free, V] if j + q == 0 else (), inc=j == 3 and q == n - 1)
            cut = slice(t * P, (t + 1) * P)
            V(nc.vector.tensor_tensor, y[:, :, cut], y[:, :, cut], split(b.ap, 4, P), ALU.mult, after=[T])
            b.free = [V.mark()]

    squares = decay.rearrange("p a b -> p (a b)")
    l2_normalise(qkvT[:, 0], split(squares, 4, S), table("ones")[:, 0:1], P ** -0.5, after=[A, V])
    l2_normalise(qkvT[:, 1], split(squares, 4, S), table("ones")[:, 0:1], 1.0, after=[A, V, T])

    def tokens_first(src, dst, tiles, after):
        for t in range(TT):
            b = k.bank()
            for j in range(tiles):
                k.transpose(b.ap[:, j * P:(j + 1) * P], src[:, j, t * P:(t + 1) * P],
                            after=[*b.free, *after] if j == 0 else (), inc=j == tiles - 1)
            b.free = [k.copy((V, A)[t], dst[:, t, :], b.ap[:, 0:tiles * P], after=[T])]
        fill()

    tokens_first(qkvT[:, 1], k_tok, 4, after=[V, A])
    tokens_first(qkvT[:, 2], v_tok, 4, after=[V, A])

    tri.fill = fill
    qk_ready = [V.mark()]
    for d in range(2):
        incl, strict = table(f"incl{d}"), table(f"strict{d}")
        g = g_beta[:, 0, :, 4 * d:4 * d + 4]
        beta = g_beta[:, 1, :, 4 * d:4 * d + 4]
        Gc, tail, eG = (split(dn_cols[:, 8 * j:8 * j + 8], TT, 4) for j in (5, 6, 7))
        b = k.bank()
        k.matmul(b.ap[:, 0:8], incl, g, True, True, after=[*b.free, V, A])
        V(nc.vector.tensor_copy, Gc, split(b.ap[:, 0:8], TT, 4), after=[T])
        b.free = [V.mark()]
        b = k.bank()
        k.matmul(b.ap[:, 0:8], table("ones"), g, True, True, after=b.free)
        V(nc.vector.tensor_tensor, tail, split(b.ap[:, 0:8], TT, 4), Gc, ALU.subtract, after=[T, V])
        b.free = [V.mark()]
        A(nc.scalar.activation, tail, tail, ACT.Exp, after=[V])
        A(nc.scalar.activation, eG, Gc, ACT.Exp, after=[V])
        fill()
        for c in range(TT):
            b = k.bank()
            for h in range(4):
                k.matmul(b.ap[:, h * P:(h + 1) * P], g[:, c, h:h + 1].to_broadcast([P, P]), incl, True, True,
                         after=b.free if h == 0 else (), inc=h == 3)
            for h in range(4):
                V(nc.vector.tensor_scalar, decay[:, 4 * c + h, :], b.ap[:, h * P:(h + 1) * P], Gc[:, c, h:h + 1], 0.0,
                  ALU.subtract, ALU.min, after=[T, V])
            b.free = [V.mark()]
        fill()
        A(nc.scalar.activation, decay, decay, ACT.Exp, after=[V])
        V(nc.vector.tensor_tensor, decay, decay, incl.unsqueeze(1).to_broadcast([P, 8, P]), ALU.mult, after=[A])
        fill(2)
        for c in range(TT):
            cut = slice(c * P, (c + 1) * P)
            us = slice(4 * c, 4 * c + 4)
            for right, dst in ((0, AT), (1, NT)):
                b = k.bank()
                for h in range(4):
                    k.matmul(b.ap[:, h * P:(h + 1) * P], qkvT[:, 1, h, cut], qkvT[:, right, h, cut], True, True,
                             after=[*b.free, *qk_ready] if h == 0 else (), inc=h == 3)
                V(nc.vector.tensor_tensor, dst[:, us], split(b.ap, 4, P), decay[:, us], ALU.mult, after=[T, V])
                b.free = [V.mark()]
            b = k.bank()
            for h in range(4):
                k.matmul(b.ap[:, h * P:(h + 1) * P], beta[:, c, h:h + 1].to_broadcast([P, P]), table("ident"), True, True,
                         after=b.free if h == 0 else (), inc=h == 3)
            V(nc.vector.tensor_tensor, NT[:, us], NT[:, us], split(b.ap, 4, P), ALU.mult, after=[T, V])
            b.free = [V.mark()]
            fill()
        V(nc.vector.tensor_tensor, NT, NT, strict.unsqueeze(1).to_broadcast([P, 8, P]), ALU.mult, after=[V])
        tri.invert(NT, d, [V.mark()])
        bc = lambda col: col.unsqueeze(2).to_broadcast([P, 4, P])
        rhs4, U4, work4 = (split(a, 4, P) for a in (rhs, U, work))
        for step in range(TT):
            c = step if d == 0 else TT - 1 - step
            cut = slice(c * P, (c + 1) * P)
            units = list(range(4 * c, 4 * c + 4))
            vs = split(v_tok[:, c, :], 4, P)
            if step == 0:
                V(nc.vector.tensor_tensor, rhs4, vs, bc(beta[:, c, :]), ALU.mult, after=[V, A])
            else:
                b = k.bank()
                for h in range(4):
                    k.matmul(b.ap[:, h * P:(h + 1) * P], qkvT[:, 1, h, cut], state[:, h * P:(h + 1) * P], True, True,
                             after=[*b.free, V, A] if h == 0 else (), inc=h == 3)
                V(nc.vector.tensor_tensor, rhs4, split(b.ap, 4, P), bc(eG[:, c, :]), ALU.mult, after=[T, V])
                b.free = [V.mark()]
                V(nc.vector.tensor_tensor, rhs4, vs, rhs4, ALU.subtract, after=[V])
                V(nc.vector.tensor_tensor, rhs4, rhs4, bc(beta[:, c, :]), ALU.mult, after=[V])
            fill()
            tri.solve(units, rhs4, U4, work4, P, [V.mark()])
            b = k.bank()
            for h in range(4):
                k.matmul(b.ap[:, h * P:(h + 1) * P], AT[:, 4 * c + h, :], U4[:, h, :], True, True,
                         after=[*b.free, V] if h == 0 else (), inc=h == 3)
            o = o_dn[:, c, :]
            if d == 0:
                V(nc.vector.tensor_copy, o, b.ap, after=[T])
            else:
                V(nc.vector.tensor_tensor, o, o, b.ap, ALU.add, after=[T, V])
            b.free = [V.mark()]
            if step == 0:
                V(nc.vector.tensor_tensor, work4, U4, bc(tail[:, c, :]), ALU.mult, after=[V, A, T])
                fill()
                b = k.bank()
                for h in range(4):
                    k.matmul(b.ap[:, h * P:(h + 1) * P], k_tok[:, c, h * P:(h + 1) * P], work4[:, h, :], True, True,
                             after=[*b.free, V] if h == 0 else (), inc=h == 3)
                b.free = [k.copy(A, state, b.ap, after=[T])]
                fill()
            else:
                b = k.bank()
                for h in range(4):
                    k.matmul(b.ap[:, h * P:(h + 1) * P], qkvT[:, 0, h, cut], state[:, h * P:(h + 1) * P], True, True,
                             after=b.free if h == 0 else (), inc=h == 3)
                V(nc.vector.tensor_tensor, work4, split(b.ap, 4, P), bc(eG[:, c, :]), ALU.mult, after=[T, V])
                b.free = [V.mark()]
                V(nc.vector.tensor_tensor, o, o, work, ALU.add, after=[V])

    fill.finish()
    sq = squares[:, 0:WB]
    for t in range(TT):
        V(nc.vector.tensor_tensor, sq, o_dn[:, t, :], o_dn[:, t, :], ALU.mult, after=[V])
        V(nc.vector.tensor_reduce, stats[:, 4 * t:4 * t + 4], split(sq, 4, P), AX.X, ALU.add, after=[V])
    k.rstd(stats[:, 8:16], stats[:, 0:8], P, EPS_RMS, after=[V])
    for t in range(TT):
        o4 = split(o_dn[:, t, :], 4, P)
        V(nc.vector.tensor_tensor, o4, o4, stats[:, 8 + 4 * t:12 + 4 * t].unsqueeze(2).to_broadcast([P, 4, P]), ALU.mult, after=[V])
        V(nc.vector.tensor_tensor, o4, o4, dn_norm.unsqueeze(1).to_broadcast([P, 4, P]), ALU.mult, after=[V])
        V(nc.vector.tensor_tensor, o_dn[:, t, :], o_dn[:, t, :], silu_dn[:, t, :], ALU.mult, after=[V, A])

    k.top = body_at
    dn_done = [V.mark(), T.mark(), A.mark()]
    kkT, bT = take(4, S), take(4, S)
    arT = take(4, 2, S)
    dbT, dkT = take(4, S), take(4, S)
    cur = take(4, S)
    tmp = take(4, S)
    M = split(k.words_at(m_at, RK_HEADS * 4 * P), RK_HEADS, 4, P)
    db_tok, dk_tok = take(WB), take(WB)
    bonus = take(TT, 8)
    scale_state = take(4)
    assert k.top <= body_at + rk_words
    o_rk = mixed[:, :, WB:]
    for m0 in range(0, 4, 2):
        b = k.bank()
        for j in range(2):
            k.matmul(b.ap[:, j * S:(j + 1) * S], lora[0:LORA, 1, (m0 + j) * P:(m0 + j + 1) * P], loraT[0:LORA, 1, :],
                     True, True, after=[*b.free, V] if j == 0 else ())
        for j in range(2):
            A(nc.scalar.activation, bT[:, m0 + j, :], b.ap[:, j * S:(j + 1) * S], ACT.Sigmoid, bias=a0[:, m0 + j:m0 + j + 1], after=[T])
        b.free = [A.mark()]
    for m in range(4):
        V(nc.vector.tensor_scalar, kkT[:, m, :], rkvT[:, 1, m, :], k_k[:, m:m + 1], None, ALU.mult, after=[V])
        V(nc.vector.tensor_scalar, tmp[:, m, :], bT[:, m, :], -1.0, k_a[:, m:m + 1], ALU.add, ALU.mult, after=[A, V])
    V(nc.vector.scalar_tensor_tensor, rkvT[:, 1], tmp, 1.0, rkvT[:, 1], ALU.add, ALU.mult, after=[V])
    l2_normalise(kkT, tmp, table("head_sel"), 1.0, after=[V])
    V(nc.vector.tensor_tensor, bT, bT, kkT, ALU.mult, after=[V])
    for m in range(4):
        V(nc.vector.scalar_tensor_tensor, tmp[:, m, :], rkvT[:, 0, m, :], r_k[:, m:m + 1], rkvT[:, 1, m, :],
          ALU.mult, ALU.mult, after=[V])
    b = k.bank()
    for t in range(TT):
        for m in range(4):
            k.matmul(b.ap[:, 8 * t + 2 * m:8 * t + 2 * m + 2], tmp[:, m, t * P:(t + 1) * P], table("head_sel"), True, True,
                     after=[*b.free, V] if t + m == 0 else ())
    V(nc.vector.tensor_copy, bonus, split(b.ap[:, 0:16], TT, 8), after=[T])
    b.free = [V.mark()]
    tokens_first(rkvT[:, 2], v_tok, 4, after=[V, T])
    v_ready = [V.mark(), A.mark()]
    A(nc.scalar.activation, loraT[:, 0, :], loraT[:, 0, :], ACT.Tanh, after=[V])

    for d in range(2):
        rows = slice(64 * d, 64 * d + 64)
        logw = arT[:, :, 0, :]
        for m0 in range(0, 4, 2):
            b = k.bank()
            for j in range(2):
                k.matmul(b.ap[:, j * S:(j + 1) * S], lora[rows, 0, (m0 + j) * P:(m0 + j + 1) * P], loraT[rows, 0, :],
                         True, True, after=[*b.free, A, V] if j == 0 else ())
            for j in range(2):
                A(nc.scalar.activation, cur[:, m0 + j, :], b.ap[:, j * S:(j + 1) * S], ACT.Sigmoid,
                  bias=w0[:, d, m0 + j:m0 + j + 1], after=[T, V])
            b.free = [A.mark()]
        flat = lambda a: a.rearrange("p a b -> p (a b)")
        V(nc.vector.tensor_scalar, flat(cur), flat(cur), -math.exp(-0.5), None, ALU.mult, after=[A])
        V(nc.vector.tensor_tensor_scan, flat(tmp), table("fresh"), flat(cur), 0.0, ALU.mult, ALU.add, after=[V, T])
        V(nc.vector.tensor_tensor, flat(cur), flat(tmp), flat(cur), ALU.subtract, after=[V])
        chunked = lambda a: split(flat(a), 8, P)
        upto, before = chunked(tmp), chunked(cur)
        mid = (upto[:, :, 63:64], before[:, :, 64:65])[d]
        total = stats[:, 48:56]
        mids = stats[:, 56:64]
        V(nc.vector.tensor_copy, total.unsqueeze(2), upto[:, :, P - 1:P], after=[V])
        V(nc.vector.tensor_copy, mids.unsqueeze(2), mid, after=[V])
        midb = mids.unsqueeze(2).to_broadcast([P, 8, P])
        total2, mids2 = split(total, 4, 2), split(mids, 4, 2)
        if d == 0:
            V(nc.vector.tensor_tensor, upto, upto, midb, ALU.subtract, after=[V])
            V(nc.vector.tensor_tensor, before, before, midb, ALU.subtract, after=[V])
            plus, less = tmp, cur
            V(nc.vector.tensor_tensor, scale_state, total2[:, :, 0], mids2[:, :, 0], ALU.subtract, after=[V])
            V(nc.vector.tensor_tensor, scale_state, scale_state, mids2[:, :, 1], ALU.add, after=[V])
        else:
            V(nc.vector.tensor_tensor, upto, midb, upto, ALU.subtract, after=[V])
            V(nc.vector.tensor_tensor, before, midb, before, ALU.subtract, after=[V])
            plus, less = cur, tmp
            V(nc.vector.tensor_tensor, scale_state, total2[:, :, 0], mids2[:, :, 0], ALU.subtract, after=[V])
            V(nc.vector.tensor_tensor, scale_state, scale_state, mids2[:, :, 1], ALU.add, after=[V])
        A(nc.scalar.activation, scale_state, scale_state, ACT.Exp, after=[V])
        A(nc.scalar.activation, flat(less), flat(less), ACT.Exp, after=[V])
        V(nc.vector.scalar_tensor_tensor, arT[:, :, 0, :], less, -1.0, kkT, ALU.mult, ALU.mult, after=[A])
        A(nc.scalar.activation, flat(less), flat(plus), ACT.Exp, scale=-1.0, after=[V])
        V(nc.vector.tensor_tensor, dbT, less, bT, ALU.mult, after=[A])
        V(nc.vector.tensor_tensor, dkT, less, rkvT[:, 1], ALU.mult, after=[A])
        A(nc.scalar.activation, flat(plus), flat(plus), ACT.Exp, after=[A])
        V(nc.vector.tensor_tensor, arT[:, :, 1, :], plus, rkvT[:, 0], ALU.mult, after=[A])

        decayed = [V.mark()]
        for step in range(TT):
            c = step if d == 0 else TT - 1 - step
            cut = slice(c * P, (c + 1) * P)
            for h in range(RK_HEADS):
                hr = slice(64 * (h % 2), 64 * (h % 2) + 64)
                b = k.bank()
                for j, left in enumerate((dbT, dkT)):
                    k.matmul(b.ap[:, j * 2 * P:(j + 1) * 2 * P], left[hr, h // 2, cut], arT[hr, h // 2, :, cut], True, True,
                             after=[*b.free, *decayed] if j == 0 else ())
                V(nc.vector.tensor_tensor, M[:, h].rearrange("p a b -> p (a b)"), b.ap, table(f"rk_mask{d}"), ALU.mult, after=[T])
                b.free = [V.mark()]
            tri.invert(M[:, :, 0, :], d, [V.mark()])
            heads = lambda a: split(a, 8, 64)

            def pair_sums(terms, through_state, after):
                b = k.bank()
                first = True
                for m in range(RK_PAIRS):
                    if step:
                        k.matmul(b.ap[:, m * P:(m + 1) * P], arT[:, m, through_state, cut], state[:, m * P:(m + 1) * P],
                                 True, False, after=[*b.free, *after] if first else ())
                        first = False
                    for h in (2 * m, 2 * m + 1):
                        for j, (which, right) in enumerate(terms):
                            k.matmul(b.ap[:, h * 64:(h + 1) * 64], M[:, h, which, :], right[:, h * 64:(h + 1) * 64],
                                     not step and j == 0, j == len(terms) - 1 and (not step or h % 2 == 1), after=[*b.free, *after] if first else ())
                            first = False
                return b

            b = pair_sums([(2, v_tok[:, c, :])], 0, [V, A, *v_ready])
            b.free = [k.copy(V, rhs, b.ap, after=[T])]
            tri.solve(list(range(8)), heads(rhs), heads(U), heads(work), 64, [V.mark()])
            b = pair_sums([(1, U), (3, v_tok[:, c, :])], 1, [V])
            if d == 0:
                V(nc.vector.tensor_copy, o_rk[:, c, :], b.ap, after=[T])
            else:
                V(nc.vector.tensor_tensor, o_rk[:, c, :], o_rk[:, c, :], b.ap, ALU.add, after=[T, V])
            b.free = [V.mark()]
            if step == 0:
                for src, dst in ((dbT, db_tok), (dkT, dk_tok)):
                    b = k.bank()
                    for m in range(4):
                        k.transpose(b.ap[:, m * P:(m + 1) * P], src[:, m, cut], after=[*b.free, V] if m == 0 else (), inc=m == 3)
                    b.free = [k.copy(A, dst, b.ap, after=[T])]
                b = k.bank()
                for m in range(RK_PAIRS):
                    ms = slice(m * P, (m + 1) * P)
                    k.matmul(b.ap[:, ms], db_tok[:, ms], U[:, ms], True, False, after=[*b.free, A, V] if m == 0 else ())
                    k.matmul(b.ap[:, ms], dk_tok[:, ms], v_tok[:, c, ms], False, True)
                for m in range(RK_PAIRS):
                    ms = slice(m * P, (m + 1) * P)
                    V(nc.vector.scalar_tensor_tensor, state[:, ms], b.ap[:, ms], scale_state[:, m:m + 1], table("pairs"),
                      ALU.mult, ALU.mult, after=[T, A])
                b.free = [V.mark()]

    for t in range(TT):
        o = o_rk[:, t, :]
        o8, w8 = split(o, 8, 64), split(work, 8, 64)
        mean, var, st = stats[:, 64:72], stats[:, 72:80], stats[:, 80:88]
        bc = lambda a: a.unsqueeze(2).to_broadcast([P, 8, 64])
        V(nc.vector.tensor_reduce, mean, o8, AX.X, ALU.add, after=[V, T])
        V(nc.vector.tensor_scalar, mean, mean, 1.0 / 64, None, ALU.mult, after=[V])
        V(nc.vector.tensor_tensor, o8, o8, bc(mean), ALU.subtract, after=[V])
        V(nc.vector.tensor_tensor, work, o, o, ALU.mult, after=[V])
        V(nc.vector.tensor_reduce, var, w8, AX.X, ALU.add, after=[V])
        k.rstd(st, var, 64, EPS_GN, after=[V])
        V(nc.vector.tensor_tensor, o8, o8, bc(st), ALU.mult, after=[V])
        V(nc.vector.tensor_tensor, o, o, ln_w, ALU.mult, after=[V])
        V(nc.vector.tensor_tensor, o, o, ln_b, ALU.add, after=[V])
        V(nc.vector.tensor_tensor, w8, split(v_tok[:, t, :], 8, 64), bc(bonus[:, t, :]), ALU.mult, after=[V])
        V(nc.vector.tensor_tensor, o, o, work, ALU.add, after=[V])
        V(nc.vector.tensor_tensor, o, o, silu_rk[:, t, :], ALU.mult, after=[V, A])
    close_layer(k, 0, x, mixed, hT, free_at)
    k.top = floor


def odd_layer(k, x):
    nc, T, V, A, G, SP = k.nc, k.T, k.V, k.A, k.G, k.SP
    dram, table, take = k.dram, k.table, k.take
    k.begin()
    floor = k.top
    w_in = dram["odd_w_in"].rearrange("(k p) n -> p k n", p=P)
    mixed = take(TT, D)
    hT = k.take_parts("hT_odd", KT, S)
    free_at = k.top
    cols = take(100)
    xv = take(3, TT, D)
    H = take(5, D)
    U = take(4, D)
    Y = take(4, D)
    deltas = split(k.words_at(free_at - 4 * D, 2 * D), 2, D)
    filter_w = k.words_at(free_at - 2 * D, 2 * D)
    skip = take(D)
    sine = take(4, S)
    w123 = take(3, HY_F)
    over = U.rearrange("p a b -> p (a b)")
    raw = [k.c.buf(split(over[:, j * 2 * (S + 4):(j + 1) * 2 * (S + 4)], 2, S + 4)) for j in range(2)]
    conv = [k.c.buf(split(over[:, (4 + j) * WB:(5 + j) * WB], 2, S)) for j in range(2)]
    norm = take(D)
    sums = take(KT)
    cw, cb = split(cols[:, 0:72], HY_SHORT, 24), cols[:, 72:96]
    fb, freq = cols[0:HY_F, 96:99], cols[0:HY_F, 99:100]

    k.load_tables("odd")
    SP.dma(k.small_loaded, cols, dram["odd_cols"])
    for j, (name, n) in enumerate((("hy_w1", HY_EMB), ("hy_w2", HY_F), ("hy_w3", HY_F))):
        SP.dma(k.small_loaded, w123[0:n, j, :], dram[name])
    small_ready = k.small_loaded.mark()
    for r in raw:
        V(nc.vector.memset, r.ap.rearrange("p a b -> p (a b)"), 0.0)
    first_of = lambda i, j: k.columns(w_in, i * D + j * S)
    k.plan(first_of(0, 0))
    k.transposes_cut(x, hT, KT, [[]] * TT)
    h_ready = [V.mark()]

    hid = sine[0:HY_F, 0, :]
    for j, n in enumerate((HY_EMB, HY_F, HY_F)):
        b = k.bank()
        right = table("feats")[0:n, :] if j == 0 else hid
        k.matmul(b.ap[0:HY_F, 0:S], w123[0:n, j, :], right, True, True, after=[*b.free, small_ready, A])
        ang, turns, work = (sine[0:HY_F, m, :] for m in (1, 2, 3))
        V(nc.vector.tensor_scalar, ang, b.ap[0:HY_F, 0:S], fb[:, j:j + 1], freq, ALU.add, ALU.mult, after=[T, small_ready])
        b.free = [V.mark()]
        k.wrapped_sin(hid, ang, turns, work, 0, after=[V])
    hid_ready = A.mark()


    def project(i, more):
        k.plan(*(first_of(i, j) for j in (1, 2, 3)), *([first_of(i + 1, 0)] if more else after_loop))
        for j in range(2):
            for m0 in (0, 2):
                b, mark = k.two_tiles(hT, h_ready)
                r, y = raw[m0 // 2], conv[m0 // 2]
                padded_copy(k, r.ap, b, 2, 2, after=[mark, *r.free, *raw_zeroed])
                b.free = [A.mark()]
                for q in range(2):
                    f = i * 8 + (j * 4 + m0 + q)
                    col = lambda a: a[:, pick(f, 1)]
                    m = V(nc.vector.tensor_scalar, y.ap[:, q, :], r.ap[:, q, 1:1 + S], col(cw[:, 0, :]), col(cb),
                          ALU.mult, ALU.add, after=[A, small_ready, *y.free])
                    for tap in (1, 2):
                        m = V(nc.vector.scalar_tensor_tensor, y.ap[:, q, :], r.ap[:, q, 1 + tap:1 + tap + S],
                              col(cw[:, tap, :]), y.ap[:, q, :], ALU.mult, ALU.add, after=[m])
                r.free = [m]
                bt = k.bank()
                for t in range(TT):
                    for q in range(2):
                        k.transpose(bt.ap[:, (2 * t + q) * P:(2 * t + q + 1) * P], y.ap[:, q, t * P:(t + 1) * P],
                                    after=[*bt.free, m] if t + q == 0 else (), inc=t + q == 2)
                y.free = [T.mark()]
                at = (j * 4 + m0) * P
                dst = xv[:, pick(i, 1)][:, 0][:, :, at:at + 2 * P]
                bt.free = [k.copy(A, dst, split(bt.ap, TT, 2 * P), after=[T])]

    raw_zeroed = [V.mark()]
    after_loop = [*k.by_rows(w_in, HY_XV), *k.by_rows(w_in, HY_XV + WB), *closing_pieces(k, 1)]
    k.c.loop(2, lambda i: project(i, True))
    project(2, False)
    for hf in range(2):
        for t, b, mark in k.token_major(hT, WB, ready=h_ready):
            A(nc.scalar.activation, mixed[:, t, hf * WB:(hf + 1) * WB], b.ap, ACT.Silu, after=[mark])
            b.free = [A.mark()]

    ft = split(Y.rearrange("p a b -> p (a b)"), 2, TT, D)
    dft_re = split(table("dft_re"), TT, S)
    dft_im = split(table("dft_im_signal"), TT, S)
    dft_im0 = split(table("dft_im_filter0"), TT, P)
    dft_rc0 = split(table("dft_re_cross0"), TT, P)
    idft = split(table("idft"), 4, S)
    fw = dram["hy_out"]
    skip_free = []
    deltas_free = [V.mark(), A.mark(), T.mark()]
    for o in range(HY_ORDER):
        SP.dma(k.rows_loaded, deltas.rearrange("p a b -> p (a b)"),
               dram["hy_deltas"][:, o * 2 * D:(o + 1) * 2 * D].partition_broadcast(P)[:, 0, :], after=deltas_free)
        SP.dma(k.rows_loaded, filter_w[0:HY_F, :], fw[:, o * 2 * D:(o + 1) * 2 * D])
        A(nc.scalar.activation, deltas.rearrange("p a b -> p (a b)"), deltas.rearrange("p a b -> p (a b)"), ACT.Abs,
          after=[k.rows_loaded])
        halves = [slice(hf * WB, (hf + 1) * WB) for hf in range(2)]
        mag = split(U.rearrange("p a b -> p (a b)"), 2, TT, D)
        before, abs_made, diff_made = [V.mark(), T.mark(), G.mark()], [], []
        for hf, cut in enumerate(halves):
            for f in range(2):
                for t in range(TT):
                    b = k.bank()
                    n = 2 * f + hf
                    k.matmul(b.ap, hid[:, t * P:(t + 1) * P], filter_w[0:HY_F, n * WB:(n + 1) * WB], True, True,
                             after=[*b.free, k.rows_loaded, hid_ready])
                    A(nc.scalar.activation, ft[:, f, t, cut], deltas[:, f, cut], ACT.Exp, scale=table("minus_t")[:, t:t + 1],
                      after=[A, *before])
                    V(nc.vector.tensor_tensor, ft[:, f, t, cut], ft[:, f, t, cut], b.ap, ALU.mult, after=[A, T])
                    b.free = [V.mark()]
            V(nc.vector.memset, ft[0:1, 1, 0, cut], 0.0, after=[V])
            abs_made.append(A(nc.scalar.activation, mag[:, :, :, cut], ft[:, :, :, cut], ACT.Abs, after=[V, *before]))
        deltas_free = [A.mark(), T.mark(), V.mark()]
        SP.dma(k.small_loaded, skip, dram["hy_skip"][o:o + 1, :].partition_broadcast(P)[:, 0, :], after=skip_free)
        for hf in range(2):
            cut = halves[hf]
            V(nc.vector.tensor_tensor, mag[:, 0, :, cut], mag[:, 0, :, cut], mag[:, 1, :, cut], ALU.add, after=[abs_made[hf]])
            V(nc.vector.tensor_tensor, mag[:, 0, 0, cut], mag[:, 0, 0, cut], mag[:, 0, 1, cut], ALU.add, after=[V])
            b, part = k.bank(), sums[:, 4 * hf:4 * hf + 4]
            for j in range(4):
                at = (4 * hf + j) * P
                k.matmul(b.ap[:, j:j + 1], mag[:, 0, 0, at:at + P], table("ones")[:, 0:1], True, True,
                         after=[*b.free, V] if j == 0 else ())
            V(nc.vector.tensor_scalar, part, b.ap[:, 0:4], EPS_RMS, None, ALU.add, after=[T])
            b.free = [V.mark()]
            sums_made = V(nc.vector.reciprocal, part, part, after=[V])
            G(nc.gpsimd.tensor_tensor, mag[:, 0, :, cut], ft[:, 0, :, cut], ft[:, 1, :, cut], ALU.add, after=[T, V])
            V(nc.vector.tensor_tensor, mag[:, 1, :, cut], ft[:, 0, :, cut], ft[:, 1, :, cut], ALU.subtract, after=[T])
            diff_made.append([V.mark(), G.mark()])
        for hf in range(2):
            b = k.bank()
            for j in range(4):
                k.matmul(b.ap[:, j * P:(j + 1) * P], sums[:, 4 * hf + j:4 * hf + j + 1].to_broadcast([P, P]), table("ident"),
                         True, True, after=[*b.free, sums_made] if j == 0 else (), inc=j == 3)
            b.free = [k.copy(A, norm[:, halves[hf]], b.ap, after=[T, *before])]
        norm_made = A.mark()
        spectrum = [(0, 0, lambda t: dft_re[:, t, 0:P]), (1, 0, lambda t: dft_re[:, t, P:]),
                    (2, 1, lambda t: dft_im0[:, t, :]), (3, 1, lambda t: dft_im[:, t, P:]),
                    (4, 0, lambda t: dft_rc0[:, t, :])]
        for hf, cut in enumerate(halves):
            for tile, which, left in spectrum:
                b = k.bank()
                for t in range(TT):
                    k.matmul(b.ap, left(t), mag[:, which, t, cut], t == 0, t == TT - 1,
                             after=[*b.free, *diff_made[hf]] if t == 0 else ())
                V(nc.vector.tensor_tensor, H[:, tile, cut], b.ap, norm[:, cut], ALU.mult, after=[T, norm_made])
                b.free = [V.mark()]
        signal = xv[:, 2]
        filter_done = [V.mark(), T.mark(), G.mark()]
        signal_ready, product = [V.mark(), A.mark()], []
        for cut in halves:
            for tile in range(4):
                left = (dft_re if tile < 2 else dft_im)[:, :, (tile % 2) * P:(tile % 2 + 1) * P]
                b = k.bank()
                for t in range(TT):
                    k.matmul(b.ap, left[:, t, :], signal[:, t, cut], t == 0, t == TT - 1,
                             after=[*b.free, *filter_done, *signal_ready] if t == 0 else ())
                b.free = [k.copy(A, U[:, tile, cut], b.ap, after=[T, *filter_done])]
            spectrum_made = A.mark()
            for tile in range(2):
                re, im = U[:, tile, cut], U[:, 2 + tile, cut]
                hr, hi, own = H[:, tile, cut], H[:, 2 + tile, cut], H[:, 4 if tile == 0 else 1, cut]
                yr, yi = Y[:, tile, cut], Y[:, 2 + tile, cut]
                V(nc.vector.tensor_tensor, yr, re, hr, ALU.mult, after=[spectrum_made, *filter_done])
                G(nc.gpsimd.tensor_tensor, yi, re, hi, ALU.mult, after=[spectrum_made, *filter_done])
                V(nc.vector.tensor_tensor, re, im, hi, ALU.mult, after=[V, G])
                V(nc.vector.tensor_tensor, yr, yr, re, ALU.subtract, after=[V])
                G(nc.gpsimd.tensor_tensor, im, im, own, ALU.mult, after=[V])
                G(nc.gpsimd.tensor_tensor, yi, yi, im, ALU.add, after=[G])
            product.append([V.mark(), G.mark()])
        for hf, cut in enumerate(halves):
            for t in range(TT):
                b = k.bank()
                for kk in range(4):
                    k.matmul(b.ap, idft[:, kk, t * P:(t + 1) * P], Y[:, kk, cut], kk == 0, kk == 3,
                             after=[*b.free, *product[hf]] if kk == 0 else ())
                s = signal[:, t, cut]
                V(nc.vector.tensor_tensor, s, s, skip[:, cut], ALU.mult, after=[V, k.small_loaded, T])
                V(nc.vector.tensor_tensor, s, s, b.ap, ALU.add, after=[T, V])
                b.free = [V.mark()]
                V(nc.vector.tensor_tensor, s, s, xv[:, o, t, cut], ALU.mult, after=[V])
        skip_free = [V.mark()]
    for t in range(TT):
        V(nc.vector.tensor_tensor, mixed[:, t, :], mixed[:, t, :], xv[:, 2, t, :], ALU.mult, after=[V, A])
    close_layer(k, 1, x, mixed, hT, free_at)
    k.top = floor



def build(nc, dram, table_at, table_words):
    k = Core(nc, dram, table_at, table_words)
    x = k.take(TT, D)
    by_tokens = lambda ap: ap.rearrange("b (t p) d -> p (b t) d", p=P)
    nc.sync.dma_start(x, by_tokens(dram["x"])).then_inc(k.small_loaded.sem, 16)
    nc.sync.dma_start(k.tables[:, 0:dram["tables_all"].shape[1]], dram["tables_all"]).then_inc(k.small_loaded.sem, 16)
    nc.sync.wait_ge(k.small_loaded.sem, 32)
    first_block(k, x)
    even_layer(k, x)
    odd_layer(k, x)
    k.begin()
    k.SP.dma(k.out_stored, by_tokens(dram["out"]), x)
    k.SP.wait([k.out_stored])


def feature_columns(*arrays):
    out = []
    for a in arrays:
        a = a.reshape(-1, a.shape[-1])
        pad = -a.shape[1] % P
        a = np.concatenate([a, np.zeros((a.shape[0], pad), a.dtype)], 1) if pad else a
        out.append(a.reshape(-1, P).T)
    return np.ascontiguousarray(np.concatenate(out, 1))


def heads_apart(w, first):
    l, r, n = w.shape
    w = w.reshape(l, r, MLA_HEADS, n // MLA_HEADS)
    return np.ascontiguousarray(np.concatenate([w[..., :first].reshape(l, r, -1), w[..., first:].reshape(l, r, -1)], 2))


def lay_out(inputs):
    a = {name: np.asarray(v) for name, v in inputs.items()}
    out = {f"tables_{which}": np.concatenate(list(t.values()), 1) for which, t in const_tables().items()}
    for name in ("x", "rel_bias", "w_in", "w_branch", "w_out", "w_up", "w_down", "norm_mix_pre", "norm_mlp_pre", "norm_mix_post", "norm_mlp_post", "w_out_2"):
        out[name] = a[name]
    out["positions"] = np.ascontiguousarray(a["positions"].reshape(TT, P).T)
    out["mla_w_uq"] = heads_apart(a["mla_w_uq"], NOPE)
    out["mla_w_ukv"] = heads_apart(a["mla_w_ukv"], NOPE)
    out["diff_lambda"] = a["diff_lambda"].reshape(DEPTH, -1)
    out["cols"] = np.stack([feature_columns(*(a[n][l] for n in ("diff_subln", "mla_q_norm", "mla_kv_norm")))
                            for l in range(DEPTH)], 1)
    out["pT"] = np.ascontiguousarray(a["p_2"][:, 0].transpose(0, 2, 1))
    out["even_w_in"] = a["even_w_in_2"][0]
    out["odd_w_in"] = a["odd_w_in_2"][0]
    for name in ("dn_a_log", "dn_dt_bias", "dn_norm", "rk_ln_w", "rk_ln_b", "hy_deltas"):
        out[name] = a[name + "_2"].reshape(1, -1)
    out["rk_w2"] = a["rk_w2_2"].reshape(P, RK_W)
    out["rk_a2"] = a["rk_a2_2"][0]
    out["hy_skip"] = a["hy_skip_2"][0]
    for j in (1, 2, 3):
        out[f"hy_w{j}"] = a[f"hy_ffn_w{j}_2"][0]
    out["hy_out"] = a["hy_ffn_out_2"][0]
    for name in ("ln_g", "ln_b", "ple_norm", "ple_w", "ple_gate"):
        out[name] = a[name + "_2"]
    out["even_cols"] = feature_columns(a["dn_conv_2"], a["rk_mu_2"], a["rk_w0_2"], a["rk_a0_2"], a["rk_k_k_2"], a["rk_k_a_2"],
                                       a["rk_r_k_2"].reshape(1, -1))
    out["odd_cols"] = feature_columns(a["hy_conv_w_2"], a["hy_conv_b_2"], a["hy_ffn_b1_2"], a["hy_ffn_b2_2"], a["hy_ffn_b3_2"],
                                      a["hy_ffn_freq_2"])
    return out


def declare_and_build(nc, arrays):
    dram = {name: nc.dram_tensor(f"{name}_dram", a.shape, mybir.dt.from_np(a.dtype), kind="ExternalInput").ap()
            for name, a in arrays.items()}
    dram["diagonals"] = nc.dram_tensor("diagonals", (N_BIAS, REL_W + 1), FP32).ap()
    dram["out"] = nc.dram_tensor("out_dram", (1, S, D), FP32, kind="ExternalOutput").ap()
    at, words = offsets(const_tables())
    build(nc, dram, at, words)


def kernel(**inputs):
    import concourse.bacc as bacc
    from concourse.bass_utils import run_bass_kernel_spmd

    arrays = lay_out(inputs)
    nc = bacc.Bacc("TRN2", target_bir_lowering=False, num_devices=1)
    declare_and_build(nc, arrays)
    ran = run_bass_kernel_spmd(nc, [{f"{name}_dram": a for name, a in arrays.items()}], core_ids=[0])
    return ran.results[0]["out_dram"]
```
